# Optimizing a Trainium2 kernel written in Bass

```python
import jax, jax.numpy as jnp
from jax import lax
import numpy as np
import math

D_MODEL = 1024
BATCH = 1
SEQ = 256
DEPTH = 4

N_MIXERS = 3
HEAD_DIM = 64
RMS_EPS = 1e-6

NSA_HEADS = 16
NSA_GROUPS = 4
NSA_REP = NSA_HEADS // NSA_GROUPS
NSA_KV = NSA_GROUPS * HEAD_DIM
CMP_BLOCK = 32
CMP_STRIDE = 16
CMP_HIDDEN = 256
SLC_BLOCK = 64
SLC_TOPK = 16
WINDOW = 512
WIN_QBLOCK = 128
NSA_Q_CHUNK = 64
NSA_IN = NSA_HEADS * HEAD_DIM + 6 * NSA_KV + 3 * NSA_HEADS
NSA_SPLITS = [NSA_HEADS * HEAD_DIM + i * NSA_KV for i in range(7)]

MOBA_HEADS = 16
MOBA_BLOCK = 256
MOBA_TOPK = 3
MOBA_Q_CHUNK = 32

CONV_WIDTH = 3

D_FF = -(-8 * D_MODEL // (3 * 256)) * 256


def rms_norm(x, g):
    xf = x.astype(jnp.float32)
    y = xf * lax.rsqrt(jnp.mean(xf * xf, axis=-1, keepdims=True) + RMS_EPS)
    return (y * g.astype(jnp.float32)).astype(x.dtype)

def masked_softmax(s, mask):
    s = jnp.where(mask, s.astype(jnp.float32), -jnp.inf)
    m = jnp.max(s, axis=-1, keepdims=True)
    m = jnp.where(jnp.isfinite(m), m, 0.0)
    e = jnp.where(mask, jnp.exp(s - m), 0.0)
    d = jnp.sum(e, axis=-1, keepdims=True)
    return e / jnp.where(d > 0, d, 1.0)

def gather_blocks(blocks, idx):
    return jax.vmap(jax.vmap(lambda b, i: b[i]))(blocks, idx)

def swiglu(a, w_gate, w_up, w_down):
    return (jax.nn.silu(a @ w_gate) * (a @ w_up)) @ w_down

def nsa_mixer(h, w_in, w_out, pos_k, pos_v, k_w1, k_w2, v_w1, v_w2):
    B_, S_, _ = h.shape
    G, R, dh = NSA_GROUPS, NSA_REP, HEAD_DIM
    q, k_c, v_c, k_s, v_s, k_w, v_w, gates = jnp.split(h @ w_in, NSA_SPLITS, axis=-1)
    q = q.reshape(B_, S_, G, R, dh) * (HEAD_DIM ** -0.5)
    kvs = [a.reshape(B_, S_, G, dh) for a in (k_c, v_c, k_s, v_s, k_w, v_w)]
    k_c, v_c, k_s, v_s, k_w, v_w = kvs
    gates = jax.nn.sigmoid(gates.astype(jnp.float32)).reshape(B_, S_, 3, G, R)
    t = jnp.arange(S_)

    n_cmp = (S_ - CMP_BLOCK) // CMP_STRIDE + 1
    cmp_idx = jnp.arange(n_cmp)[:, None] * CMP_STRIDE + jnp.arange(CMP_BLOCK)[None, :]

    def compress(kv, pos, w1, w2):
        blk = kv[:, cmp_idx] + pos[None, None, :, None, :]
        blk = jnp.moveaxis(blk, 3, 2).reshape(B_, n_cmp, G, CMP_BLOCK * dh)
        return jax.nn.gelu(blk @ w1) @ w2

    kc = compress(k_c, pos_k, k_w1, k_w2)
    vc = compress(v_c, pos_v, v_w1, v_w2)
    cmp_end = jnp.arange(n_cmp) * CMP_STRIDE + CMP_BLOCK - 1
    cmp_mask = cmp_end[None, :] <= t[:, None]
    s_cmp = jnp.einsum('bsgrd,bcgd->bgrsc', q, kc)
    p_cmp = masked_softmax(s_cmp, cmp_mask)
    o_cmp = jnp.einsum('bgrsc,bcgd->bsgrd', p_cmp.astype(vc.dtype), vc)

    n_slc = S_ // SLC_BLOCK
    c_start = jnp.arange(n_cmp) * CMP_STRIDE
    j_start = jnp.arange(n_slc) * SLC_BLOCK
    overlap = ((c_start[:, None] < j_start[None, :] + SLC_BLOCK)
               & (c_start[:, None] + CMP_BLOCK > j_start[None, :])).astype(jnp.float32)
    imp = jnp.einsum('bgrsc,cn->bgsn', p_cmp, overlap)
    cur = t // SLC_BLOCK
    blk_ids = jnp.arange(n_slc)
    forced = ((blk_ids[None, :] == 0) | (blk_ids[None, :] == cur[:, None])
              | (blk_ids[None, :] == cur[:, None] - 1))
    imp = jnp.where(forced, jnp.inf,
                    jnp.where(blk_ids[None, :] <= cur[:, None], imp, -jnp.inf))
    n_sel = min(SLC_TOPK, n_slc)
    _, sel = lax.top_k(imp, n_sel)

    kb = k_s.reshape(B_, n_slc, SLC_BLOCK, G, dh).transpose(0, 3, 1, 2, 4)
    vb = v_s.reshape(B_, n_slc, SLC_BLOCK, G, dh).transpose(0, 3, 1, 2, 4)
    Qc = NSA_Q_CHUNK
    n_qc = S_ // Qc
    q_chunks = q.reshape(B_, n_qc, Qc, G, R, dh).transpose(1, 0, 2, 3, 4, 5)
    sel_chunks = sel.reshape(B_, G, n_qc, Qc, n_sel).transpose(2, 0, 1, 3, 4)

    def slc_chunk(args):
        ci, qc, ix = args
        tq = ci * Qc + jnp.arange(Qc)
        kg = gather_blocks(kb, ix)
        vg = gather_blocks(vb, ix)
        kpos = ix[..., None] * SLC_BLOCK + jnp.arange(SLC_BLOCK)
        mask = (kpos <= tq[:, None, None]).reshape(B_, G, Qc, n_sel * SLC_BLOCK)[:, :, None]
        s = jnp.einsum('bqgrd,bgqnkd->bgrqnk', qc, kg).reshape(B_, G, R, Qc, n_sel * SLC_BLOCK)
        p = masked_softmax(s, mask).reshape(B_, G, R, Qc, n_sel, SLC_BLOCK)
        return jnp.einsum('bgrqnk,bgqnkd->bqgrd', p.astype(vg.dtype), vg)

    o_slc = lax.map(slc_chunk, (jnp.arange(n_qc), q_chunks, sel_chunks))
    o_slc = o_slc.transpose(1, 0, 2, 3, 4, 5).reshape(B_, S_, G, R, dh)

    QB = WIN_QBLOCK
    nqb = S_ // QB
    n_back = WINDOW // QB
    pad = n_back * QB

    def band(kv):
        kp = jnp.pad(kv, ((0, 0), (pad, 0), (0, 0), (0, 0))).reshape(B_, nqb + n_back, QB, G, dh)
        return jnp.concatenate([kp[:, i:i + nqb] for i in range(n_back + 1)], axis=2)

    kwb = band(k_w)
    vwb = band(v_w)
    qb = q.reshape(B_, nqb, QB, G, R, dh)
    qpos = t.reshape(nqb, QB)
    kpos = (jnp.arange(nqb)[:, None] - n_back) * QB + jnp.arange((n_back + 1) * QB)[None, :]
    wmask = ((kpos[:, None, :] <= qpos[:, :, None])
             & (kpos[:, None, :] > qpos[:, :, None] - WINDOW)
             & (kpos[:, None, :] >= 0))
    s_win = jnp.einsum('bnqgrd,bnkgd->bgrnqk', qb, kwb)
    p_win = masked_softmax(s_win, wmask)
    o_win = jnp.einsum('bgrnqk,bnkgd->bnqgrd', p_win.astype(vwb.dtype), vwb).reshape(B_, S_, G, R, dh)

    o = (gates[:, :, 0, :, :, None] * o_cmp + gates[:, :, 1, :, :, None] * o_slc
         + gates[:, :, 2, :, :, None] * o_win).astype(h.dtype)
    return o.reshape(B_, S_, NSA_HEADS * dh) @ w_out

def moba_mixer(h, w_in, w_out):
    B_, S_, _ = h.shape
    H, dh = MOBA_HEADS, HEAD_DIM
    q, k, v = jnp.split(h @ w_in, 3, axis=-1)
    n_blk = -(-S_ // MOBA_BLOCK)
    S_pad = n_blk * MOBA_BLOCK

    def heads(a):
        a = jnp.pad(a, ((0, 0), (0, S_pad - S_), (0, 0)))
        return a.reshape(B_, S_pad, H, dh).transpose(0, 2, 1, 3)

    q = heads(q) * (HEAD_DIM ** -0.5)
    k = heads(k)
    v = heads(v)
    kb = k.reshape(B_, H, n_blk, MOBA_BLOCK, dh)
    vb = v.reshape(B_, H, n_blk, MOBA_BLOCK, dh)
    k_mean = jnp.mean(kb.astype(jnp.float32), axis=3)
    t = jnp.arange(S_pad)
    cur = t // MOBA_BLOCK
    n_sel = min(MOBA_TOPK, n_blk - 1)
    if n_sel > 0:
        score = jnp.einsum('bhsd,bhnd->bhsn', q.astype(jnp.float32), k_mean)
        past = jnp.arange(n_blk)[None, :] < cur[:, None]
        _, sel = lax.top_k(jnp.where(past, score, -jnp.inf), n_sel)
    else:
        sel = jnp.zeros((B_, H, S_pad, 0), jnp.int32)
    Qc = MOBA_Q_CHUNK
    n_qc = S_pad // Qc
    q_chunks = q.reshape(B_, H, n_qc, Qc, dh).transpose(2, 0, 1, 3, 4)
    sel_chunks = sel.reshape(B_, H, n_qc, Qc, n_sel).transpose(2, 0, 1, 3, 4)

    def chunk(args):
        ci, qc, ix = args
        tq = ci * Qc + jnp.arange(Qc)
        own = (ci * Qc) // MOBA_BLOCK
        k_own = lax.dynamic_index_in_dim(kb, own, axis=2, keepdims=False)
        v_own = lax.dynamic_index_in_dim(vb, own, axis=2, keepdims=False)
        own_pos = own * MOBA_BLOCK + jnp.arange(MOBA_BLOCK)
        m_own = jnp.broadcast_to(own_pos[None, :] <= tq[:, None], (B_, H, Qc, MOBA_BLOCK))
        s_own = jnp.einsum('bhqd,bhkd->bhqk', qc, k_own)
        if n_sel == 0:
            p = masked_softmax(s_own, m_own)
            return jnp.einsum('bhqk,bhkd->bhqd', p.astype(v_own.dtype), v_own)
        kg = gather_blocks(kb, ix)
        vg = gather_blocks(vb, ix)
        n_keys = n_sel * MOBA_BLOCK
        s_sel = jnp.einsum('bhqd,bhqnkd->bhqnk', qc, kg).reshape(B_, H, Qc, n_keys)
        valid = ix < own
        m_sel = jnp.broadcast_to(valid[..., None], (B_, H, Qc, n_sel, MOBA_BLOCK)).reshape(B_, H, Qc, n_keys)
        p = masked_softmax(jnp.concatenate([s_sel, s_own], axis=-1),
                           jnp.concatenate([m_sel, m_own], axis=-1))
        p_sel = p[..., :n_keys].reshape(B_, H, Qc, n_sel, MOBA_BLOCK).astype(vg.dtype)
        p_own = p[..., n_keys:].astype(v_own.dtype)
        return (jnp.einsum('bhqnk,bhqnkd->bhqd', p_sel, vg)
                + jnp.einsum('bhqk,bhkd->bhqd', p_own, v_own))

    o = lax.map(chunk, (jnp.arange(n_qc), q_chunks, sel_chunks))
    o = o.transpose(1, 2, 0, 3, 4).reshape(B_, H, S_pad, dh)[:, :, :S_]
    o = o.transpose(0, 2, 1, 3).reshape(B_, S_, H * dh)
    return o @ w_out

def short_conv_mixer(h, w_in, conv_w, w_out):
    d = h.shape[-1]
    b_gate, c_gate, u = jnp.split(h @ w_in, 3, axis=-1)
    z = c_gate * u
    y = lax.conv_general_dilated(
        z, conv_w[:, None, :].astype(z.dtype), window_strides=(1,),
        padding=[(CONV_WIDTH - 1, 0)],
        dimension_numbers=('NWC', 'WIO', 'NWC'), feature_group_count=d)
    return (b_gate * y) @ w_out

def first_inputs(seed: int = 0) -> dict:
    key = jax.random.key(seed)
    ks = jax.random.split(key, 20)
    f32 = jnp.float32
    n_a = (DEPTH + 2) // 3
    n_b = (DEPTH + 1) // 3
    n_c = DEPTH // 3

    def w(k, shape, fan_in):
        return jax.random.normal(k, shape, f32) * (fan_in ** -0.5)

    def gain(k, shape):
        return 1.0 + 0.02 * jax.random.normal(k, shape, f32)

    return {
        "x": jax.random.normal(ks[0], (BATCH, SEQ, D_MODEL), f32),
        "norm_mix": gain(ks[1], (DEPTH, D_MODEL)),
        "norm_ffn": gain(ks[2], (DEPTH, D_MODEL)),
        "norm_final": gain(ks[3], (D_MODEL,)),
        "ffn_w_gate": w(ks[4], (DEPTH, D_MODEL, D_FF), D_MODEL),
        "ffn_w_up": w(ks[5], (DEPTH, D_MODEL, D_FF), D_MODEL),
        "ffn_w_down": w(ks[6], (DEPTH, D_FF, D_MODEL), D_FF),
        "nsa_w_in": w(ks[7], (n_a, D_MODEL, NSA_IN), D_MODEL),
        "nsa_w_out": w(ks[8], (n_a, NSA_HEADS * HEAD_DIM, D_MODEL), NSA_HEADS * HEAD_DIM),
        "nsa_cmp_pos_k": 0.1 * jax.random.normal(ks[9], (n_a, CMP_BLOCK, HEAD_DIM), f32),
        "nsa_cmp_pos_v": 0.1 * jax.random.normal(ks[10], (n_a, CMP_BLOCK, HEAD_DIM), f32),
        "nsa_cmp_k_w1": w(ks[11], (n_a, CMP_BLOCK * HEAD_DIM, CMP_HIDDEN), CMP_BLOCK * HEAD_DIM),
        "nsa_cmp_k_w2": w(ks[12], (n_a, CMP_HIDDEN, HEAD_DIM), CMP_HIDDEN),
        "nsa_cmp_v_w1": w(ks[13], (n_a, CMP_BLOCK * HEAD_DIM, CMP_HIDDEN), CMP_BLOCK * HEAD_DIM),
        "nsa_cmp_v_w2": w(ks[14], (n_a, CMP_HIDDEN, HEAD_DIM), CMP_HIDDEN),
        "moba_w_in": w(ks[15], (n_b, D_MODEL, 3 * MOBA_HEADS * HEAD_DIM), D_MODEL),
        "moba_w_out": w(ks[16], (n_b, MOBA_HEADS * HEAD_DIM, D_MODEL), MOBA_HEADS * HEAD_DIM),
        "conv_w_in": w(ks[17], (n_c, D_MODEL, 3 * D_MODEL), D_MODEL),
        "conv_w": w(ks[18], (n_c, CONV_WIDTH, D_MODEL), CONV_WIDTH),
        "conv_w_out": w(ks[19], (n_c, D_MODEL, D_MODEL), D_MODEL),
    }

def first_block(x, norm_mix, norm_ffn, norm_final, ffn_w_gate, ffn_w_up, ffn_w_down,
              nsa_w_in, nsa_w_out, nsa_cmp_pos_k, nsa_cmp_pos_v, nsa_cmp_k_w1,
              nsa_cmp_k_w2, nsa_cmp_v_w1, nsa_cmp_v_w2, moba_w_in, moba_w_out,
              conv_w_in, conv_w, conv_w_out):
    h = x
    for i in range(DEPTH):
        kind, j = i % N_MIXERS, i // N_MIXERS
        a = rms_norm(h, norm_mix[i])
        if kind == 0:
            m = nsa_mixer(a, nsa_w_in[j], nsa_w_out[j], nsa_cmp_pos_k[j], nsa_cmp_pos_v[j],
                          nsa_cmp_k_w1[j], nsa_cmp_k_w2[j], nsa_cmp_v_w1[j], nsa_cmp_v_w2[j])
        elif kind == 1:
            m = moba_mixer(a, moba_w_in[j], moba_w_out[j])
        else:
            m = short_conv_mixer(a, conv_w_in[j], conv_w[j], conv_w_out[j])
        h = h + m
        a = rms_norm(h, norm_ffn[i])
        h = h + swiglu(a, ffn_w_gate[i], ffn_w_up[i], ffn_w_down[i])
    return rms_norm(h, norm_final)


DEPTH_2 = 2

MEM_LEN = 256
N_MIXERS_2 = 2
N_LAYERS_A = (DEPTH_2 + 1) // 2
N_LAYERS_B = DEPTH_2 // 2

MEM_HEADS = 4
MEM_HEAD_DIM = 128
MEM_W = MEM_HEADS * MEM_HEAD_DIM

CHUNK = 128
A_WIDTH = D_MODEL
A_GROUPS = 8
A_GROUP_DIM = A_WIDTH // A_GROUPS

MLA_HEADS = 8
Q_LORA = 512
KV_LORA = 256
NOPE_DIM = 128
ROPE_DIM = 64
V_DIM = 128
QK_DIM = NOPE_DIM + ROPE_DIM
ROPE_BASE = 10000.0
Q_BLOCK = 128

N_GROUPS = 4
EXPERTS_PER_GROUP = 8
N_EXPERTS = N_GROUPS * EXPERTS_PER_GROUP
TOP_K = 2
EXPERT_FF = 256
TOKEN_BLOCK = 2048

EPS = 1e-6


def rms_norm_2(x, g):
    xf = x.astype(jnp.float32)
    y = xf * lax.rsqrt(jnp.mean(xf * xf, axis=-1, keepdims=True) + EPS)
    return (y * g.astype(jnp.float32)).astype(x.dtype)

def layer_norm(x, g, b):
    xf = x.astype(jnp.float32)
    mu = jnp.mean(xf, axis=-1, keepdims=True)
    var = jnp.mean(jnp.square(xf - mu), axis=-1, keepdims=True)
    y = (xf - mu) * lax.rsqrt(var + EPS)
    return (y * g.astype(jnp.float32) + b.astype(jnp.float32)).astype(x.dtype)

def rope(x, pos):
    r = x.shape[-1]
    half = r // 2
    inv = ROPE_BASE ** (-(jnp.arange(half, dtype=jnp.float32) * 2.0 / r))
    ang = pos.astype(jnp.float32)[:, :, None, None] * inv
    cos, sin = jnp.cos(ang), jnp.sin(ang)
    xf = x.astype(jnp.float32)
    x1, x2 = xf[..., :half], xf[..., half:]
    return jnp.concatenate([x1 * cos - x2 * sin, x1 * sin + x2 * cos], axis=-1).astype(x.dtype)

def causal_block_attention(q, k, v):
    b, s, h, dk = q.shape
    nb = s // Q_BLOCK
    scale = dk ** -0.5
    qb = q.reshape(b, nb, Q_BLOCK, h, dk).transpose(1, 0, 2, 3, 4)
    kpos = jnp.arange(s)
    neg = jnp.finfo(jnp.float32).min

    def one_block(args):
        i, qi = args
        sc = jnp.einsum('bqhd,bkhd->bhqk', qi, k, preferred_element_type=jnp.float32) * scale
        qpos = i * Q_BLOCK + jnp.arange(Q_BLOCK)
        sc = jnp.where(kpos[None, :] <= qpos[:, None], sc, neg)
        p = jax.nn.softmax(sc, axis=-1)
        return jnp.einsum('bhqk,bkhd->bqhd', p.astype(v.dtype), v)

    out = lax.map(one_block, (jnp.arange(nb), qb))
    return out.transpose(1, 0, 2, 3, 4).reshape(b, s, h, v.shape[-1])

def memory_attention(q, mem_k, mem_v, qn_g, kn_g):
    q = rms_norm_2(q, qn_g)
    k = rms_norm_2(mem_k, kn_g)
    sc = jnp.einsum('bshd,bmhd->bhsm', q, k, preferred_element_type=jnp.float32) * (MEM_HEAD_DIM ** -0.5)
    p = jax.nn.softmax(sc, axis=-1)
    o = jnp.einsum('bhsm,bmhd->bshd', p.astype(mem_v.dtype), mem_v)
    return o.reshape(q.shape[0], q.shape[1], MEM_W)

def gmlp_mixer(h, w_in, ln_g, ln_b, w_s, b_s):
    b, s, _ = h.shape
    z = h @ w_in
    uv = jax.nn.gelu(z[..., :2 * A_WIDTH], approximate=False)
    u, v = uv[..., :A_WIDTH], uv[..., A_WIDTH:]
    q_mem = z[..., 2 * A_WIDTH:].reshape(b, s, MEM_HEADS, MEM_HEAD_DIM)
    v = layer_norm(v, ln_g, ln_b)
    vc = v.reshape(b, s // CHUNK, CHUNK, A_GROUPS, A_GROUP_DIM)
    causal = jnp.tril(jnp.ones((CHUNK, CHUNK), dtype=bool))
    w = jnp.where(causal[None], w_s, jnp.zeros((), w_s.dtype))
    mixed = jnp.einsum('gts,bnsgc->bntgc', w, vc) + b_s.T[None, None, :, :, None]
    return u * mixed.reshape(b, s, A_WIDTH), q_mem

def mla_mixer(h, positions, w_in, q_norm_g, kv_norm_g, w_q_up, w_kv_up, qn_g, kn_g):
    b, s, _ = h.shape
    z = h @ w_in
    o1 = Q_LORA
    o2 = o1 + KV_LORA
    o3 = o2 + ROPE_DIM
    cq = rms_norm_2(z[..., :o1], q_norm_g)
    ckv = rms_norm_2(z[..., o1:o2], kv_norm_g)
    k_rope = z[..., o2:o3]
    q_mem = z[..., o3:].reshape(b, s, MEM_HEADS, MEM_HEAD_DIM)
    q = (cq @ w_q_up).reshape(b, s, MLA_HEADS, QK_DIM)
    kv = (ckv @ w_kv_up).reshape(b, s, MLA_HEADS, NOPE_DIM + V_DIM)
    k_nope, v = kv[..., :NOPE_DIM], kv[..., NOPE_DIM:]
    k_rope = jnp.broadcast_to(k_rope[:, :, None, :], (b, s, MLA_HEADS, ROPE_DIM))
    k = jnp.concatenate([k_nope, k_rope], axis=-1)
    q = rms_norm_2(q, qn_g)
    k = rms_norm_2(k, kn_g)
    q = jnp.concatenate([q[..., :NOPE_DIM], rope(q[..., NOPE_DIM:], positions)], axis=-1)
    k = jnp.concatenate([k[..., :NOPE_DIM], rope(k[..., NOPE_DIM:], positions)], axis=-1)
    o = causal_block_attention(q, k, v)
    return o.reshape(b, s, MLA_HEADS * V_DIM), q_mem

def hierarchical_moe(h, w_group, b_group, w_expert, b_expert, w_gate, w_up, w_down):
    b, s, d = h.shape
    t = h.reshape(-1, d)
    n = t.shape[0]
    g_prob = jax.nn.softmax((t @ w_group).astype(jnp.float32) + b_group.astype(jnp.float32), axis=-1)
    g_idx = jnp.argmax(g_prob, axis=-1)
    g_w = jnp.take_along_axis(g_prob, g_idx[:, None], axis=-1)
    e_logits = ((t @ w_expert).astype(jnp.float32) + b_expert.astype(jnp.float32))
    e_logits = e_logits.reshape(n, N_GROUPS, EXPERTS_PER_GROUP)
    e_sel = jnp.take_along_axis(e_logits, g_idx[:, None, None], axis=1)[:, 0]
    e_prob = jax.nn.softmax(e_sel, axis=-1)
    top_w, top_i = lax.top_k(e_prob, TOP_K)
    top_w = top_w / jnp.sum(top_w, axis=-1, keepdims=True)
    expert_id = g_idx[:, None] * EXPERTS_PER_GROUP + top_i
    weights = g_w * top_w
    combine = jnp.sum(jax.nn.one_hot(expert_id, N_EXPERTS, dtype=jnp.float32) * weights[..., None], axis=1)
    tb = math.gcd(n, TOKEN_BLOCK)
    nb = n // tb

    def expert_block(args):
        xb, cb = args
        gate = jnp.einsum('td,edf->tef', xb, w_gate)
        up = jnp.einsum('td,edf->tef', xb, w_up)
        act = jax.nn.silu(gate) * up * cb[..., None].astype(xb.dtype)
        return jnp.einsum('tef,efd->td', act, w_down)

    y = lax.map(expert_block, (t.reshape(nb, tb, d), combine.reshape(nb, tb, N_EXPERTS)))
    return y.reshape(b, s, d)

def second_inputs(seed: int = 0) -> dict:
    key = jax.random.key(seed)
    ks = iter(jax.random.split(key, 40))
    f32 = jnp.float32

    def nrm(shape, scale):
        return jax.random.normal(next(ks), shape, f32) * scale

    def gain(shape):
        return 1.0 + 0.05 * jax.random.normal(next(ks), shape, f32)

    D = D_MODEL
    a_in = 2 * A_WIDTH + MEM_W
    a_out = A_WIDTH + MEM_W
    b_in = Q_LORA + KV_LORA + ROPE_DIM + MEM_W
    b_out = MLA_HEADS * V_DIM + MEM_W
    x = jax.random.normal(next(ks), (BATCH, SEQ, D), f32)
    mem = jax.random.normal(next(ks), (BATCH, MEM_LEN, D), f32)
    offsets = jax.random.randint(next(ks), (BATCH, 1), 0, 4096, dtype=jnp.int32)
    positions = offsets + jnp.arange(SEQ, dtype=jnp.int32)[None, :]
    return {
        "x": x,
        "mem": mem,
        "positions": positions,
        "mem_norm_g": gain((D,)),
        "w_mem_kv": nrm((D, 2 * MEM_W), D ** -0.5),
        "mem_qn_g": gain((DEPTH_2, MEM_HEAD_DIM)),
        "mem_kn_g": gain((DEPTH_2, MEM_HEAD_DIM)),
        "norm1_g": gain((DEPTH_2, D)),
        "norm2_g": gain((DEPTH_2, D)),
        "a_w_in": nrm((N_LAYERS_A, D, a_in), D ** -0.5),
        "a_ln_g": gain((N_LAYERS_A, A_WIDTH)),
        "a_ln_b": nrm((N_LAYERS_A, A_WIDTH), 0.02),
        "a_w_s": nrm((N_LAYERS_A, A_GROUPS, CHUNK, CHUNK), CHUNK ** -0.5),
        "a_b_s": gain((N_LAYERS_A, A_GROUPS, CHUNK)),
        "a_w_out": nrm((N_LAYERS_A, a_out, D), a_out ** -0.5),
        "b_w_in": nrm((N_LAYERS_B, D, b_in), D ** -0.5),
        "b_q_norm_g": gain((N_LAYERS_B, Q_LORA)),
        "b_kv_norm_g": gain((N_LAYERS_B, KV_LORA)),
        "b_w_q_up": nrm((N_LAYERS_B, Q_LORA, MLA_HEADS * QK_DIM), Q_LORA ** -0.5),
        "b_w_kv_up": nrm((N_LAYERS_B, KV_LORA, MLA_HEADS * (NOPE_DIM + V_DIM)), KV_LORA ** -0.5),
        "b_qn_g": gain((N_LAYERS_B, QK_DIM)),
        "b_kn_g": gain((N_LAYERS_B, QK_DIM)),
        "b_w_out": nrm((N_LAYERS_B, b_out, D), b_out ** -0.5),
        "moe_w_group": nrm((DEPTH_2, D, N_GROUPS), D ** -0.5),
        "moe_b_group": nrm((DEPTH_2, N_GROUPS), 0.01),
        "moe_w_expert": nrm((DEPTH_2, D, N_EXPERTS), D ** -0.5),
        "moe_b_expert": nrm((DEPTH_2, N_EXPERTS), 0.01),
        "moe_w_gate": nrm((DEPTH_2, N_EXPERTS, D, EXPERT_FF), D ** -0.5),
        "moe_w_up": nrm((DEPTH_2, N_EXPERTS, D, EXPERT_FF), D ** -0.5),
        "moe_w_down": nrm((DEPTH_2, N_EXPERTS, EXPERT_FF, D), EXPERT_FF ** -0.5),
    }

def second_block(x, mem, positions, mem_norm_g, w_mem_kv, mem_qn_g, mem_kn_g, norm1_g, norm2_g,
              a_w_in, a_ln_g, a_ln_b, a_w_s, a_b_s, a_w_out,
              b_w_in, b_q_norm_g, b_kv_norm_g, b_w_q_up, b_w_kv_up, b_qn_g, b_kn_g, b_w_out,
              moe_w_group, moe_b_group, moe_w_expert, moe_b_expert, moe_w_gate, moe_w_up, moe_w_down):
    b = x.shape[0]
    m = mem.shape[1]
    mem_kv = rms_norm_2(mem, mem_norm_g) @ w_mem_kv
    mem_k = mem_kv[..., :MEM_W].reshape(b, m, MEM_HEADS, MEM_HEAD_DIM)
    mem_v = mem_kv[..., MEM_W:].reshape(b, m, MEM_HEADS, MEM_HEAD_DIM)
    for i in range(DEPTH_2):
        h = rms_norm_2(x, norm1_g[i])
        j = i // N_MIXERS_2
        if i % N_MIXERS_2 == 0:
            mix, q_mem = gmlp_mixer(h, a_w_in[j], a_ln_g[j], a_ln_b[j], a_w_s[j], a_b_s[j])
            w_out = a_w_out[j]
        else:
            mix, q_mem = mla_mixer(h, positions, b_w_in[j], b_q_norm_g[j], b_kv_norm_g[j],
                                   b_w_q_up[j], b_w_kv_up[j], b_qn_g[j], b_kn_g[j])
            w_out = b_w_out[j]
        mem_out = memory_attention(q_mem, mem_k, mem_v, mem_qn_g[i], mem_kn_g[i])
        x = x + jnp.concatenate([mix, mem_out], axis=-1) @ w_out
        x = x + hierarchical_moe(rms_norm_2(x, norm2_g[i]), moe_w_group[i], moe_b_group[i],
                                 moe_w_expert[i], moe_b_expert[i], moe_w_gate[i],
                                 moe_w_up[i], moe_w_down[i])
    return x


def setup_inputs(seed=0):
    out = dict(first_inputs(seed))
    for name, value in second_inputs(seed + 1).items():
        if name != "x":
            out[name + "_2"] = value
    return out


def reference(
    x, norm_mix, norm_ffn, norm_final, ffn_w_gate, ffn_w_up, ffn_w_down, nsa_w_in, nsa_w_out,
    nsa_cmp_pos_k, nsa_cmp_pos_v, nsa_cmp_k_w1, nsa_cmp_k_w2, nsa_cmp_v_w1, nsa_cmp_v_w2,
    moba_w_in, moba_w_out, conv_w_in, conv_w, conv_w_out, mem_2, positions_2, mem_norm_g_2,
    w_mem_kv_2, mem_qn_g_2, mem_kn_g_2, norm1_g_2, norm2_g_2, a_w_in_2, a_ln_g_2, a_ln_b_2,
    a_w_s_2, a_b_s_2, a_w_out_2, b_w_in_2, b_q_norm_g_2, b_kv_norm_g_2, b_w_q_up_2, b_w_kv_up_2,
    b_qn_g_2, b_kn_g_2, b_w_out_2, moe_w_group_2, moe_b_group_2, moe_w_expert_2, moe_b_expert_2,
    moe_w_gate_2, moe_w_up_2, moe_w_down_2,
):
    x = first_block(
        x, norm_mix, norm_ffn, norm_final, ffn_w_gate, ffn_w_up, ffn_w_down, nsa_w_in,
        nsa_w_out, nsa_cmp_pos_k, nsa_cmp_pos_v, nsa_cmp_k_w1, nsa_cmp_k_w2, nsa_cmp_v_w1,
        nsa_cmp_v_w2, moba_w_in, moba_w_out, conv_w_in, conv_w, conv_w_out,
    )
    return second_block(
        x, mem_2, positions_2, mem_norm_g_2, w_mem_kv_2, mem_qn_g_2, mem_kn_g_2, norm1_g_2,
        norm2_g_2, a_w_in_2, a_ln_g_2, a_ln_b_2, a_w_s_2, a_b_s_2, a_w_out_2, b_w_in_2,
        b_q_norm_g_2, b_kv_norm_g_2, b_w_q_up_2, b_w_kv_up_2, b_qn_g_2, b_kn_g_2, b_w_out_2,
        moe_w_group_2, moe_b_group_2, moe_w_expert_2, moe_b_expert_2, moe_w_gate_2, moe_w_up_2,
        moe_w_down_2,
    )


_drawn_inputs = setup_inputs


def setup_inputs(seed=0):
    import zlib

    import numpy as np

    out = dict(_drawn_inputs(seed))
    spreads = {}
    factors = {'mem_norm_g_2': 3.344,
     'mem_qn_g_2': 4.887,
     'mem_kn_g_2': 3.466,
     'a_ln_b_2': 2.711,
     'b_q_norm_g_2': 3.79,
     'b_qn_g_2': 3.256,
     'b_kn_g_2': 5.362,
     'moe_b_group_2': 3.065,
     'moe_b_expert_2': 3.12}
    for name, (base, spread) in spreads.items():
        noise = np.random.default_rng([zlib.crc32(name.encode()), seed]).standard_normal(out[name].shape)
        drawn = base * np.exp(spread * noise) if base else spread * noise
        out[name] = __import__('jax').numpy.asarray(drawn.astype(out[name].dtype))
    for name, factor in factors.items():
        out[name] = (out[name] * factor).astype(out[name].dtype)
    return out
```

```python
import concourse.bass as bass
from concourse import mybir
from contextlib import ExitStack
import numpy as np


def const_table():
    p = np.arange(128)
    parts, at, n = {}, {}, 0

    def add(name, a):
        nonlocal n
        parts[name] = np.broadcast_to(np.asarray(a, np.float32), (128, np.asarray(a).shape[-1]))
        at[name] = n
        n += parts[name].shape[1]

    add("ident", np.eye(128))
    add("ones", np.ones((128, 128)))
    tri = np.where(p[None, :] <= p[:, None], 0.0, -1e30)
    add("mask", np.concatenate([np.zeros((128, 256)), tri], 1))
    c = np.arange(16)
    cm = [np.where((16 * c[None] + 31 <= p[:, None] + 128 * q) & (c[None] < 15), 0.0, -1e30) for q in range(2)]
    add("cmask", np.concatenate(cm, 1))
    add("before", (p[:, None] < p[None, :]).astype(np.float32))
    add("iota", np.arange(32)[None, :])
    add("inv", (10000.0 ** (-(np.arange(32) * 2.0 / 64))).astype(np.float32)[None, :])
    add("eps", np.full((128, 1), 1e-6))
    return np.ascontiguousarray(np.concatenate(list(parts.values()), 1)), at, n


CONST, CAT, NCONST = const_table()

PARAMS = [("norm_mix", 32), ("norm_ffn", 32), ("norm_final", 8), ("mem_norm", 8), ("norm1", 16), ("norm2", 16),
          ("mem_qn", 2), ("mem_kn", 2), ("conv_w", 24), ("q_norm", 4), ("kv_norm", 2), ("qn_nope", 1), ("kn_nope", 1),
          ("qn_rope", 64), ("kn_rope", 64), ("cmp_pos", 128), ("cmp_w2", 512), ("r_bias", 72)]
PAT, NPARAM = {}, 0
for _name, _n in PARAMS:
    PAT[_name] = NPARAM
    NPARAM += _n

NRAW, NW = 12, 4
NSCR = 13824


def blocks_kernel(nc, a, out, upto=None):
    F32, F32R, I32 = mybir.dt.float32, mybir.dt.float32r, mybir.dt.int32
    ALU, ACT, AX = mybir.AluOpType, mybir.ActivationFunctionType, mybir.AxisListType
    ctx = ExitStack()

    def sb(name, shape, dt=F32):
        return ctx.enter_context(nc.sbuf_tensor(name, shape, dt))

    def sem(name):
        return ctx.enter_context(nc.semaphore(name))

    def call(f, *args, **kw):
        return lambda: f(*args, **kw)

    class Queue:

        def __init__(self, name, e):
            self.sem, self.e, self.ops, self.count, self.met = sem(name), e, [], 0, {}

        def wait(self, *tokens):
            for t in tokens:
                if t is not None and self.met.get(t[0].name, 0) < t[1]:
                    self.met[t[0].name] = t[1]
                    self.ops.append(call(self.e.wait_ge, t[0], t[1]))

        def run(self, op, *tokens):
            self.wait(*tokens)
            self.ops.append(op)

        def do(self, op, *tokens):
            self.wait(*tokens)
            self.count += 1
            self.ops.append(lambda: op().then_inc(self.sem, 1))
            return (self.sem, self.count)

        @property
        def last(self):
            return (self.sem, self.count) if self.count else None

        def dma(self, dst, src, s, *tokens):
            self.wait(*tokens)
            s[1] += 16
            v = s[1]
            self.ops.append(lambda: self.e.dma_start(dst, src).then_inc(s[0], 16))
            return (s[0], v)

    with ctx:
        RAW = sb("RAW", [128, NRAW, 1024])
        WH = sb("WH", [128, NW, 1024], F32R)
        WL = sb("WL", [128, NW, 1024], F32R)
        XH = [sb("XH0", [128, 8, 256], F32R), sb("XH1", [128, 12, 256], F32R)]
        XL = [sb("XL0", [128, 8, 256], F32R), sb("XL1", [128, 12, 256], F32R)]
        H = sb("H", [128, 8, 256])
        GH = sb("GH", [128, 3, 256], F32R)
        GL = sb("GL", [128, 3, 256], F32R)
        CST = sb("CST", [128, NCONST])
        PRM = sb("PRM", [128, NPARAM])
        RB = sb("RB", [128, 2, 256])
        RC = sb("RC", [128, 2, 2])
        SQ = sb("SQ", [128, 2, 256])
        ACC = sb("ACC", [128, 256])
        NT = sb("NT", [128, 3, 256])
        ST = sb("ST", [128, 4, 24])
        SM = sb("SM", [128, 320])
        ROT = sb("ROT", [128, 384])
        POSI = sb("POSI", [128, 2], I32)
        FLAG = sb("FLAG", [128, 2], I32)
        SCR = sb("SCR", [128, NSCR])
        PS = ctx.enter_context(nc.psum_tensor("PS", [128, 8, 512], F32))

        pe, act, dve, pool, sp = (Queue(*n) for n in (
            ("s_pe", nc.tensor), ("s_act", nc.scalar), ("s_dve", nc.vector), ("s_pool", nc.gpsimd), ("s_sp", nc.sync)))
        everyone = (pe, act, dve, pool)

        def cst(name, n, at=0):
            return CST[:, CAT[name] + at:CAT[name] + at + n]

        def prm(name, at=0, n=1):
            return PRM[:, PAT[name] + at:PAT[name] + at + n]

        def lasts():
            return [q.last for q in everyone]

        def f32(ap):
            return ap.bitcast(F32)

        units, dense_ids, raw_ids = [], [], []

        def section(name, j):
            for b in range(a[name].shape[1]):
                dense_ids.append(len(units))
                units.append((a[name][j, b], 1))

        def raws(name, j, n):
            for b in range(a[name].shape[1]):
                raw_ids.append(len(units))
                units.append((a[name][j, b], n))

        bounds = {}
        for i in range(4):
            if i % 3 == 0:
                section("nsa_in1", i // 3)
                raws("w_cmp", i // 3, 1)
                section("nsa_in2", i // 3)
                section("nsa_out", i // 3)
            elif i % 3 == 1:
                section("moba_in", 0)
                section("moba_out", 0)
            else:
                section("conv_in", 0)
                section("conv_out", 0)
            section("ffn", i)
        section("mem_kv", 0)
        section("a_in", 0)
        section("a_out", 0)
        bounds[0] = len(dense_ids)
        raws("router", 0, 1)
        raws("moe", 0, 2)
        section("b_in", 0)
        section("b_q_up", 0)
        section("b_kv_up", 0)
        section("b_out", 0)
        bounds[1] = len(dense_ids)
        raws("router", 1, 1)
        raws("moe", 1, 2)

        slot_sem = [[sem(f"s_raw{i}"), 0] for i in range(NRAW)]
        slot_free = [[] for _ in range(NRAW)]
        where = {}
        st = dict(issued=0, cursor=0, prepped=0, limit=bounds[0], raw=0)

        def pump():
            while st["issued"] < len(units):
                src, n = units[st["issued"]]
                c = st["cursor"]
                if n == 2 and (c % 2 or c + 2 > NRAW):
                    c = (c + 1) % NRAW
                    if c % 2 or c + 2 > NRAW:
                        c = 0
                if any(slot_free[c + i] is None for i in range(n)):
                    return
                tokens = [t for i in range(n) for t in slot_free[c + i]]
                dst = RAW[:, c, :] if n == 1 else RAW[:, c:c + 2, :].rearrange("p a b -> p (a b)")
                where[st["issued"]] = (c, n, sp.dma(dst, src, slot_sem[c], *tokens))
                for i in range(n):
                    slot_free[c + i] = None
                st["cursor"] = (c + n) % NRAW
                st["issued"] += 1

        def give_back(u, tokens):
            c, n, _ = where[u]
            for i in range(n):
                slot_free[c + i] = list(tokens)
            pump()

        w_free = [[] for _ in range(NW)]
        w_ready = {}
        taken = dict(block=0, at=0)

        def refill(n=99):
            while n and st["prepped"] < st["limit"] and w_free[st["prepped"] % NW] is not None:
                b = st["prepped"]
                u = dense_ids[b]
                if u not in where:
                    return
                c, _, loaded = where[u]
                s = b % NW
                raw, wh, wl = RAW[:, c, :], WH[:, s, :], WL[:, s, :]
                t = act.do(call(act.e.activation, wh, raw, ACT.Copy), loaded, *w_free[s])
                t = dve.do(call(dve.e.tensor_tensor, wl, raw, f32(wh), ALU.subtract), t)
                w_free[s] = None
                w_ready[b] = t
                st["prepped"] += 1
                n -= 1
                give_back(u, [t])

        def piece(n):
            b = taken["block"]
            if b not in w_ready:
                refill()
            pe.wait(w_ready[b])
            s, x = b % NW, taken["at"]
            taken["at"] += n
            assert taken["at"] <= 1024
            return WH[:, s, x:x + n], WL[:, s, x:x + n]

        def block_done(token):
            assert token[0] is pe.sem
            w_free[taken["block"] % NW] = [token]
            taken["block"] += 1
            taken["at"] = 0

        def next_raw():
            u = raw_ids[st["raw"]]
            st["raw"] += 1
            c, n, loaded = where[u]
            ap = RAW[:, c, :] if n == 1 else RAW[:, c:c + 2, :].rearrange("p a b -> p (a b)")
            return u, ap, loaded

        bank_free = [[] for _ in range(8)]
        turn = dict(b=0)

        def next_bank(banks):
            b = banks[turn["b"] % len(banks)]
            turn["b"] += 1
            return b

        def three(o, wh, wl, xh, xl, start, stop, signal, swap=False):
            for i, (l, r) in enumerate(((wh, xh), (wh, xl), (wl, xh))):
                if swap:
                    l, r = r, l
                f = (call(pe.e.matmul, o, l, r, start=start and i == 0, stop=stop and i == 2,
                                                     skip_group_check=True))
                if signal and i == 2:
                    return pe.do(f)
                pe.run(f)

        def mtile(xi, ks, o, x_tokens=None, first=True):
            for n, k in enumerate(ks):
                wh, wl = piece(128)
                if x_tokens is not None:
                    pe.wait(x_tokens[k])
                full = taken["at"] == 1024
                t = three(o, wh, wl, XH[xi][:, k, :], XL[xi][:, k, :], n == 0, n == len(ks) - 1, full or n == len(ks) - 1)
                if full:
                    block_done(t)
            return t

        def vtile(xi, ks, cols, per_block, banks, x_tokens=None):
            for n, k in enumerate(ks):
                wh, wl = piece(cols)
                if x_tokens is not None:
                    pe.wait(x_tokens[k])
                end = (n + 1) % per_block == 0 or n == len(ks) - 1
                for tt in range(2):
                    sl = slice(128 * tt, 128 * (tt + 1))
                    t = three(PS[:, banks[tt], 0:cols], wh, wl, XH[xi][:, k, sl], XL[xi][:, k, sl],
                              n == 0, n == len(ks) - 1, tt == 1, swap=True)
                if end:
                    block_done(t)
            return t

        once = [sem("s_in"), 0]
        t_cst = sp.dma(CST[:, :], a["cst"], once)
        once2 = [sem("s_in2"), 0]
        t_prm = sp.dma(PRM[:, :], a["prm"], once2)
        once3 = [sem("s_in3"), 0]
        t_x = sp.dma(H[:, :, :].rearrange("p k t -> p (k t)"), a["xT"], once3)
        once4 = [sem("s_in4"), 0]
        t_pos = sp.dma(POSI[:, :], a["pos"], once4)
        pump()
        for q in (pe, act, dve, pool):
            q.wait(t_cst, t_prm)

        ident = cst("ident", 128)
        ones = cst("ones", 128)
        eps = cst("eps", 1)

        def scr(at, n, **dims):
            return SCR[:, at:at + n]

        h_tok = [t_x] * 8
        x_tok = {0: [None] * 12, 1: [None] * 12}
        x_free = {0: [], 1: []}
        sq_tok = [None, None]
        norm = dict(acc=None, n=0, rb=0, readers=[])

        def split_into(xi, k, src, tokens, gain=None, src_psum=False):
            xh, xl = XH[xi][:, k, :], XL[xi][:, k, :]
            if gain is None:
                t1 = act.do(call(act.e.activation, xh, src, ACT.Copy), *tokens, *x_free[xi])
                t2 = dve.do(call(dve.e.tensor_tensor, xl, src, f32(xh), ALU.subtract), t1)
            else:
                t1 = act.do(call(act.e.activation, xh, src, ACT.Copy, scale=gain), *tokens, *x_free[xi])
                t2 = dve.do(call(dve.e.scalar_tensor_tensor, xl, src, gain, f32(xh), ALU.mult, ALU.subtract), t1)
            x_tok[xi][k] = t2
            return t2

        def square_into(k, src, tokens):
            if k == 0:
                norm["acc"] = act.do(call(act.e.activation, ACC[:, :], src, ACT.Square), *tokens, norm["acc"],
                                     *norm["readers"])
                return
            b = k % 2
            t = act.do(call(act.e.activation, SQ[:, b, :], src, ACT.Square), *tokens, sq_tok[b])
            t = pool.do(call(pool.e.tensor_tensor, ACC[:, :], ACC[:, :], SQ[:, b, :], ALU.add), t, norm["acc"], pool.last)
            sq_tok[b] = t
            norm["acc"] = t

        nt_free = [[], [], []]

        def newton(y, y0, x, tok, tmp):
            t = dve.do(call(dve.e.tensor_tensor, tmp, y0, y0, ALU.mult), tok)
            t = dve.do(call(dve.e.tensor_tensor, tmp, tmp, x, ALU.mult), t)
            t = dve.do(call(dve.e.tensor_scalar, tmp, tmp, -0.5, 1.5, op0=ALU.mult, op1=ALU.add), t)
            return dve.do(call(dve.e.tensor_tensor, y, tmp, y0, ALU.mult), t)

        def rstd_bcast(bank, mean=1024):
            i = norm["rb"] = 1 - norm["rb"]
            o = PS[:, bank, 0:256]
            t = pe.do(call(pe.e.matmul, o, ones, ACC[:, :], start=True, stop=True), norm["acc"], *bank_free[bank])
            norm["readers"] = [t]
            y0, x, tmp = NT[:, 0, :], NT[:, 1, :], NT[:, 2, :]
            t1 = dve.do(call(dve.e.tensor_scalar, x, o, 1.0 / mean, 1e-6, op0=ALU.mult, op1=ALU.add), t, dve.last)
            t2 = act.do(call(act.e.activation, y0, x, ACT.Abs_reciprocal_sqrt), t1)
            bank_free[bank] = [t1]
            norm["t_rb"] = newton(RB[:, i, :], y0, x, t2, tmp)
            return RB[:, i, :], norm["t_rb"]

        def rstd_cols(bank, dst, mean=1024):
            for tt in range(2):
                o = PS[:, bank, tt:tt + 1]
                t = pe.do(call(pe.e.matmul, o, ACC[:, 128 * tt:128 * tt + 128], ones[:, 0:1], start=True,
                                                         stop=True, skip_group_check=True),
                          norm["acc"], *bank_free[bank])
            norm["readers"] = [t]
            x, y0, tmp = ST[:, 0, 0:2], ST[:, 0, 2:4], ST[:, 0, 4:6]
            t1 = dve.do(call(dve.e.tensor_scalar, x, PS[:, bank, 0:2], 1.0 / mean, 1e-6, op0=ALU.mult, op1=ALU.add),
                        t, dve.last)
            bank_free[bank] = [t1]
            t2 = act.do(call(act.e.activation, y0, x, ACT.Abs_reciprocal_sqrt), t1)
            norm["t_rc"] = newton(dst, y0, x, t2, tmp)
            return norm["t_rc"]

        def cols_of_rb(bank, rb, t_rb):
            for tt in range(2):
                o = PS[:, bank, 128 * tt:128 * tt + 128]
                t = pe.do(call(pe.e.transpose, o, rb[:, 128 * tt:128 * tt + 128], ident), t_rb,
                          *bank_free[bank])
            src = PS[:, bank, 0:256].rearrange("p (a b) -> p a b", a=2)[:, :, 0:1]
            dst = RC[:, 0, :].unsqueeze(2)
            t = dve.do(call(dve.e.tensor_copy, dst, src), t, dve.last)
            bank_free[bank] = [t]
            return t

        def add_residual(k, o, t, bank_release=None):
            t1 = dve.do(call(dve.e.tensor_tensor, H[:, k, :], o, H[:, k, :], ALU.add), t, h_tok[k])
            h_tok[k] = t1
            return t1

        def new_h(k, gain, split=True):
            if split:
                split_into(0, k, H[:, k, :], [h_tok[k]], gain)
            square_into(k, H[:, k, :], [h_tok[k]])

        def out_proj(kt, gain_name, gain_at, also=None):
            for m in range(8):
                b = next_bank((0, 1, 2, 3))
                pe.wait(*bank_free[b])
                o = PS[:, b, 0:256]
                t = mtile(1, range(kt), o, x_tok[1])
                if m == 7:
                    x_free[1] = [t]
                t1 = add_residual(m, o, t)
                bank_free[b] = [t1]
                new_h(m, prm(gain_name, gain_at + m))
                if also:
                    also(m)
                refill()

        def ffn(i, next_gain, hook=None):
            def temp(b, o):
                return SCR[:, 512 * o + 256 * b:512 * o + 256 * b + 256]

            rb = t_rb = None
            acts = {}
            down_tok = {}
            g_free = [[], [], []]

            def gate_up(f):
                b = next_bank((0, 1, 2, 3))
                pe.wait(*bank_free[b])
                tg = mtile(0, range(8), PS[:, b, 0:256], x_tok[0])
                tu = mtile(0, range(8), PS[:, b, 256:512], x_tok[0])
                return b, tu

            def chain(f, b, tu):
                p = f % 2
                t1, sg, t2 = temp(p, 0), temp(p, 1), temp(p, 2)
                ta = dve.do(call(dve.e.tensor_tensor, t1, PS[:, b, 0:256], rb, ALU.mult), tu, t_rb)
                tb = dve.do(call(dve.e.tensor_tensor, t2, PS[:, b, 256:512], rb, ALU.mult))
                bank_free[b] = [tb]
                ts = act.do(call(act.e.activation, sg, t1, ACT.Silu), ta)
                refill(1)
                tc = dve.do(call(dve.e.tensor_tensor, t2, sg, t2, ALU.mult), ts, tb)
                s = f % 3
                th = act.do(call(act.e.activation, GH[:, s, :], t2, ACT.Copy), tc, *g_free[s])
                refill(1)
                acts[f] = dve.do(call(dve.e.tensor_tensor, GL[:, s, :], t2, f32(GH[:, s, :]), ALU.subtract), th)

            def down(fs):
                b0 = taken["block"]
                for f in fs:
                    pe.wait(acts[f])
                for j in range(len(fs)):
                    if b0 + j not in w_ready:
                        refill()
                    pe.wait(w_ready[b0 + j])
                for d in range(8):
                    bank = 4 + d // 2
                    o = PS[:, bank, 256 * (d % 2):256 * (d % 2) + 256]
                    if fs[0] == 0 and d % 2 == 0:
                        pe.wait(*bank_free[bank])
                    for j, f in enumerate(fs):
                        s = (b0 + j) % NW
                        last = f == 21
                        for n, (w, x) in enumerate(((WH, GH), (WH, GL), (WL, GH))):
                            op = (call(pe.e.matmul, 
                                o, w[:, s, 128 * d:128 * d + 128], x[:, f % 3, :],
                                start=(f == 0 and n == 0 and d % 2 == 0), stop=(f == 21 and n == 2),
                                skip_group_check=True))
                            if n == 2 and (last or d == 7):
                                t = pe.do(op)
                            else:
                                pe.run(op)
                        if d == 7:
                            w_free[s] = [t]
                            g_free[f % 3] = [t]
                    if fs[-1] == 21:
                        down_tok[d] = t
                taken["block"] += len(fs)

            for f in range(22):
                b, tu = gate_up(f)
                if f == 0:
                    rb, t_rb = rstd_bcast(7)
                if f == 21:
                    x_free[0] = [tu]
                if hook:
                    hook(f)
                chain(f, b, tu)
                if 1 <= f <= 19:
                    down([f - 1])
                refill()
            down([19, 20, 21])
            for d in range(8):
                bank = 4 + d // 2
                o = PS[:, bank, 256 * (d % 2):256 * (d % 2) + 256]
                t1 = add_residual(d, o, down_tok[d | 1])
                bank_free[bank] = [t1]
                if next_gain is not None:
                    new_h(d, prm(*next_gain(d)))
                else:
                    new_h(d, None, split=False)
                if d % 2:
                    refill(1)
            refill()

        def attention(n, unit, P_at, PT_at, width, xi, finish, causal=True):
            heads = len(unit(0)["heads"])
            NP = 3 if heads * width * 3 <= PT_at - P_at else 2
            n0, n1 = (128, 256) if causal else (256, 256)
            sbank = (lambda u, h: (u % 2) * heads + h) if heads == 2 else (lambda u, h: u % 3)
            tbank = (lambda u, h: 4 + h) if heads == 2 else (lambda u, h: 4 + u % 2)
            obank = lambda j: 6 + j % 2
            Pb = lambda u, h: SCR[:, P_at + ((u % NP) * heads + h) * width:P_at + ((u % NP) * heads + h) * width + width]
            Tb = lambda u, h: SCR[:, PT_at + ((u % 2) * heads + h) * width:PT_at + ((u % 2) * heads + h) * width + width]
            tok = {}
            p_free = [[t for t in lasts()] for _ in range(NP)]
            t_free = [[t for t in lasts()] for _ in range(2)]

            def A(u):
                w = unit(u)
                for h, hd in enumerate(w["heads"]):
                    b = sbank(u, h)
                    pe.wait(*bank_free[b])
                    ms = hd["score"]
                    for i, (x, nn, l, r, s0, s1) in enumerate(ms):
                        f = call(pe.e.matmul, 
                            PS[:, b, x:x + nn], l, r, start=s0, stop=s1, skip_group_check=True)
                        pe.wait(*hd.get("wait", ()))
                        if i == len(ms) - 1:
                            tok["A", u, h] = pe.do(f)
                        else:
                            pe.run(f)

            def B(u):
                w = unit(u)
                for h, hd in enumerate(w["heads"]):
                    b = sbank(u, h)
                    p = Pb(u, h)
                    nb = ST[:, u % 4, 2 * h:2 * h + 2]
                    for q, (x, nn) in enumerate(((0, n0), (n0, n1))):
                        mask = cst("mask", nn, 384 - nn) if causal else cst("mask", nn)
                        sc = hd["scale"][q] if hd["scale"] is not None else -1.0
                        t = dve.do(call(dve.e.tensor_tensor_reduce, 
                            out=p[:, x:x + nn], in0=PS[:, b, x:x + nn], in1=mask, scale=sc, scalar=3e38,
                            op0=ALU.add, op1=ALU.min, accum_out=nb[:, q:q + 1]),
                            tok["A", u, h], *p_free[u % NP])
                    tok["B", u, h] = t
                    bank_free[b] = [t]

            def C(u):
                w = unit(u)
                for h, hd in enumerate(w["heads"]):
                    p = Pb(u, h)
                    for q, (x, nn) in enumerate(((0, n0), (n0, n1))):
                        t = act.do(call(act.e.activation, 
                            p[:, x:x + nn], p[:, x:x + nn], ACT.Exp, scale=-1.0,
                            bias=ST[:, u % 4, 2 * h + q:2 * h + q + 1],
                            accum_out=ST[:, u % 4, 8 + 2 * h + q:9 + 2 * h + q]), tok["B", u, h])
                    tok["C", u, h] = t

            def D(u):
                w = unit(u)
                k = 2 * heads
                r, s = ST[:, u % 4, 16:16 + k], ST[:, u % 4, 8:8 + k]
                t = dve.do(call(dve.e.reciprocal, r, s), *[tok["C", u, h] for h in range(heads)])
                for h, hd in enumerate(w["heads"]):
                    if hd["gate"] is not None:
                        r2 = ST[:, u % 4, 16 + 2 * h:18 + 2 * h]
                        g = hd["gate"]
                        tg = dve.do(call(dve.e.tensor_tensor, r2, r2, g, ALU.mult), t)
                    else:
                        tg = t
                    p = Pb(u, h)
                    for q, (x, nn) in enumerate(((0, n0), (n0, n1))):
                        t2 = dve.do(call(dve.e.tensor_scalar, 
                            p[:, x:x + nn], p[:, x:x + nn], ST[:, u % 4, 16 + 2 * h + q:17 + 2 * h + q], None,
                            op0=ALU.mult), tg)
                    tok["D", u, h] = t2

            def E(u):
                order = (0, 1, 2) if causal else (0, 2, 1, 3)
                for h in range(heads):
                    b = tbank(u, h)
                    pe.wait(*bank_free[b])
                    p = Pb(u, h)
                    for i, x in enumerate(order):
                        f = call(pe.e.transpose, PS[:, b, 128 * x:128 * x + 128],
                                                                      p[:, 128 * i:128 * i + 128], ident)
                        if i == len(order) - 1:
                            t = pe.do(f, tok["D", u, h])
                        else:
                            pe.run(f, tok["D", u, h])
                    tok["E", u, h] = t
                p_free[u % NP] = [t]

            def F(u):
                for h in range(heads):
                    b = tbank(u, h)
                    d = Tb(u, h)
                    q = act if h else dve
                    if heads == 1:
                        q = dve if u % 2 else act
                    w = width
                    if q is act:
                        t = act.do(call(act.e.activation, d, PS[:, b, 0:w], ACT.Copy), tok["E", u, h],
                                   *t_free[u % 2])
                    else:
                        t = dve.do(call(dve.e.tensor_copy, d, PS[:, b, 0:w]), tok["E", u, h], *t_free[u % 2])
                    bank_free[b] = [t]
                    tok["F", u, h] = t

            def G(u):
                w = unit(u)
                b = obank(w["o"])
                if w["first"]:
                    pe.wait(*bank_free[b])
                    if w["extra"]:
                        w["extra"](b)
                for h in range(heads):
                    pe.wait(tok["F", u, h])
                for kb in range(2):
                    for h, hd in enumerate(w["heads"]):
                        rows = slice(0, 128) if heads == 1 else slice(64 * h, 64 * h + 64)
                        q0 = 128 if (causal and kb) else 0
                        x = 256 * kb
                        v = hd["v"][kb]
                        start = w["first"] and kb == 0 and not w["extra"]
                        f = call(pe.e.matmul, 
                            PS[rows, b, q0:256], v, Tb(u, h)[:, x:x + 256 - q0], start=start,
                            stop=w["last"] and kb == 1, skip_group_check=True)
                        t = pe.do(f)
                t_free[u % 2] = [t]
                if w["last"]:
                    finish(w["o"], b, t)

            for s in range(n + 3):
                if s < n:
                    A(s)
                if 0 <= s - 2 < n:
                    D(s - 2)
                    E(s - 2)
                if s < n:
                    B(s)
                if 0 <= s - 1 < n:
                    C(s - 1)
                if 0 <= s - 2 < n:
                    F(s - 2)
                if 0 <= s - 3 < n:
                    G(s - 3)

        def o_split(base=0):
            def finish(j, b, t):
                o = PS[:, b, 0:256]
                bank_free[b] = [split_into(1, base + j, o, [t])]
            return finish

        def nsa(j):
            ctr = [0]

            def alloc(n):
                ctr[0] += n
                return ctr[0] - n
            q_at, ks_at, kw_at = alloc(2048), alloc(1024), alloc(1024)
            kc_at, v_at, gate_at = alloc(64), alloc(1024), alloc(192)
            hid_at, hk_at, hv_at, vc_at = alloc(256), alloc(128), alloc(256), alloc(512)
            pc_at, pp_at, pct_at = alloc(512), alloc(1024), alloc(1024)
            tmp_at = alloc(128)
            un_at = alloc(3072)
            c_at, blk_at = un_at, un_at + 1024
            P_at, PT_at = un_at, un_at + 1536
            assert ctr[0] <= NSCR, ctr
            Q = SCR[:, q_at:q_at + 2048].rearrange("p (j t) -> p j t", j=8)
            KZ = [SCR[:, x:x + 1024].rearrange("p (g t) -> p g t", g=4) for x in (ks_at, kw_at)]
            KC = SCR[:, kc_at:kc_at + 64].rearrange("p (g c) -> p g c", g=4)
            V = SCR[:, v_at:v_at + 1024].rearrange("p (b t d) -> p b t d", b=2, t=2)
            GA = SCR[:, gate_at:gate_at + 96].rearrange("p (t c) -> p t c", t=2)
            GB = SCR[:, gate_at + 96:gate_at + 192].rearrange("p (t c) -> p t c", t=2)
            C = SCR[:, c_at:c_at + 1024].rearrange("p (i t) -> p i t", i=4)
            BLK = SCR[:, blk_at:blk_at + 1920].rearrange("p (v i g c) -> p v i g c", v=2, i=16, g=4)
            HID = SCR[:, hid_at:hid_at + 256]
            HK = SCR[:, hk_at:hk_at + 128].rearrange("p (k g c) -> p k g c", k=2, g=4)
            HV = SCR[:, hv_at:hv_at + 256].rearrange("p (k g c) -> p k g c", k=2, g=4)
            VC = SCR[:, vc_at:vc_at + 512].rearrange("p (n c) -> p n c", n=4)
            PC = SCR[:, pc_at:pc_at + 512].rearrange("p (n c) -> p n c", n=32)
            PP = SCR[:, pp_at:pp_at + 1024].rearrange("p (n c) -> p n c", n=32)
            PCT = SCR[:, pct_at:pct_at + 1024].rearrange("p (n t) -> p n t", n=4)
            TMP = SCR[:, tmp_at:tmp_at + 128]

            prior = lasts()
            tz = None
            for ap in (SCR[64:128, ks_at:ks_at + 2048].rearrange("p (g t) -> p g t", g=8)[:, 0::2, :],
                       SCR[0:64, ks_at:ks_at + 2048].rearrange("p (g t) -> p g t", g=8)[:, 1::2, :],
                       SCR[:, kc_at:kc_at + 64], SCR[:, hid_at:hid_at + 256 + 128 + 256 + 512],
                       SCR[:, pp_at:pp_at + 1024]):
                tz = pool.do(call(pool.e.memset, ap, 0.0), pool.last, *prior)

            banks = (0, 1, 2, 3)
            rb = t_rb = None
            c_tok = [None] * 4
            for i in range(4):
                b = next_bank(banks)
                pe.wait(*bank_free[b])
                o = PS[:, b, 0:256]
                t = mtile(0, range(8), o, x_tok[0])
                if i == 0:
                    rb, t_rb = rstd_bcast(7)
                c_tok[i] = dve.do(call(dve.e.tensor_tensor, C[:, i, :], o, rb, ALU.mult), t, t_rb, *prior)
                bank_free[b] = [c_tok[i]]
                refill()
            t_rc = cols_of_rb(7, rb, t_rb)
            blk_tok = {}
            for v in range(2):
                eng = pool if v else dve
                for g in range(4):
                    rows = slice(64 * (g % 2), 64 * (g % 2) + 64)
                    for jj in range(2):
                        full = C[rows, 2 * v + g // 2, 0:256].rearrange("p (c i) -> p i c", i=16)
                        for half in range(2):
                            s2 = full[:, jj::2, half:half + 15]
                            pos = PRM[rows, PAT["cmp_pos"] + 64 * j + 32 * v + 16 * jj + 8 * half:
                                      PAT["cmp_pos"] + 64 * j + 32 * v + 16 * jj + 8 * half + 8]
                            pos = pos.unsqueeze(2).broadcast_to([64, 8, 15])
                            dst = BLK[64 * jj:64 * jj + 64, v, 8 * half:8 * half + 8, g, :]
                            blk_tok[v] = eng.do(call(eng.e.tensor_tensor, dst, s2, pos, ALU.add),
                                                c_tok[2 * v + g // 2], *([pool.last] if v else []), *prior)
            q_tok = [None] * 8
            for i in range(8):
                b = next_bank(banks)
                pe.wait(*bank_free[b])
                o = PS[:, b, 0:256]
                t = mtile(0, range(8), o, x_tok[0])
                q_tok[i] = dve.do(call(dve.e.scalar_tensor_tensor, Q[:, i, :], o, 0.125, rb, ALU.mult, ALU.mult), t)
                bank_free[b] = [q_tok[i]]
                refill()
            pe.wait(blk_tok[0], blk_tok[1], *bank_free[6])
            for n in range(8):
                u, w, loaded = next_raw()
                w = w.rearrange("p (i v c) -> p i v c", i=2, v=2)
                pe.wait(loaded)
                for ii in range(2):
                    for v in range(2):
                        i = 2 * n + ii
                        l = BLK[:, v, i, :, :].rearrange("p g c -> p (g c)")
                        f = call(pe.e.matmul, 
                            PS[64 * v:64 * v + 60, 6, 0:256], l, w[:, ii, v, :], start=i == 0, stop=i == 15,
                            skip_group_check=True)
                        t = pe.do(f)
                give_back(u, [t])
            ht = None
            for v in range(2):
                ht = act.do(call(act.e.activation, HID[64 * v:64 * v + 60, :], PS[64 * v:64 * v + 60, 6, 0:256],
                                                        ACT.Gelu_apprx_tanh), t, tz)
            bank_free[6] = [ht]
            k_tok = {}
            for i in range(4):
                b = next_bank(banks)
                pe.wait(*bank_free[b])
                t = mtile(0, range(8), PS[:, b, 0:256], x_tok[0])
                br, gg = i // 2, 2 * (i % 2)
                for hh in range(2):
                    rows = slice(64 * hh, 64 * hh + 64)
                    k_tok[br, gg + hh] = dve.do(call(dve.e.tensor_tensor, 
                        KZ[br][rows, gg + hh, :], PS[rows, b, 0:256], rb[rows, :], ALU.mult), t, tz)
                bank_free[b] = [k_tok[br, gg + 1]]
                refill()
                if i == 0:
                    for x in range(2):
                        t2 = pe.do(call(pe.e.transpose, PS[:, 6, 128 * x:128 * x + 128],
                                                              HID[:, 128 * x:128 * x + 128], ident), ht, *bank_free[6])
                    src = PS[:, 6, 0:256].rearrange("p (k n) -> p k n", k=2)
                    t3 = dve.do(call(dve.e.tensor_copy, HK[:, :, :, 0:15], src[:, :, 0:60].rearrange(
                        "p k (g c) -> p k g c", g=4)), t2, tz)
                    t4 = dve.do(call(dve.e.tensor_copy, HV[:, :, :, 0:15], src[:, :, 64:124].rearrange(
                        "p k (g c) -> p k g c", g=4)), t2)
                    bank_free[6] = [t4]
                if i == 1:
                    w2 = lambda v, k: PRM[:, PAT["cmp_w2"] + 256 * j + 128 * v + 64 * k:
                                          PAT["cmp_w2"] + 256 * j + 128 * v + 64 * k + 64]
                    pe.wait(t4, *bank_free[6], *bank_free[7])
                    for hh in range(2):
                        for k in range(2):
                            t5 = pe.do(call(pe.e.matmul, 
                                PS[64 * hh:64 * hh + 64, 6, 0:64], w2(0, k),
                                HK[:, k, :, :].rearrange("p g c -> p (g c)"), start=k == 0, stop=k == 1,
                                skip_group_check=True))
                    for k in range(2):
                        t6 = pe.do(call(pe.e.matmul, PS[:, 7, 0:64], HV[:, k, :, :].rearrange("p g c -> p (g c)"),
                                                           w2(1, k), start=k == 0, stop=k == 1))
                    kc = PS[:, 6, 0:64].rearrange("p (g c) -> p g c", g=4)
                    for hh in range(2):
                        rows = slice(64 * hh, 64 * hh + 64)
                        t_kc = dve.do(call(dve.e.tensor_copy, KC[rows, hh::2, 0:15],
                                                                                kc[rows, hh::2, 0:15]), t5, tz)
                    bank_free[6] = [t_kc]
                    for pg in range(2):
                        for aa in range(2):
                            for hh in range(2):
                                g = 2 * pg + hh
                                d0 = 64 * aa + 32 * hh
                                t_vc = dve.do(call(dve.e.tensor_copy, 
                                    VC[d0:d0 + 32, 2 * pg + aa, 64 * hh:64 * hh + 64],
                                    PS[32 * g:32 * g + 32, 7, 0:64]), t6, tz)
                    bank_free[7] = [t_vc]
                if i == 2:
                    pe.wait(*bank_free[6], t_kc)
                    for tt in range(2):
                        for pr in range(8):
                            pg = pr // 4
                            l = Q[:, pr, 128 * tt:128 * tt + 128]
                            r = KC[:, 2 * pg:2 * pg + 2, :].rearrange("p g c -> p (g c)")
                            x = 256 * tt + 32 * pr
                            t_sc = pe.do(call(pe.e.matmul, PS[:, 6, x:x + 32], l, r, start=True, stop=True,
                                                                           skip_group_check=True), q_tok[pr])
            v_tok = None
            for br, (cols, per) in enumerate(((304, 3), (256, 4))):
                bb = (0, 1) if br == 0 else (2, 3)
                pe.wait(*bank_free[bb[0]], *bank_free[bb[1]])
                t = vtile(0, range(8), cols, per, bb, x_tok[0])
                for tt in range(2):
                    v_tok = act.do(call(act.e.activation, 
                        V[:, br, tt, :], PS[:, bb[tt], 0:256], ACT.Copy, scale=RC[:, 0, tt:tt + 1]), t, t_rc, *prior)
                    if br == 0:
                        tg = dve.do(call(dve.e.tensor_scalar, 
                            GA[:, tt, :], PS[:, bb[tt], 256:304], RC[:, 0, tt:tt + 1], None, op0=ALU.mult), t, t_rc, v_tok)
                        bank_free[bb[tt]] = [tg]
                    else:
                        bank_free[bb[tt]] = [v_tok]
                if br == 0:
                    t1 = act.do(call(act.e.activation, GB[:, :, :], GA[:, :, :], ACT.Exp, scale=-1.0), tg)
                    t1 = dve.do(call(dve.e.tensor_scalar, GB[:, :, :], GB[:, :, :], 1.0, None, op0=ALU.add), t1)
                    t_g = dve.do(call(dve.e.reciprocal, GA[:, :, :], GB[:, :, :]), t1)
                    sc = PS[:, 6, :].rearrange("p (t n c) -> p t n c", t=2, n=16)
                    p4 = SCR[:, pc_at:pc_at + 512].rearrange("p (t n c) -> p t n c", t=2, n=16)
                    cm = cst("cmask", 32).rearrange("p (t c) -> p t c", t=2).unsqueeze(2).broadcast_to([128, 2, 16, 16])
                    mx, sm = TMP[:, 0:32], TMP[:, 32:64]
                    bc = lambda ap: ap.unsqueeze(2).broadcast_to([128, 32, 16])
                    t2 = dve.do(call(dve.e.tensor_tensor, p4, sc, cm, ALU.add), t_sc, *prior)
                    bank_free[6] = [t2]
                    t2 = dve.do(call(dve.e.tensor_reduce, mx, PC[:, :, :], AX.X, ALU.max), t2)
                    t2 = dve.do(call(dve.e.tensor_scalar, mx, mx, -1e29, None, op0=ALU.max), t2)
                    t2 = dve.do(call(dve.e.tensor_tensor, PC[:, :, :], PC[:, :, :], bc(mx), ALU.subtract), t2)
                    t3 = act.do(call(act.e.activation, PC[:, :, :], PC[:, :, :], ACT.Exp), t2)
                    t3 = dve.do(call(dve.e.tensor_reduce, sm, PC[:, :, :], AX.X, ALU.add), t3)
                    t3 = dve.do(call(dve.e.tensor_scalar, sm, sm, 1e-30, None, op0=ALU.max), t3)
                    t3 = dve.do(call(dve.e.reciprocal, mx, sm), t3)
                    for tt in range(2):
                        m4 = TMP[:, 16 * tt:16 * tt + 16].rearrange("p (g r h) -> p g r h", g=2, r=4)
                        g4 = GA[:, tt, 0:16].rearrange("p (g h r) -> p g r h", g=2, h=2)
                        t4 = dve.do(call(dve.e.tensor_tensor, m4, m4, g4, ALU.mult), t3, t_g)
                    t_pp = dve.do(call(dve.e.tensor_tensor, PP[:, :, 0:16], PC[:, :, :], bc(mx), ALU.mult), t4, tz)
                refill()
            x_free[0] = [t]
            for half in range(2):
                pe.wait(*bank_free[4 + half])
                for cc in range(2):
                    ch = 2 * half + cc
                    for tt in range(2):
                        src = PP[:, 16 * tt + 4 * ch:16 * tt + 4 * ch + 4, :].rearrange("p n c -> p (n c)")
                        t = pe.do(call(pe.e.transpose, 
                            PS[:, 4 + half, 256 * cc + 128 * tt:256 * cc + 128 * tt + 128], src, ident), t_pp)
                dst = PCT[:, 2 * half:2 * half + 2, :].rearrange("p n t -> p (n t)")
                t_pct = act.do(call(act.e.activation, dst, PS[:, 4 + half, :], ACT.Copy), t, *prior)
                bank_free[4 + half] = [t_pct]

            def unit(u):
                pr, br = u // 2, u % 2
                pg, r = pr // 4, pr % 4

                def extra(b):
                    l, rr = VC[:, 2 * pg + pr % 2, :], PCT[:, pr // 2, :]
                    pe.run(call(pe.e.matmul, PS[:, b, 0:256], l, rr, start=True, stop=False, skip_group_check=True),
                           t_pct, t_vc)
                heads = []
                for h in range(2):
                    g = 2 * pg + h
                    col = 16 * (1 + br) + 4 * g + r
                    heads.append(dict(
                        score=[(0, 128, Q[:, pr, 0:128], KZ[br][:, g, 0:128], True, True),
                               (128, 256, Q[:, pr, 128:256], KZ[br][:, g, :], True, True)],
                        wait=(q_tok[pr], k_tok[br, g]), scale=None, gate=GA[:, :, col],
                        v=[V[:, br, kb, 64 * g:64 * g + 64] for kb in range(2)]))
                return dict(heads=heads, o=pr, first=br == 0, last=br == 1, extra=extra if br == 0 else None)
            pe.wait(v_tok)
            dve.wait(t_g)
            attention(16, unit, P_at, PT_at, 384, 1, o_split())

        def moba():
            Q = SCR[:, 0:2048].rearrange("p (j t) -> p j t", j=8)
            KZ = SCR[:, 2048:6144].rearrange("p (h t) -> p h t", h=16)
            V = SCR[:, 6144:8192].rearrange("p (t c) -> p t c", t=2)
            prior = lasts()
            for ap in (KZ[64:128, 0::2, :], KZ[0:64, 1::2, :]):
                tz = pool.do(call(pool.e.memset, ap, 0.0), pool.last, *prior)
            q_tok, k_tok = [None] * 8, [None] * 16
            for i in range(16):
                b = next_bank((0, 1, 2, 3))
                pe.wait(*bank_free[b])
                o = PS[:, b, 0:256]
                t = mtile(0, range(8), o, x_tok[0])
                if i == 0:
                    rb, t_rb = rstd_bcast(7)
                if i < 8:
                    q_tok[i] = dve.do(call(dve.e.scalar_tensor_tensor, 
                        Q[:, i, :], o, 0.125, rb, ALU.mult, ALU.mult), t, t_rb, *prior)
                    bank_free[b] = [q_tok[i]]
                else:
                    for hh in range(2):
                        rows = slice(64 * hh, 64 * hh + 64)
                        h = 2 * (i - 8) + hh
                        k_tok[h] = dve.do(call(dve.e.tensor_tensor, 
                            KZ[rows, h, :], PS[rows, b, 0:256], rb[rows, :], ALU.mult), t, tz)
                    bank_free[b] = [k_tok[h]]
                if i == 2:
                    t_rc = cols_of_rb(7, rb, t_rb)
                refill()
            for n in range(2):
                bb = (0, 1) if n == 0 else (2, 3)
                pe.wait(*bank_free[bb[0]], *bank_free[bb[1]])
                t = vtile(0, range(8), 512, 2, bb, x_tok[0])
                for tt in range(2):
                    v_tok = act.do(call(act.e.activation, 
                        V[:, tt, 512 * n:512 * n + 512], PS[:, bb[tt], :], ACT.Copy, scale=RC[:, 0, tt:tt + 1]),
                        t, t_rc, *prior)
                    bank_free[bb[tt]] = [v_tok]
                refill()
            x_free[0] = [t]
            pe.wait(v_tok)

            def unit(u):
                heads = [dict(score=[(0, 128, Q[:, u, 0:128], KZ[:, 2 * u + h, 0:128], True, True),
                                     (128, 256, Q[:, u, 128:256], KZ[:, 2 * u + h, :], True, True)],
                              wait=(q_tok[u], k_tok[2 * u + h]), scale=None, gate=None,
                              v=[V[:, kb, 128 * u + 64 * h:128 * u + 64 * h + 64] for kb in range(2)]) for h in range(2)]
                return dict(heads=heads, o=u, first=True, last=True, extra=None)
            attention(8, unit, 8192, 8192 + 2304, 384, 1, o_split())

        def conv():
            prior = lasts()
            R2 = SCR[:, 0:256]
            Z = [SCR[:, 256 + 258 * i:256 + 258 * (i + 1)] for i in range(2)]
            Y = [SCR[:, 1024 + 256 * i:1280 + 256 * i] for i in range(2)]
            CC = [SCR[:, 1536 + 256 * i:1792 + 256 * i] for i in range(2)]
            for i in range(2):
                tz = pool.do(call(pool.e.memset, Z[i][:, 0:2], 0.0), pool.last, *prior)
            for d in range(8):
                s = d % 2
                bs = []
                ts = []
                for i in range(3):
                    b = 3 * (d % 2) + i
                    pe.wait(*bank_free[b])
                    ts.append(mtile(0, range(8), PS[:, b, 0:256], x_tok[0]))
                    bs.append(b)
                    if d == 0 and i == 0:
                        rb, t_rb = rstd_bcast(7)
                        t_r2 = dve.do(call(dve.e.tensor_tensor, R2, rb, rb, ALU.mult), t_rb, *prior)
                    if i < 2:
                        refill(1)
                c_, u_, b_ = (PS[:, x, 0:256] for x in bs)
                w = lambda i: prm("conv_w", 3 * d + i)
                z, y, cc = Z[s], Y[s], CC[s]
                t = dve.do(call(dve.e.tensor_tensor, cc, c_, R2, ALU.mult), ts[0], t_r2, dve.last)
                bank_free[bs[0]] = [t]
                t = dve.do(call(dve.e.tensor_tensor, z[:, 2:258], u_, cc, ALU.mult), ts[1], t, tz)
                bank_free[bs[1]] = [t]
                t = dve.do(call(dve.e.tensor_scalar, y, z[:, 0:256], w(0), None, op0=ALU.mult), t)
                t = dve.do(call(dve.e.scalar_tensor_tensor, y, z[:, 1:257], w(1), y, ALU.mult, ALU.add), t)
                t = dve.do(call(dve.e.scalar_tensor_tensor, y, z[:, 2:258], w(2), y, ALU.mult, ALU.add), t)
                t = dve.do(call(dve.e.tensor_tensor, y, y, rb, ALU.mult), t)
                t = dve.do(call(dve.e.tensor_tensor, y, b_, y, ALU.mult), t, ts[2])
                bank_free[bs[2]] = [t]
                split_into(1, d, y, [t])
                refill()
            x_free[0] = [ts[2]]

        MEMK = SCR[:, 11776:12800].rearrange("p (h t) -> p h t", h=4)
        MEMV = SCR[:, 12800:13824].rearrange("p (t c) -> p t c", t=2)

        def chain(q, t, *ops):
            for op in ops:
                t = q.do(op, t)
            return t

        def inv_sqrt(y, x, t, tmp):
            y0 = tmp[0]
            t = act.do(call(act.e.activation, y0, x, ACT.Abs_reciprocal_sqrt), t)
            return newton(y, y0, x, t, tmp[1])

        def small(at, *shape):
            n = int(np.prod(shape))
            ap = SM[:, at:at + n]
            if len(shape) == 2:
                ap = ap.rearrange("p (a b) -> p a b", a=shape[0])
            return ap

        def squares(dst, src, junk, *tokens):
            return act.do(call(act.e.activation, junk, src, ACT.Square, accum_out=dst), *tokens)

        MT = SCR[:, 8192:10240].rearrange("p (k t) -> p k t", k=8)
        ld = {n: [sem(f"s_{n}"), 0] for n in ("memT", "a_ln", "a_ws", "a_bs")}
        mem = {}

        def load_mem():
            prior = lasts()
            mem["x"] = sp.dma(SCR[:, 8192:10240], a["memT"], ld["memT"], *prior)
            mem["ln"] = sp.dma(SCR[:, 4096:6144], a["a_ln"], ld["a_ln"])
            mem["ws"] = sp.dma(SCR[:, 6144:7168], a["a_ws"], ld["a_ws"])
            mem["bs"] = sp.dma(SCR[:, 7168:8192], a["a_bs"], ld["a_bs"])

        def mem_hook(f):
            k = f - 3
            if 0 <= k < 8:
                split_into(1, k, MT[:, k, :], [mem["x"]], prm("mem_norm", k))
                square_into(k, MT[:, k, :], [mem["x"]])
            if k == 8:
                b = next_bank((0, 1, 2, 3))
                mem["rc"] = rstd_cols(b, RC[:, 1, :])
            if f == 14:
                ws = SCR[:, 6144:7168].rearrange("p (g t) -> p g t", g=8)
                mem["ws"] = pool.do(call(pool.e.affine_select, ws, ws, [[0, 8], [1, 128]], ALU.is_ge, 0.0, base=0,
                                         channel_multiplier=-1), mem["ws"], pool.last)

        def mem_kv_keys():
            vt = vtile(1, range(8), 512, 2, (0, 1), x_tok[1])
            KM = SCR[:, 0:1024].rearrange("p (t c) -> p t c", t=2)
            JK = SCR[:, 1024:1152]
            ss, m2, y, t0, t1 = small(0, 2, 4), small(8, 2), small(10, 2, 4), small(18, 8), small(26, 8)
            prior = lasts()
            for tt in range(2):
                for h in range(4):
                    t = squares(ss[:, tt, h:h + 1], PS[:, tt, 128 * h:128 * h + 128], JK, vt, act.last, *prior)
            m2b = m2.unsqueeze(2).broadcast_to([128, 2, 4])
            x = small(34, 2, 4)
            t = chain(dve, t, call(dve.e.tensor_tensor, m2, RC[:, 1, :], RC[:, 1, :], ALU.mult),
                      call(dve.e.tensor_tensor, x, ss, m2b, ALU.mult),
                      call(dve.e.tensor_scalar, x, x, 1.0 / 128, 1e-6, op0=ALU.mult, op1=ALU.add))
            t = inv_sqrt(small(10, 8), small(34, 8), t, (t0, t1))
            rb_ = RC[:, 1, :].unsqueeze(2).broadcast_to([128, 2, 4])
            t = dve.do(call(dve.e.tensor_tensor, y, y, rb_, ALU.mult), t)
            for tt in range(2):
                for h in range(4):
                    tk = dve.do(call(dve.e.tensor_scalar, KM[:, tt, 128 * h:128 * h + 128],
                                     PS[:, tt, 128 * h:128 * h + 128], y[:, tt, h:h + 1], None, op0=ALU.mult), t)
            bank_free[0] = bank_free[1] = [tk]
            mem["km"], mem["KM"] = tk, KM

        def mem_kv_values():
            vt = vtile(1, range(8), 512, 2, (2, 3), x_tok[1])
            x_free[1] = [vt]
            for tt in range(2):
                t = act.do(call(act.e.activation, MEMV[:, tt, :], PS[:, 2 + tt, :], ACT.Copy, scale=RC[:, 1, tt:tt + 1]),
                           vt, mem["rc"])
                bank_free[2 + tt] = [t]
            mem["v"] = t
            mem["k"] = to_features(mem["KM"], 4, MEMK, (6, 7), [mem["km"]])

        def to_features(src, heads, dst, banks, tokens, gain=None):
            for h in range(heads):
                b = banks[(h // 2) % len(banks)]
                if h % 2 == 0:
                    pe.wait(*bank_free[b])
                for tt in range(2):
                    t = pe.do(call(pe.e.transpose, PS[:, b, 256 * (h % 2) + 128 * tt:256 * (h % 2) + 128 * tt + 128],
                                   src[:, tt, 128 * h:128 * h + 128], ident), *tokens)
                if h % 2:
                    d = dst[:, h - 1:h + 1, :].rearrange("p h t -> p (h t)")
                    if (h // 2) % 2:
                        t = act.do(call(act.e.activation, d, PS[:, b, :], ACT.Copy, scale=1.0 if gain is None else gain),
                                   t, *lasts_dp())
                    else:
                        t = dve.do(call(dve.e.tensor_scalar, d, PS[:, b, :], 1.0 if gain is None else gain, None,
                                        op0=ALU.mult), t, *lasts_ap())
                    bank_free[b] = [t]
                    out_t = (out_t if h > 1 else []) + [t]
            return out_t

        def lasts_dp():
            return [dve.last, pool.last]

        def lasts_ap():
            return [act.last, pool.last]

        def final_norm(bank):
            rb, t_rb = rstd_bcast(bank)
            for k in range(8):
                h_tok[k] = dve.do(call(dve.e.scalar_tensor_tensor, H[:, k, :], H[:, k, :], prm("norm_final", k), rb,
                                       ALU.mult, ALU.mult), t_rb, h_tok[k])
                new_h(k, prm("norm1", k))

        def query_scales(ss, dst, n, c, mean, tokens, at):
            c2 = small(at, 2)
            x = small(at + 2, 2, n)
            xf, y0, tmp = small(at + 2, 2 * n), small(at + 2 + 2 * n, 2 * n), small(at + 2 + 4 * n, 2 * n)
            wide = lambda ap: ap.unsqueeze(2).broadcast_to([128, 2, n])
            t = dve.do(call(dve.e.tensor_tensor, c2, c, c, ALU.mult), *tokens)
            t = chain(dve, t, call(dve.e.tensor_tensor, x, ss, wide(c2), ALU.mult),
                      call(dve.e.tensor_scalar, xf, xf, 1.0 / mean, 1e-6, op0=ALU.mult, op1=ALU.add))
            t = inv_sqrt(xf, xf, t, (y0, tmp))
            t = dve.do(call(dve.e.tensor_scalar, xf, xf, -float(mean) ** -0.5, None, op0=ALU.mult), t)
            return dve.do(call(dve.e.tensor_tensor, dst, x, wide(c), ALU.mult), t)

        def mem_queries(i, banks, vt, QM, JK, r, t_r, at):
            ss, ns = small(at, 2, 4), small(at + 8, 2, 4)
            for tt in range(2):
                for h in range(4):
                    ts = squares(ss[:, tt, h:h + 1], PS[:, banks[tt], 128 * h:128 * h + 128], JK[:, 0:128], vt, act.last,
                                 dve.last, pool.last)
                tc = act.do(call(act.e.activation, QM[:, tt, :], PS[:, banks[tt], :], ACT.Copy), vt)
                bank_free[banks[tt]] = [tc]
            g = small(at + 16, 1)
            tg = dve.do(call(dve.e.tensor_tensor, g, prm("mem_qn", i), prm("mem_kn", i), ALU.mult), dve.last)
            tn = query_scales(ss, ns, 4, r, 128, [ts, t_r], at + 18)
            return ns, tn, g, tg, tc

        def mem_attention(i, QM, QT, ns, tn, g, tg, tc, P_at, PT_at):
            tq = to_features(QM, 4, QT, (6, 7), [tc, tg], gain=g)

            def unit(u):
                return dict(heads=[dict(
                    score=[(0, 256, QT[:, u, 0:128], MEMK[:, u, :], True, True),
                           (256, 256, QT[:, u, 128:256], MEMK[:, u, :], True, True)],
                    wait=(*tq, *mem["k"]), scale=(ns[:, 0, u:u + 1], ns[:, 1, u:u + 1]), gate=None,
                    v=[MEMV[:, kb, 128 * u:128 * u + 128] for kb in range(2)])], o=u, first=True, last=True, extra=None)
            pe.wait(mem["v"])
            dve.wait(tn)
            attention(4, unit, P_at, PT_at, 512, 1, o_split(8), causal=False)

        def gmlp():
            VV = SCR[:, 0:2048].rearrange("p (t c) -> p t c", t=2)
            U = SCR[:, 2048:4096].rearrange("p (k t) -> p k t", k=8)
            LNG, LNB = SCR[:, 4096:5120], SCR[:, 5120:6144]
            WS = SCR[:, 6144:7168].rearrange("p (g t) -> p g t", g=8)
            BS = SCR[:, 7168:8192].rearrange("p (g t) -> p g t", g=8)
            QM = SCR[:, 8192:9216].rearrange("p (t c) -> p t c", t=2)
            QT = SCR[:, 9216:10240].rearrange("p (h t) -> p h t", h=4)
            JK = SCR[:, 10240:10752]
            prior = lasts()
            for n in range(2):
                bb = (0, 1) if n == 0 else (2, 3)
                pe.wait(*bank_free[bb[0]], *bank_free[bb[1]])
                vt = vtile(0, range(8), 512, 2, bb, x_tok[0])
                if n == 0:
                    rb, t_rb = rstd_bcast(4)
                    t_rc = cols_of_rb(4, rb, t_rb)
                for tt in range(2):
                    tv = act.do(call(act.e.activation, VV[:, tt, 512 * n:512 * n + 512], PS[:, bb[tt], :], ACT.Gelu,
                                     scale=RC[:, 0, tt:tt + 1]), vt, t_rc, *prior)
                    bank_free[bb[tt]] = [tv]
                refill()
            pe.wait(*bank_free[0], *bank_free[1])
            vt = vtile(0, range(8), 512, 2, (0, 1), x_tok[0])
            ns, tn, g, tg, tc = mem_queries(0, (0, 1), vt, QM, JK, RC[:, 0, :], t_rc, 0)
            refill()
            t_vn = []
            for tt in range(2):
                s6, mv = small(64 + 16 * tt, 12), small(76 + 16 * tt, 2)
                for n in range(2):
                    t = dve.do(call(dve.e.bn_stats, s6[:, 6 * n:6 * n + 6], VV[:, tt, 512 * n:512 * n + 512]), tv)
                t = dve.do(call(dve.e.bn_aggr, mv, s6), t)
                x, y0, tmp = small(96 + 4 * tt, 1), small(97 + 4 * tt, 1), small(98 + 4 * tt, 1)
                t = dve.do(call(dve.e.tensor_scalar, x, mv[:, 1:2], 1e-6, None, op0=ALU.add), t)
                t = inv_sqrt(x, x, t, (y0, tmp))
                v = VV[:, tt, :]
                t_vn.append(chain(dve, t,
                                  call(dve.e.tensor_scalar, v, v, mv[:, 0:1], x, op0=ALU.subtract, op1=ALU.mult),
                                  call(dve.e.tensor_tensor, v, v, LNG, ALU.mult),
                                  call(dve.e.tensor_tensor, v, v, LNB, ALU.add)))
                dve.wait(mem["ln"])
            tu = [None] * 8
            for m in range(8):
                b = next_bank((2, 3))
                pe.wait(*bank_free[b])
                t = mtile(0, range(8), PS[:, b, 0:256], x_tok[0])
                t = dve.do(call(dve.e.tensor_tensor, U[:, m, :], PS[:, b, 0:256], rb, ALU.mult), t, t_rb)
                bank_free[b] = [t]
                tu[m] = act.do(call(act.e.activation, U[:, m, :], U[:, m, :], ACT.Gelu), t)
                refill()
            x_free[0] = [pe.last]
            mem_attention(0, QM, QT, ns, tn, g, tg, tc, 4096, 5120)
            pe.wait(mem["ws"])
            dve.wait(mem["bs"])
            for gi in range(8):
                b = gi % 4
                pe.wait(*bank_free[b])
                for n in range(2):
                    t = pe.do(call(pe.e.matmul, PS[:, b, 128 * n:128 * n + 128], VV[:, n, 128 * gi:128 * gi + 128],
                                   WS[:, gi, :], start=True, stop=True, skip_group_check=True), t_vn[n])
                tmp = SCR[:, 8192 + 256 * (gi % 4):8448 + 256 * (gi % 4)]
                tmp3 = tmp.rearrange("p (n t) -> p n t", n=2)
                bs = BS[:, gi, :].unsqueeze(1).broadcast_to([128, 2, 128])
                t = dve.do(call(dve.e.tensor_tensor, tmp3, PS[:, b, 0:256].rearrange("p (n t) -> p n t", n=2), bs,
                                ALU.add), t, dve.last, act.last)
                bank_free[b] = [t]
                t = dve.do(call(dve.e.tensor_tensor, tmp, tmp, U[:, gi, :], ALU.mult), t, tu[gi])
                split_into(1, gi, tmp, [t])

        def mla():
            QNT = SCR[:, 0:2048].rearrange("p (h t) -> p h t", h=8)
            QRT = SCR[:, 2048:3072].rearrange("p (h t) -> p h t", h=4)
            KNT = SCR[:, 3072:5120].rearrange("p (h t) -> p h t", h=8)
            KZR = SCR[:, 5120:7168].rearrange("p (h t) -> p h t", h=8)
            VT = SCR[:, 7168:9216].rearrange("p (t c) -> p t c", t=2)
            P_at, PT_at = 9216, 10368
            CQ = SCR[:, 3072:4096].rearrange("p (t c) -> p t c", t=2)
            CKV = SCR[:, 4096:4608].rearrange("p (t c) -> p t c", t=2)
            QM = SCR[:, 4608:5632].rearrange("p (t c) -> p t c", t=2)
            JK = SCR[:, 5632:6144]
            QT = SCR[:, 6144:7168].rearrange("p (h t) -> p h t", h=4)
            KR = SCR[:, 11648:11776].rearrange("p (t c) -> p t c", t=2)
            QK = SCR[:, 7168:10240].rearrange("p (t h c) -> p t h c", t=2, h=8)
            QKf = SCR[:, 7168:10240].rearrange("p (t c) -> p t c", t=2)
            QR = SCR[:, 10240:11264].rearrange("p (t h c) -> p t h c", t=2, h=8)
            KT = SCR[:, 7168:9216].rearrange("p (t c) -> p t c", t=2)
            prior = lasts()
            pf = small(0, 2)
            ang = ROT[:, 0:64].rearrange("p (t i) -> p t i", t=2)
            A, N, NH, TMP = (ROT[:, 64 * i:64 * i + 64] for i in range(4))
            SIN, COS = ROT[:, 256:320], ROT[:, 320:384]
            two_pi = 2 * np.pi
            C1 = 6.28125
            C2 = float(np.floor((two_pi - C1) * 2 ** 20) / 2 ** 20)
            C3 = float(two_pi - C1 - C2)
            M = 12582912.0
            t = dve.do(call(dve.e.tensor_copy, pf, POSI[:, :]), t_pos, *prior)
            for tt in range(2):
                t = dve.do(call(dve.e.tensor_scalar, ang[:, tt, :], cst("inv", 32), pf[:, tt:tt + 1], None,
                                op0=ALU.mult), t)
            stt = lambda o, x, s, y: call(dve.e.scalar_tensor_tensor, o, x, s, y, ALU.mult, ALU.add)
            ts = lambda o, x, s1, s2, o0, o1: call(dve.e.tensor_scalar, o, x, s1, s2, op0=o0, op1=o1)
            one = lambda o, x, s1, o0: call(dve.e.tensor_scalar, o, x, s1, None, op0=o0)
            t = chain(
                dve, t,
                ts(N, A, 1.0 / two_pi, M, ALU.mult, ALU.add), one(N, N, M, ALU.subtract),
                ts(NH, N, 1.0 / 4096, M, ALU.mult, ALU.add), ts(NH, NH, M, 4096.0, ALU.subtract, ALU.mult),
                call(dve.e.tensor_tensor, TMP, N, NH, ALU.subtract),
                stt(A, NH, -C1, A), stt(A, TMP, -C1, A), stt(A, NH, -C2, A), stt(A, TMP, -C2, A), stt(A, N, -C3, A),
                one(N, A, np.pi / 2, ALU.add), one(TMP, N, np.pi, ALU.is_gt), stt(N, TMP, -two_pi, N),
                ts(A, A, -3.1415925, 3.1415925, ALU.max, ALU.min), ts(N, N, -3.1415925, 3.1415925, ALU.max, ALU.min))
            t1 = act.do(call(act.e.activation, SIN, A, ACT.Sin), t)
            t_rot = act.do(call(act.e.activation, COS, N, ACT.Sin), t)
            cos3 = COS.rearrange("p (t i) -> p t i", t=2)
            sin3 = SIN.rearrange("p (t i) -> p t i", t=2)

            pe.wait(*bank_free[0], *bank_free[1])
            vt = vtile(0, range(8), 512, 2, (0, 1), x_tok[0])
            t_rc = rstd_cols(4, RC[:, 0, :])
            r = RC[:, 0, :]
            ss1 = small(16, 2, 3)
            for tt in range(2):
                t1 = squares(ss1[:, tt, 0:1], PS[:, tt, :], JK, vt, act.last, *prior)
                tq = dve.do(call(dve.e.tensor_copy, CQ[:, tt, :], PS[:, tt, :]), t1, *prior)
                bank_free[tt] = [tq]
            refill()
            pe.wait(*bank_free[2], *bank_free[3])
            vt = vtile(0, range(8), 320, 3, (2, 3), x_tok[0])
            for tt in range(2):
                t1 = squares(ss1[:, tt, 1:2], PS[:, 2 + tt, 0:256], JK[:, 0:256], vt, act.last)
                t1 = squares(ss1[:, tt, 2:3], PS[:, 2 + tt, 256:320], JK[:, 0:64], act.last)
                t2 = dve.do(call(dve.e.tensor_copy, CKV[:, tt, :], PS[:, 2 + tt, 0:256]), t1, *prior)
                t2 = dve.do(call(dve.e.tensor_copy, KR[:, tt, :], PS[:, 2 + tt, 256:320]))
                bank_free[2 + tt] = [t2]
            refill()
            pe.wait(*bank_free[0], *bank_free[1])
            vt = vtile(0, range(8), 512, 2, (0, 1), x_tok[0])
            x_free[0] = [vt]
            r2, x, y0, tmp, c = small(24, 2), small(26, 2, 2), small(30, 4), small(34, 4), small(38, 2, 2)
            xf = small(26, 4)
            wide = lambda ap, n: ap.unsqueeze(2).broadcast_to([128, 2, n])
            t = dve.do(call(dve.e.tensor_tensor, r2, r, r, ALU.mult), t_rc, t1)
            t = chain(dve, t, call(dve.e.tensor_tensor, x, ss1[:, :, 0:2], wide(r2, 2), ALU.mult),
                      one(x[:, :, 0:1], x[:, :, 0:1], 1.0 / 512, ALU.mult), one(x[:, :, 1:2], x[:, :, 1:2], 1.0 / 256, ALU.mult),
                      one(xf, xf, 1e-6, ALU.add))
            t = inv_sqrt(xf, xf, t, (y0, tmp))
            t_c = dve.do(call(dve.e.tensor_tensor, c, x, wide(r, 2), ALU.mult), t)
            cq, ckv = small(42, 2), small(44, 2)
            t_c = dve.do(call(dve.e.tensor_copy, cq.unsqueeze(2), c[:, :, 0:1]), t_c)
            t_c = dve.do(call(dve.e.tensor_copy, ckv.unsqueeze(2), c[:, :, 1:2]), t_c)
            for k in range(6):
                src, name, kk = (CQ, "q_norm", k) if k < 4 else (CKV, "kv_norm", k - 4)
                b = 5 + k % 2
                pe.wait(*bank_free[b])
                for tt in range(2):
                    t = pe.do(call(pe.e.transpose, PS[:, b, 128 * tt:128 * tt + 128],
                                   src[:, tt, 128 * kk:128 * kk + 128], ident), tq if k < 4 else t2)
                bank_free[b] = [split_into(1, k, PS[:, b, 0:256], [t], prm(name, kk))]
            ns, tn, g, tg, tc = mem_queries(1, (0, 1), vt, QM, JK, r, t_rc, 50)
            refill()
            mem_attention(1, QM, QT, ns, tn, g, tg, tc, 9216, 10240)
            for n in range(3):
                bb = (0, 1) if n % 2 == 0 else (2, 3)
                pe.wait(*bank_free[bb[0]], *bank_free[bb[1]])
                vt = vtile(1, range(4), 512, 2, bb, x_tok[1])
                for tt in range(2):
                    dst, src = QKf[:, tt, 512 * n:512 * n + 512], PS[:, bb[tt], :]
                    if tt:
                        tq = dve.do(call(dve.e.tensor_copy, dst, src), vt, *lasts())
                    else:
                        ta = act.do(call(act.e.activation, dst, src, ACT.Copy), vt, *lasts())
                    bank_free[bb[tt]] = [tq if tt else ta]
                refill()
            ssq = small(128, 2, 8)
            JQ = JK[:, 0:192]
            for tt in range(2):
                for h in range(8):
                    t_ss = squares(ssq[:, tt, h:h + 1], QK[:, tt, h, :], JQ, ta, tq, act.last)
            nsq = small(144, 2, 8)
            t_nsq = query_scales(ssq, nsq, 8, cq, 192, [t_ss, t_c], 160)
            gp = small(46, 1)
            t_gp = dve.do(call(dve.e.tensor_tensor, gp, prm("qn_nope"), prm("kn_nope"), ALU.mult), dve.last)
            RT = [SCR[:, 3072 + 256 * i:3328 + 256 * i].rearrange("p (h i) -> p h i", h=8) for i in range(4)]

            def rotate(dst, src, heads, tt, tok):
                co = cos3[:, tt, :].unsqueeze(1).broadcast_to([128, heads, 32])
                si = sin3[:, tt, :].unsqueeze(1).broadcast_to([128, heads, 32])
                p = [x[:, 0:heads, :] for x in RT]
                x1, x2 = src[:, :, 0:32], src[:, :, 32:64]
                t = dve.do(call(dve.e.tensor_tensor, p[0], x1, co, ALU.mult), tok, t_rot, dve.last)
                dve.do(call(dve.e.tensor_tensor, p[1], x2, si, ALU.mult))
                dve.do(call(dve.e.tensor_tensor, p[2], x1, si, ALU.mult))
                t = dve.do(call(dve.e.tensor_tensor, p[3], x2, co, ALU.mult))
                dve.do(call(dve.e.tensor_tensor, dst[:, :, 0:32], p[0], p[1], ALU.subtract), t)
                return dve.do(call(dve.e.tensor_tensor, dst[:, :, 32:64], p[2], p[3], ALU.add), t)

            for tt in range(2):
                gq = prm("qn_rope", 0, 64).unsqueeze(1).broadcast_to([128, 8, 64])
                src = QK[:, tt, :, 128:192]
                t = dve.do(call(dve.e.tensor_tensor, src, src, gq, ALU.mult), t_ss, dve.last)
                t_qr = rotate(QR[:, tt], src, 8, tt, t)
            kvt = []
            for n in range(2):
                bb = (0, 1) if n % 2 else (2, 3)
                pe.wait(*bank_free[bb[0]], *bank_free[bb[1]])
                kvt.append((bb, vtile(1, (4, 5), 512, 2, bb, x_tok[1])))
                refill()
            QN = SCR[:, 7168:10240].rearrange("p (t h c) -> p t h c", t=2, h=8)
            t_qn = []
            for h in range(8):
                b = 4 + (h // 2) % 2
                if h % 2 == 0:
                    pe.wait(*bank_free[b])
                for tt in range(2):
                    t = pe.do(call(pe.e.transpose, PS[:, b, 256 * (h % 2) + 128 * tt:256 * (h % 2) + 128 * tt + 128],
                                   QN[:, tt, h, 0:128], ident), ta, tq)
                if h % 2:
                    d = QNT[:, h - 1:h + 1, :].rearrange("p h t -> p (h t)")
                    if (h // 2) % 2:
                        t = act.do(call(act.e.activation, d, PS[:, b, :], ACT.Copy, scale=gp), t, t_gp)
                    else:
                        t = dve.do(call(dve.e.tensor_scalar, d, PS[:, b, :], gp, None, op0=ALU.mult), t, t_gp)
                    bank_free[b] = [t]
                    t_qn.append(t)
            QRf = SCR[:, 10240:11264].rearrange("p (t c) -> p t c", t=2)
            t_qrt = to_features(QRf, 4, QRT, (6, 7), [t_qr])
            ssk = small(208, 2, 8)
            for n, (bb, vt) in enumerate(kvt):
                for tt in range(2):
                    for h in range(4):
                        t1 = squares(ssk[:, tt, 4 * n + h:4 * n + h + 1], PS[:, bb[tt], 128 * h:128 * h + 128],
                                     JK[:, 0:128], vt, act.last)
                    t2 = dve.do(call(dve.e.tensor_copy, KT[:, tt, 512 * n:512 * n + 512], PS[:, bb[tt], :]), t1,
                                pe.last)
                    bank_free[bb[tt]] = [t2]
            c2, kx, ky = small(224, 2), small(226, 2, 8), small(242, 2)
            kxf, k0, k1 = small(226, 16), small(244, 16), small(260, 16)
            fk, fr = small(276, 2, 8), small(292, 2, 8)
            t = dve.do(call(dve.e.tensor_tensor, c2, ckv, ckv, ALU.mult), t_c, t1)
            t = chain(dve, t, call(dve.e.tensor_tensor, kx, ssk, wide(c2, 8), ALU.mult),
                      call(dve.e.tensor_tensor, ky.unsqueeze(2), ss1[:, :, 2:3], r2.unsqueeze(2), ALU.mult),
                      call(dve.e.tensor_tensor, kx, kx, wide(ky, 8), ALU.add),
                      ts(kxf, kxf, 1.0 / 192, 1e-6, ALU.mult, ALU.add))
            t = inv_sqrt(kxf, kxf, t, (k0, k1))
            t_fk = chain(dve, t, call(dve.e.tensor_tensor, fk, kx, wide(ckv, 8), ALU.mult),
                         call(dve.e.tensor_tensor, fr, kx, wide(r, 8), ALU.mult))
            KRR = SCR[:, 11520:11648].rearrange("p (t c) -> p t c", t=2)
            KRH = SCR[:, 10240:11264].rearrange("p (t h c) -> p t h c", t=2, h=8)
            for tt in range(2):
                kr = KR[:, tt, :].unsqueeze(1)
                gk = prm("kn_rope", 0, 64).unsqueeze(1)
                t = dve.do(call(dve.e.tensor_tensor, kr, kr, gk, ALU.mult), t_fk)
                t = rotate(KRR[:, tt, :].unsqueeze(1), kr, 1, tt, t)
                t_kr = dve.do(call(dve.e.tensor_tensor, KRH[:, tt], KRR[:, tt, :].unsqueeze(1).broadcast_to([128, 8, 64]),
                                   fr[:, tt, :].unsqueeze(2).broadcast_to([128, 8, 64]), ALU.mult), t, *t_qrt)
                k3 = KT[:, tt, :].rearrange("p (h c) -> p h c", h=8)
                t_kt = dve.do(call(dve.e.tensor_tensor, k3, k3, fk[:, tt, :].unsqueeze(2).broadcast_to([128, 8, 128]),
                                   ALU.mult), t_fk, t2)
            t_knt = to_features(KT, 8, KNT, (4, 5), [t_kt])
            for ap in (SCR[64:128, 5120:7168].rearrange("p (h t) -> p h t", h=8)[:, 0::2, :],
                       SCR[0:64, 5120:7168].rearrange("p (h t) -> p h t", h=8)[:, 1::2, :]):
                t_z = pool.do(call(pool.e.memset, ap, 0.0), pool.last, t_kt, act.last, pe.last)
            KRf = SCR[:, 10240:11264].rearrange("p (t c) -> p t c", t=2)
            for pr in range(4):
                b = 6 + pr % 2
                pe.wait(*bank_free[b])
                for tt in range(2):
                    t = pe.do(call(pe.e.transpose, PS[:, b, 128 * tt:128 * tt + 128],
                                   KRf[:, tt, 128 * pr:128 * pr + 128], ident), t_kr)
                for hh in range(2):
                    rows = slice(64 * hh, 64 * hh + 64)
                    t_kz = dve.do(call(dve.e.tensor_copy, KZR[rows, 2 * pr + hh, :], PS[rows, b, 0:256]), t, t_z)
                bank_free[b] = [t_kz]
            for n in range(2):
                bb = (0, 1) if n % 2 else (2, 3)
                pe.wait(*bank_free[bb[0]], *bank_free[bb[1]])
                vt = vtile(1, (4, 5), 512, 2, bb, x_tok[1])
                for tt in range(2):
                    t_v = act.do(call(act.e.activation, VT[:, tt, 512 * n:512 * n + 512], PS[:, bb[tt], :], ACT.Copy,
                                      scale=ckv[:, tt:tt + 1]), vt, t_c, *t_knt)
                    bank_free[bb[tt]] = [t_v]
                refill()
            x_free[1] = [vt]
            pe.wait(t_v, t_kz)
            dve.wait(t_nsq)

            def unit(u):
                return dict(heads=[dict(
                    score=[(0, 128, QNT[:, u, 0:128], KNT[:, u, 0:128], True, False),
                           (0, 128, QRT[:, u // 2, 0:128], KZR[:, u, 0:128], False, True),
                           (128, 256, QNT[:, u, 128:256], KNT[:, u, :], True, False),
                           (128, 256, QRT[:, u // 2, 128:256], KZR[:, u, :], False, True)],
                    wait=(*t_qn, *t_qrt, *t_knt), scale=(nsq[:, 0, u:u + 1], nsq[:, 1, u:u + 1]), gate=None,
                    v=[VT[:, kb, 128 * u:128 * u + 128] for kb in range(2)])], o=u, first=True, last=True, extra=None)
            attention(8, unit, P_at, PT_at, 384, 1, o_split())

        HG = SCR[:, 0:2048].rearrange("p (k t) -> p k t", k=8)
        hg_tok = [None] * 8

        def out_proj_moe(li):
            prior = lasts()
            for m in range(8):
                b = next_bank((0, 1, 2, 3))
                pe.wait(*bank_free[b])
                o = PS[:, b, 0:256]
                t = mtile(1, range(12), o, x_tok[1])
                if m == 7:
                    x_free[1] = [t]
                t1 = add_residual(m, o, t)
                bank_free[b] = [t1]
                hg_tok[m] = act.do(call(act.e.activation, HG[:, m, :], H[:, m, :], ACT.Copy,
                                        scale=prm("norm2", 8 * li + m)), t1, *prior)
                square_into(m, H[:, m, :], [t1])
                refill()

        def overflow(li, CW, POSX, t_flag, prior):
            q = {n: Queue(f"s_over{li}_{n}", e) for n, e in (("sp", nc.sync), ("pe", nc.tensor), ("act", nc.scalar),
                                                             ("dve", nc.vector))}
            osp, ope, oact, odve = (q[n] for n in ("sp", "pe", "act", "dve"))
            o_load = [sem(f"s_over{li}_w"), 0]
            W = SCR[:, 4096:6144].rearrange("p (u c) -> p u c", u=4)
            Y = SCR[:, 6144:8192].rearrange("p (t c) -> p t c", t=2)
            A = SCR[:, 8192:8704].rearrange("p (t c) -> p t c", t=2)
            AT = SCR[:, 8704:9216].rearrange("p (k t) -> p k t", k=2)
            CWO = SCR[:, 11392:11456].rearrange("p (t e) -> p t e", t=2)
            r = RC[:, 0, :]
            src = a["moe"][li].rearrange("(g u) p (e c) -> g e p u c", u=12, e=4)
            odve.do(call(odve.e.memset, SCR[:, 6144:8192], 0.0))
            t_y = odve.do(call(odve.e.scalar_tensor_tensor, CWO, POSX, 31.5, CW, ALU.is_ge, ALU.mult))
            t_w = t_av = t_down = None
            for e in range(32):
                for hf in range(2):
                    ld_ = osp.dma(W, src[e // 4, e % 4, :, 4 * hf:4 * hf + 4, :], o_load, t_w, ope.last)
                    for tt in range(2):
                        for k in range(4):
                            t_w = ope.do(call(ope.e.matmul, PS[:, 1 + tt, :], HG[:, 4 * hf + k, 128 * tt:128 * tt + 128],
                                              W[:, k, :], start=hf == 0 and k == 0, stop=hf == 1 and k == 3,
                                              skip_group_check=True), ld_, t_av)
                for tt in range(2):
                    t = oact.do(call(oact.e.activation, A[:, tt, :], PS[:, 1 + tt, 0:256], ACT.Silu, scale=r[:, tt:tt + 1]),
                                t_w, t_down)
                    t = odve.do(call(odve.e.scalar_tensor_tensor, A[:, tt, :], PS[:, 1 + tt, 256:512], r[:, tt:tt + 1],
                                     A[:, tt, :], ALU.mult, ALU.mult), t)
                    t_av = odve.do(call(odve.e.tensor_scalar, A[:, tt, :], A[:, tt, :], CWO[:, tt, e:e + 1], None,
                                        op0=ALU.mult), t, t_y)
                for tt in range(2):
                    for k in range(2):
                        t = ope.do(call(ope.e.transpose, PS[:, 3, 256 * k + 128 * tt:256 * k + 128 * tt + 128],
                                        A[:, tt, 128 * k:128 * k + 128], ident), t_av)
                t_at = oact.do(call(oact.e.activation, AT.rearrange("p k t -> p (k t)"), PS[:, 3, :], ACT.Copy), t)
                ld_ = osp.dma(W, src[e // 4, e % 4, :, 8:12, :], o_load, t_w)
                for tt in range(2):
                    for n in range(2):
                        b = (4, 6, 7, 3)[2 * tt + n]
                        for k in range(2):
                            t_down = ope.do(call(ope.e.matmul, PS[:, b, :], AT[:, k, 128 * tt:128 * tt + 128],
                                                 W[:, 2 * n + k, :], start=k == 0, stop=k == 1, skip_group_check=True),
                                            ld_, t_at, t_y)
                for tt in range(2):
                    for n in range(2):
                        y = Y[:, tt, 512 * n:512 * n + 512]
                        t_y = odve.do(call(odve.e.tensor_tensor, y, PS[:, (4, 6, 7, 3)[2 * tt + n], :], y, ALU.add),
                                      t_down, t_y)
                t_av = t_y
            for f in range(8):
                for tt in range(2):
                    t = ope.do(call(ope.e.transpose, PS[:, 1 + f // 2, 256 * (f % 2) + 128 * tt:256 * (f % 2) + 128 * tt + 128],
                                    Y[:, tt, 128 * f:128 * f + 128], ident), t_y)
            for f in range(4):
                h2 = H[:, 2 * f:2 * f + 2, :].rearrange("p k t -> p (k t)")
                odve.do(call(odve.e.tensor_tensor, h2, PS[:, 1 + f, :], h2, ALU.add), t)
            ends = [x.last for x in (ope, oact, odve)]
            for n, main in (("sp", sp), ("pe", pe), ("act", act), ("dve", dve)):
                q[n].wait(*ends)

                def emit(n=n, e=main.e, ops=q[n].ops):
                    with e.register(f"over{li}_{n}") as flag:
                        e.reg_load(flag, FLAG[0:1, li:li + 1])
                        with e.If_ne(flag, 0):
                            for op in ops:
                                op()
                main.wait(t_flag, *prior)
                main.ops.append(emit)

        def moe(li):
            XN = SCR[:, 2048:4096].rearrange("p (t c) -> p t c", t=2)
            XE = [SCR[:, 4096 + 1024 * i:5120 + 1024 * i].rearrange("p (k s) -> p k s", k=8) for i in range(2)]
            S = [SCR[:, 6144 + 256 * i:6400 + 256 * i].rearrange("p (t s) -> p t s", t=2) for i in range(2)]
            SW = [SCR[:, 6656 + 256 * i:6912 + 256 * i].rearrange("p (t s) -> p t s", t=2) for i in range(2)]
            SWT = [SCR[:, 7168 + 256 * i:7424 + 256 * i] for i in range(2)]
            SG = [SCR[:, 7680 + 256 * i:7936 + 256 * i] for i in range(2)]
            AV = [SCR[:, 8192 + 256 * i:8448 + 256 * i] for i in range(2)]
            AT = [SCR[:, 8704 + 256 * i:8960 + 256 * i].rearrange("p (k s) -> p k s", k=2) for i in range(2)]
            OE = [SCR[:, 9216 + 1024 * i:10240 + 1024 * i] for i in range(2)]
            POSX = SCR[:, 11264:11328].rearrange("p (t e) -> p t e", t=2)
            CW = SCR[:, 11328:11392].rearrange("p (t e) -> p t e", t=2)
            r = RC[:, 0, :]
            prior = lasts()
            u, w, loaded = next_raw()
            pe.wait(loaded, *bank_free[0])
            for k in range(8):
                t = pe.do(call(pe.e.matmul, PS[:, 0, 0:256], w[:, 128 * k:128 * k + 128], HG[:, k, :], start=k == 0,
                               stop=k == 7), hg_tok[k])
            give_back(u, [t])
            LT = SCR[:, 9216:9472]
            t_lt = act.do(call(act.e.activation, LT, PS[:, 0, 0:256], ACT.Copy), t, *prior)
            bank_free[0] = [t_lt]
            t_rc = rstd_cols(5, RC[:, 0, :])
            t_xn = []
            for tt in range(2):
                for kk in range(2):
                    b = 1 + 2 * tt + kk
                    pe.wait(*bank_free[b])
                    for k in range(4):
                        t = pe.do(call(pe.e.transpose, PS[:, b, 128 * k:128 * k + 128],
                                       HG[:, 4 * kk + k, 128 * tt:128 * tt + 128], ident), hg_tok[4 * kk + k])
                    if tt == 0 and kk == 0:
                        for t2 in range(2):
                            t_l = pe.do(call(pe.e.transpose, PS[:, 0, 128 * t2:128 * t2 + 128],
                                             LT[:, 128 * t2:128 * t2 + 128], ident), t_lt)
                    x = act.do(call(act.e.activation, XN[:, tt, 512 * kk:512 * kk + 512], PS[:, b, :], ACT.Copy,
                                    scale=r[:, tt:tt + 1]), t, t_rc, *prior)
                    bank_free[b] = [x]
                    t_xn.append(x)
            at = [9472]

            def new(*shape):
                n = int(np.prod(shape))
                ap = SCR[:, at[0]:at[0] + n]
                at[0] += n
                assert at[0] <= 11264
                if len(shape) == 2:
                    ap = ap.rearrange("p (a b) -> p a b", a=shape[0])
                return ap
            TT = lambda o, x, y, op: call(dve.e.tensor_tensor, o, x, y, op)
            TS = lambda o, x, s1, s2, o0, o1: call(dve.e.tensor_scalar, o, x, s1, s2, op0=o0, op1=o1)
            RED = lambda o, x, op: call(dve.e.tensor_reduce, o, x, AX.X, op)
            STT = lambda o, x, s, y, o0, o1: call(dve.e.scalar_tensor_tensor, o, x, s, y, o0, o1)
            wide = lambda ap, n: ap.unsqueeze(2).broadcast_to([128, 2, n])
            iota = lambda n: cst("iota", n).unsqueeze(1).broadcast_to([128, 2, n])
            L = new(2, 36)
            t = t_rc
            for tt in range(2):
                t = dve.do(STT(L[:, tt, :], PS[:, 0, 128 * tt:128 * tt + 36], r[:, tt:tt + 1],
                               prm("r_bias", 36 * li, 36), ALU.mult, ALU.add), t, t_l, *prior)
            bank_free[0] = [t]
            gm, eq, oh_g, gi, d4 = new(2), new(2, 4), new(2, 4), new(2), new(2, 4)
            lg = L[:, :, 0:4]
            t = chain(dve, t, RED(gm, lg, ALU.max), TT(eq, lg, wide(gm, 4), ALU.is_equal),
                      STT(eq, eq, -100.0, iota(4), ALU.mult, ALU.add), RED(gi, eq, ALU.min),
                      TT(oh_g, eq, wide(gi, 4), ALU.is_equal), TT(d4, lg, wide(gm, 4), ALU.subtract))
            t_ge = act.do(call(act.e.activation, d4, d4, ACT.Exp), t)
            pen, E1, E2 = new(2, 4), new(2, 32), new(2, 32)
            m1, m2, i1, i2 = new(2), new(2), new(2), new(2)
            q1, q2, o1, o2 = new(2, 32), new(2, 32), new(2, 32), new(2, 32)
            el4 = lambda ap: ap.rearrange("p t (g e) -> p t g e", g=4)
            t = chain(dve, t, TS(pen, oh_g, 1e30, -1e30, ALU.mult, ALU.add),
                      TT(el4(E1), el4(L[:, :, 4:36]), pen.unsqueeze(3).broadcast_to([128, 2, 4, 8]), ALU.add),
                      RED(m1, E1, ALU.max), TT(q1, E1, wide(m1, 32), ALU.is_equal),
                      STT(q1, q1, -100.0, iota(32), ALU.mult, ALU.add), RED(i1, q1, ALU.min),
                      TT(o1, q1, wide(i1, 32), ALU.is_equal), STT(E2, o1, -2e30, E1, ALU.mult, ALU.add),
                      RED(m2, E2, ALU.max), TT(q2, E2, wide(m2, 32), ALU.is_equal),
                      STT(q2, q2, -100.0, iota(32), ALU.mult, ALU.add), RED(i2, q2, ALU.min),
                      TT(o2, q2, wide(i2, 32), ALU.is_equal))
            mk = new(2, 32)
            t_mk = dve.do(TT(mk, o1, o2, ALU.add), t)
            before = cst("before", 128)
            pe.wait(t_mk, *bank_free[5])
            pe.run(call(pe.e.matmul, PS[:, 5, 0:32], before, mk[:, 0, :], start=True, stop=True, skip_group_check=True))
            pe.run(call(pe.e.matmul, PS[:, 5, 32:64], before, mk[:, 1, :], start=True, stop=False, skip_group_check=True))
            pe.run(call(pe.e.matmul, PS[:, 5, 32:64], ones, mk[:, 0, :], start=False, stop=True, skip_group_check=True))
            pe.run(call(pe.e.matmul, PS[:, 5, 64:96], ones, mk[:, 0, :], start=True, stop=False, skip_group_check=True))
            t_pos2 = pe.do(call(pe.e.matmul, PS[:, 5, 64:96], ones, mk[:, 1, :], start=False, stop=True,
                                skip_group_check=True))
            dd, gs, den, w1, w2 = new(2), new(2), new(2), new(2), new(2)
            t = dve.do(TT(dd, m2, m1, ALU.subtract), t_mk)
            t_e = act.do(call(act.e.activation, dd, dd, ACT.Exp), t)
            t = dve.do(RED(gs, d4, ALU.add), t_ge)
            dve.wait(t)
            t = chain(dve, t_e, STT(den, dd, 1.0, gs, ALU.add, ALU.mult), call(dve.e.reciprocal, w1, den),
                      TT(w2, w1, dd, ALU.mult), TT(o1, o1, wide(w1, 32), ALU.mult), TT(o2, o2, wide(w2, 32), ALU.mult),
                      TT(CW, o1, o2, ALU.add), TS(E2, mk, -1000.0, 1000.0, ALU.mult, ALU.add))
            t_px = dve.do(TT(POSX, E2, PS[:, 5, 0:64].rearrange("p (t e) -> p t e", t=2), ALU.add), t, t_pos2)
            cm = new(2)
            t = dve.do(RED(cm[:, 0:1], PS[:, 5, 64:96], ALU.max), t_px)
            t_flag = dve.do(call(dve.e.tensor_scalar, FLAG[:, li:li + 1], cm[:, 0:1], 32.5, None, op0=ALU.is_gt), t)
            bank_free[5] = [t]
            overflow(li, CW, POSX, t_flag, [*t_xn, *lasts(), *[t for b in bank_free for t in b]])

            tk = {}

            def places(g):
                s, i = S[g % 2], g % 2
                px = POSX[:, :, 4 * g:4 * g + 4].unsqueeze(3).broadcast_to([128, 2, 4, 32])
                cw = CW[:, :, 4 * g:4 * g + 4].unsqueeze(3).broadcast_to([128, 2, 4, 32])
                io = cst("iota", 32).unsqueeze(1).unsqueeze(1).broadcast_to([128, 2, 4, 32])
                v = lambda ap: ap.rearrange("p t (e s) -> p t e s", e=4)
                t = dve.do(TT(v(S[i]), io, px, ALU.is_equal), t_px, tk.get(("gather", g - 2)), tk.get(("turn", g - 2)),
                           dve.last)
                tk["S", g] = dve.do(TT(v(SW[i]), v(S[i]), cw, ALU.mult), t)

            def gather(g):
                for hf in range(2):
                    pe.wait(*bank_free[hf])
                    for k in range(4):
                        o = PS[:, hf, 128 * k:128 * k + 128]
                        for tt in range(2):
                            t = pe.do(call(pe.e.matmul, o, XN[:, tt, 128 * (4 * hf + k):128 * (4 * hf + k) + 128],
                                           S[g % 2][:, tt, :], start=tt == 0, stop=tt == 1, skip_group_check=True),
                                      tk["S", g], *t_xn)
                    dst = XE[g % 2][:, 4 * hf:4 * hf + 4, :].rearrange("p k s -> p (k s)")
                    before_ = tk.get(("gu", g - 2))
                    if hf:
                        t2 = dve.do(call(dve.e.tensor_copy, dst, PS[:, hf, :]), t, before_)
                    else:
                        t2 = act.do(call(act.e.activation, dst, PS[:, hf, :], ACT.Copy), t, before_)
                    bank_free[hf] = [t2]
                    tk["xe", g, hf] = t2
                tk["gather", g] = t

            def gate_up(g):
                pe.wait(*bank_free[2], tk["xe", g, 0], tk["xe", g, 1])
                for k in range(8):
                    u, w, loaded = next_raw()
                    pe.wait(loaded)
                    for e in range(4):
                        t = pe.do(call(pe.e.matmul, PS[32 * e:32 * e + 32, 2, :], XE[g % 2][:, k, 32 * e:32 * e + 32],
                                       w[:, 512 * e:512 * e + 512], start=k == 0, stop=k == 7, skip_group_check=True))
                    give_back(u, [t])
                tk["gu", g] = t
                i = g % 2
                ts = act.do(call(act.e.activation, SG[i], PS[:, 2, 0:256], ACT.Silu), t, tk.get(("av", g - 2)))
                tk["av", g] = dve.do(TT(AV[i], SG[i], PS[:, 2, 256:512], ALU.mult), ts, tk.get(("turn", g - 2)))
                bank_free[2] = [tk["av", g]]

            def turn_(g):
                i = g % 2
                pe.wait(*bank_free[5])
                for k in range(2):
                    t = pe.do(call(pe.e.transpose, PS[:, 5, 128 * k:128 * k + 128], AV[i][:, 128 * k:128 * k + 128],
                                   ident), tk["av", g])
                for tt in range(2):
                    t = pe.do(call(pe.e.transpose, PS[:, 5, 256 + 128 * tt:384 + 128 * tt], SW[i][:, tt, :], ident),
                              tk["S", g])
                tk["turn", g] = t
                ta = act.do(call(act.e.activation, AT[i].rearrange("p k s -> p (k s)"), PS[:, 5, 0:256], ACT.Copy), t,
                            tk.get(("down", g - 2)))
                tk["sw", g] = dve.do(call(dve.e.tensor_copy, SWT[i], PS[:, 5, 256:512]), ta, tk.get(("comb", g - 2)))
                tk["at", g] = ta
                bank_free[5] = [tk["sw", g]]

            def down(g):
                i = g % 2
                pe.wait(tk["at", g])
                for n in range(2):
                    pe.wait(*bank_free[3 + n])
                    for k in range(2):
                        u, w, loaded = next_raw()
                        pe.wait(loaded)
                        for e in range(4):
                            t = pe.do(call(pe.e.matmul, PS[32 * e:32 * e + 32, 3 + n, :], AT[i][:, k, 32 * e:32 * e + 32],
                                           w[:, 512 * e:512 * e + 512], start=k == 0, stop=k == 1, skip_group_check=True))
                        give_back(u, [t])
                    d = OE[i][:, 512 * n:512 * n + 512]
                    if n:
                        t2 = dve.do(call(dve.e.tensor_copy, d, PS[:, 3 + n, :]), t, tk.get(("comb", g - 2)))
                    else:
                        t2 = act.do(call(act.e.activation, d, PS[:, 3 + n, :], ACT.Copy), t, tk.get(("comb", g - 2)))
                    bank_free[3 + n] = [t2]
                    tk["oe", g, n] = t2
                tk["down", g] = t

            def combine(g):
                i = g % 2
                pe.wait(tk["sw", g])
                for f in range(4):
                    b = 6 + f % 2
                    pe.wait(*bank_free[b], tk["oe", g, f // 2])
                    for x in range(2):
                        t = pe.do(call(pe.e.matmul, PS[:, b, 256 * x:256 * x + 256],
                                       OE[i][:, 128 * (2 * f + x):128 * (2 * f + x) + 128], SWT[i], start=True, stop=True,
                                       skip_group_check=True))
                    h2 = H[:, 2 * f:2 * f + 2, :].rearrange("p k t -> p (k t)")
                    t2 = dve.do(TT(h2, PS[:, b, :], h2, ALU.add), t, h_tok[2 * f], h_tok[2 * f + 1])
                    h_tok[2 * f] = h_tok[2 * f + 1] = t2
                    bank_free[b] = [t2]
                    if g == 7:
                        for k in (2 * f, 2 * f + 1):
                            if li == 0:
                                new_h(k, prm("norm1", 8 + k))
                            else:
                                t_out.append(sp.dma(out[:, 256 * k:256 * k + 256], H[:, k, :], o_sems[k], h_tok[k]))
                tk["comb", g] = t

            places(0)
            places(1)
            gather(0)
            for g in range(8):
                gate_up(g)
                if g >= 1:
                    combine(g - 1)
                if g < 7:
                    gather(g + 1)
                turn_(g)
                down(g)
                if g + 2 < 8:
                    places(g + 2)
                if g == 6 and li == 0:
                    st["limit"] = bounds[1]
            refill()
            combine(7)

        def start_layer(gain_name, at):
            for k in range(8):
                new_h(k, prm(gain_name, at + k))
                if k % 2:
                    refill(1)

        stop = {"n": False}
        t_out = []
        o_sems = [[sem(f"s_out{i}"), 0] for i in range(8)]

        def write_out():
            for k in range(8):
                t_out.append(sp.dma(out[:, 256 * k:256 * k + 256], H[:, k, :], o_sems[k], h_tok[k]))
            sp.wait(*t_out)

        def program():
            start_layer("norm_mix", 0)
            for i in range(4):
                if i % 3 == 0:
                    nsa(i // 3)
                elif i == 1:
                    moba()
                else:
                    conv()
                out_proj(8, "norm_ffn", 8 * i)
                if upto == f"mix{i}":
                    return
                if i < 3:
                    ffn(i, lambda d, i=i: ("norm_mix", 8 * (i + 1) + d))
                else:
                    load_mem()
                    ffn(i, None, mem_hook)
                if upto == f"ffn{i}":
                    return

            pe.wait(*bank_free[0], *bank_free[1])
            mem_kv_keys()
            refill()
            final_norm(4)
            pe.wait(*bank_free[2], *bank_free[3])
            mem_kv_values()
            refill()
            if upto == "final":
                return
            gmlp()
            out_proj_moe(0)
            if upto == "x2_0":
                return
            moe(0)
            if upto == "moe0":
                return
            mla()
            out_proj_moe(1)
            if upto == "x2_1":
                return
            moe(1)
            return True

        if program():
            sp.wait(*t_out)
        else:
            write_out()

        with nc.Block() as block:
            @block.sync
            def _(e):
                for op in sp.ops:
                    op()

            @block.tensor
            def _(e):
                for op in pe.ops:
                    op()

            @block.scalar
            def _(e):
                for op in act.ops:
                    op()

            @block.vector
            def _(e):
                for op in dve.ops:
                    op()

            @block.gpsimd
            def _(e):
                for op in pool.ops:
                    op()


def by_rows(w):
    k, m = w.shape[0] // 128, w.shape[1] // 128
    t = w.reshape(k, 128, m, 128).transpose(2, 0, 1, 3).reshape(m * k // 8, 8, 128, 128)
    return t.transpose(0, 2, 1, 3).reshape(-1, 128, 1024)


def by_cols(w, per):
    k, cols = w.shape[0] // 128, w.shape[1]
    t = w.reshape(k, 128, cols)
    out = np.zeros((-(-k // per), 128, 1024), w.dtype)
    for b in range(out.shape[0]):
        for i in range(min(per, k - per * b)):
            out[b, :, cols * i:cols * i + cols] = t[per * b + i]
    return out


def columns(v):
    v = v.reshape(-1, v.shape[-1] // 128, 128)
    return v.transpose(2, 0, 1).reshape(128, -1)


def layout(x):
    x = {k: np.asarray(v) for k, v in x.items()}
    out = {"cst": CONST}

    def tokens_last(v):
        return v.reshape(256, 8, 128).transpose(2, 1, 0).reshape(128, 2048)

    out["xT"] = tokens_last(x["x"])
    out["memT"] = tokens_last(x["mem_2"])
    out["pos"] = x["positions_2"].reshape(2, 128).T

    pos = []
    for j in range(2):
        for name in ("nsa_cmp_pos_k", "nsa_cmp_pos_v"):
            p = x[name][j].reshape(16, 2, 64).transpose(2, 1, 0).reshape(64, 32)
            pos.append(np.concatenate([p, p], 0))
    w2 = []
    for j in range(2):
        for name in ("nsa_cmp_k_w2", "nsa_cmp_v_w2"):
            w2.append(x[name][j].reshape(2, 128, 64).transpose(1, 0, 2).reshape(128, 128))
    rows = lambda v: np.broadcast_to(v[None, :], (128, v.shape[0]))
    bias = [rows(np.concatenate([x["moe_b_group_2"][i], x["moe_b_expert_2"][i]])) for i in range(2)]
    prm = [columns(x["norm_mix"]), columns(x["norm_ffn"]), columns(x["norm_final"]), columns(x["mem_norm_g_2"]),
           columns(x["norm1_g_2"]), columns(x["norm2_g_2"]), columns(x["mem_qn_g_2"]), columns(x["mem_kn_g_2"]),
           x["conv_w"][0].reshape(3, 8, 128).transpose(2, 1, 0).reshape(128, 24),
           columns(x["b_q_norm_g_2"]), columns(x["b_kv_norm_g_2"]),
           columns(x["b_qn_g_2"][:, :128]), columns(x["b_kn_g_2"][:, :128]),
           rows(x["b_qn_g_2"][0, 128:]), rows(x["b_kn_g_2"][0, 128:])] + pos + w2 + bias
    out["prm"] = np.concatenate(prm, 1)

    in1, in2, wo, cmp_ = [], [], [], []
    heads = np.array([4 * (2 * p + h) + r for p in range(2) for r in range(4) for h in range(2)])
    perm = (64 * heads[:, None] + np.arange(64)[None]).reshape(-1)
    for j in range(2):
        w = x["nsa_w_in"][j]
        part = lambda i: w[:, 1024 + 256 * i:1280 + 256 * i]
        in1.append(np.concatenate([by_rows(part(0)), by_rows(part(1)), by_rows(w[:, :1024][:, perm])]))
        vg = np.concatenate([part(3), w[:, 2560:2608]], 1)
        in2.append(np.concatenate([by_rows(part(2)), by_rows(part(4)), by_cols(vg, 3), by_cols(part(5), 4)]))
        wo.append(by_rows(x["nsa_w_out"][j][perm]))
        c = np.stack([x["nsa_cmp_k_w1"][j], x["nsa_cmp_v_w1"][j]])
        cmp_.append(c.reshape(2, 8, 2, 128, 256).transpose(1, 3, 2, 0, 4).reshape(8, 128, 1024))
    out["nsa_in1"], out["nsa_in2"], out["nsa_out"], out["w_cmp"] = (np.stack(v) for v in (in1, in2, wo, cmp_))

    w = x["moba_w_in"][0]
    out["moba_in"] = np.concatenate([by_rows(w[:, :2048]), by_cols(w[:, 2048:2560], 2), by_cols(w[:, 2560:], 2)])[None]
    out["moba_out"] = by_rows(x["moba_w_out"][0])[None]
    b, c, u = (by_rows(x["conv_w_in"][0][:, 1024 * i:1024 * i + 1024]) for i in range(3))
    out["conv_in"] = np.stack([c, u, b], 1).reshape(24, 128, 1024)[None]
    out["conv_out"] = by_rows(x["conv_w_out"][0])[None]

    ffn = []
    for i in range(4):
        g, u, d = by_rows(x["ffn_w_gate"][i]), by_rows(x["ffn_w_up"][i]), x["ffn_w_down"][i].reshape(22, 128, 1024)
        seq = []
        for f in range(22):
            seq += [g[f], u[f]]
            if 1 <= f <= 19:
                seq.append(d[f - 1])
        ffn.append(np.stack(seq + [d[19], d[20], d[21]]))
    out["ffn"] = np.stack(ffn)

    w = x["w_mem_kv_2"]
    out["mem_kv"] = np.concatenate([by_cols(w[:, :512], 2), by_cols(w[:, 512:], 2)])[None]
    w = x["a_w_in_2"][0]
    out["a_in"] = np.concatenate([by_cols(w[:, 1024:1536], 2), by_cols(w[:, 1536:2048], 2), by_cols(w[:, 2048:], 2),
                                  by_rows(w[:, :1024])])[None]
    out["a_out"] = by_rows(x["a_w_out_2"][0])[None]
    ln = np.concatenate([x["a_ln_g_2"][0], x["a_ln_b_2"][0]])
    out["a_ln"] = np.broadcast_to(ln[None], (128, 2048))
    out["a_ws"] = x["a_w_s_2"][0].transpose(2, 0, 1).reshape(128, 1024)
    out["a_bs"] = np.broadcast_to(x["a_b_s_2"][0].reshape(1, 1024), (128, 1024))
    rt = []
    for i in range(2):
        w = np.zeros((1024, 128), np.float32)
        w[:, :4], w[:, 4:36] = x["moe_w_group_2"][i], x["moe_w_expert_2"][i]
        rt.append(by_rows(w))
    out["router"] = np.stack(rt)
    w = x["b_w_in_2"][0]
    out["b_in"] = np.concatenate([by_cols(w[:, :512], 2), by_cols(w[:, 512:832], 3), by_cols(w[:, 832:], 2)])[None]
    w = x["b_w_q_up_2"][0]
    out["b_q_up"] = np.concatenate([by_cols(w[:, 512 * i:512 * i + 512], 2) for i in range(3)])[None]
    w = x["b_w_kv_up_2"][0].reshape(256, 8, 2, 128)
    kv = [np.ascontiguousarray(w[:, :, i]).reshape(256, 1024) for i in range(2)]
    out["b_kv_up"] = np.concatenate([by_cols(v[:, 512 * i:512 * i + 512], 2) for v in kv for i in range(2)])[None]
    out["b_out"] = by_rows(x["b_w_out_2"][0])[None]

    g, u = (x[n].reshape(2, 8, 4, 8, 128, 256) for n in ("moe_w_gate_2", "moe_w_up_2"))
    moe = np.empty((2, 8, 12, 128, 4, 512), np.float32)
    moe[:, :, :8, :, :, :256] = g.transpose(0, 1, 3, 4, 2, 5)
    moe[:, :, :8, :, :, 256:] = u.transpose(0, 1, 3, 4, 2, 5)
    d = x["moe_w_down_2"].reshape(2, 8, 4, 2, 128, 2, 512)
    moe[:, :, 8:] = d.transpose(0, 1, 5, 3, 4, 2, 6).reshape(2, 8, 4, 128, 4, 512)
    out["moe"] = moe.reshape(2, 96, 128, 2048)
    return {k: np.ascontiguousarray(v) for k, v in out.items()}


def kernel(**inputs):
    import concourse.bacc as _bacc
    from concourse import mybir as _mybir
    from concourse.bass_utils import run_bass_kernel_spmd as _run

    nc = _bacc.Bacc("TRN2", target_bir_lowering=False, num_devices=1)
    arrays = layout(inputs)
    args = {n: nc.dram_tensor(n, v.shape, _mybir.dt.from_np(v.dtype), kind="ExternalInput").ap()
            for n, v in arrays.items()}
    y = nc.dram_tensor("out_0_dram", (128, 2048), _mybir.dt.float32, kind="ExternalOutput").ap()
    blocks_kernel(nc, args, y)
    r = _run(nc, [arrays], core_ids=[0])
    got = np.asarray(r.results[0]["out_0_dram"])
    return got.reshape(128, 8, 256).transpose(2, 1, 0).reshape(1, 256, 1024)
```

```python
import concourse.bass as bass
from concourse import mybir
from contextlib import ExitStack
import numpy as np


def const_table():
    p = np.arange(128)
    parts, at, n = {}, {}, 0

    def add(name, a):
        nonlocal n
        parts[name] = np.broadcast_to(np.asarray(a, np.float32), (128, np.asarray(a).shape[-1]))
        at[name] = n
        n += parts[name].shape[1]

    add("ident", np.eye(128))
    add("ones", np.ones((128, 128)))
    tri = np.where(p[None, :] <= p[:, None], 0.0, -1e30)
    add("mask", np.concatenate([np.zeros((128, 256)), tri], 1))
    c = np.arange(16)
    cm = [np.where((16 * c[None] + 31 <= p[:, None] + 128 * q) & (c[None] < 15), 0.0, -1e30) for q in range(2)]
    add("cmask", np.concatenate(cm, 1))
    add("before", (p[:, None] < p[None, :]).astype(np.float32))
    add("iota", np.arange(32)[None, :])
    add("inv", (10000.0 ** (-(np.arange(32) * 2.0 / 64))).astype(np.float32)[None, :])
    add("eps", np.full((128, 1), 1e-6))
    return np.ascontiguousarray(np.concatenate(list(parts.values()), 1)), at, n


CONST, CAT, NCONST = const_table()

PARAMS = [("norm_mix", 32), ("norm_ffn", 32), ("norm_final", 8), ("mem_norm", 8), ("norm1", 16), ("norm2", 16),
          ("mem_qn", 2), ("mem_kn", 2), ("conv_w", 24), ("q_norm", 4), ("kv_norm", 2), ("qn_nope", 1), ("kn_nope", 1),
          ("qn_rope", 64), ("kn_rope", 64), ("cmp_pos", 128), ("cmp_w2", 512), ("r_bias", 72)]
PAT, NPARAM = {}, 0
for _name, _n in PARAMS:
    PAT[_name] = NPARAM
    NPARAM += _n

NSLOT, NMORE, NPREP = 20, 6, 8
NSCR = 13824


def blocks_kernel(nc, a, out):
    F32, F32R, I32 = mybir.dt.float32, mybir.dt.float32r, mybir.dt.int32
    ALU, ACT, AX = mybir.AluOpType, mybir.ActivationFunctionType, mybir.AxisListType
    ctx = ExitStack()

    def sb(name, shape, dt=F32):
        return ctx.enter_context(nc.sbuf_tensor(name, shape, dt))

    def both(name, shape):
        with nc.sbuf_tensor(name, shape, F32R) as rounded:
            pass
        return rounded, sb(name + "_f", shape)

    def sem(name):
        return ctx.enter_context(nc.semaphore(name))

    def call(f, *args, **kw):
        return lambda: f(*args, **kw)

    class Queue:



        def __init__(self, name, e):
            self.sem, self.e, self.ops, self.count, self.met = sem(name), e, [], 0, {}

        def wait(self, *tokens):
            for t in tokens:
                if t is not None and self.met.get(t[0].name, 0) < t[1]:
                    self.met[t[0].name] = t[1]
                    self.ops.append(call(self.e.wait_ge, t[0], t[1]))

        def run(self, op, *tokens):
            self.wait(*tokens)
            self.ops.append(op)

        def do(self, op, *tokens):
            self.wait(*tokens)
            self.count += 1
            self.ops.append(lambda: op().then_inc(self.sem, 1))
            return (self.sem, self.count)

        @property
        def last(self):
            return (self.sem, self.count) if self.count else None

        def dma(self, dst, src, s, *tokens):
            self.wait(*tokens)
            s[1] += 16
            v = s[1]
            self.ops.append(lambda: self.e.dma_start(dst, src).then_inc(s[0], 16))
            return (s[0], v)

    with ctx:
        RINGR, RING = both("RING", [128, NSLOT, 1024])
        (XH0, FH0), (XL0, FL0), (XH1, FH1), (XL1, FL1) = (both(n, [128, k, 256]) for n, k in (
            ("XH0", 8), ("XL0", 8), ("XH1", 12), ("XL1", 12)))
        XH, XL = [XH0, XH1], [XL0, XL1]
        H = sb("H", [128, 8, 256])
        (GH, FGH), (GL, FGL) = (both(n, [128, 3, 256]) for n in ("GH", "GL"))
        CST = sb("CST", [128, NCONST])
        PRM = sb("PRM", [128, NPARAM])
        RB = sb("RB", [128, 2, 256])
        RC = sb("RC", [128, 2, 2])
        SQ = sb("SQ", [128, 2, 256])
        ACC = sb("ACC", [128, 256])
        NT = sb("NT", [128, 3, 256])
        ST = sb("ST", [128, 4, 24])
        SM = sb("SM", [128, 320])
        ROT = sb("ROT", [128, 384])
        POSI = sb("POSI", [128, 2], I32)
        FLAG = sb("FLAG", [128, 2], I32)
        SCR = sb("SCR", [128, NSCR])
        PS = ctx.enter_context(nc.psum_tensor("PS", [128, 8, 512], F32))

        pe, act, dve, pool, sp = (Queue(*n) for n in (
            ("s_pe", nc.tensor), ("s_act", nc.scalar), ("s_dve", nc.vector), ("s_pool", nc.gpsimd), ("s_sp", nc.sync)))
        everyone = (pe, act, dve, pool)


        def cst(name, n, at=0):
            return CST[:, CAT[name] + at:CAT[name] + at + n]

        def prm(name, at=0, n=1):
            return PRM[:, PAT[name] + at:PAT[name] + at + n]

        def lasts():
            return [q.last for q in everyone]

        def f32(ap):
            return ap.bitcast(F32)

        units, dense_ids, raw_ids = [], [], []

        def section(name, j):
            for b in range(a[name].shape[1]):
                dense_ids.append(len(units))
                units.append(a[name][j, b])

        def raws(name, j):
            for b in range(a[name].shape[1]):
                raw_ids.append(len(units))
                units.append(a[name][j, b])

        bounds = {}
        for i in range(4):
            if i % 3 == 0:
                section("nsa_in1", i // 3)
                raws("w_cmp", i // 3)
                section("nsa_in2", i // 3)
                section("nsa_out", i // 3)
            elif i % 3 == 1:
                section("moba_in", 0)
                section("moba_out", 0)
            else:
                section("conv_in", 0)
                section("conv_out", 0)
            section("ffn", i)
        section("mem_kv", 0)
        section("a_in", 0)
        section("a_out", 0)
        bounds[0] = len(dense_ids)
        raws("router", 0)
        raws("moe", 0)
        section("b_in", 0)
        section("b_up", 0)
        section("b_out", 0)
        bounds[1] = len(dense_ids)
        raws("router", 1)
        raws("moe", 1)
        is_dense = [False] * len(units)
        for u in dense_ids:
            is_dense[u] = True

        slot_sem = [[sem(f"s_slot{i}"), 0] for i in range(NSLOT + NMORE)]
        free = [(i, []) for i in range(NSLOT)]
        where = {}
        st = dict(issued=0, dense=0, prepped=0, released=0, limit=bounds[0], raw=0, x=0)
        w_at, w_ready, w_left, halves = {}, {}, {}, []

        def slot(s):
            if s < NSLOT:
                return RING[:, s, :]
            s -= NSLOT
            x = (FH1, FL1)[s % 2]
            return x[:, 4 * (s // 2):4 * (s // 2) + 4, :].rearrange("p k t -> p (k t)")

        def take(dense):
            for i, (s, tokens) in enumerate(free):
                if s < NSLOT or not dense:
                    return free.pop(i)
            return None

        def room(dense):
            return sum(1 for s, _ in free if s < NSLOT or not dense)

        def pump(n=99999):
            while st["issued"] < min(n, len(units)):
                u = st["issued"]
                d = is_dense[u]
                kept = min(NPREP - (st["prepped"] - st["released"]), st["dense"] + d - st["prepped"])
                if room(d) - 1 < kept:
                    return
                s, tokens = take(d)
                where[u] = (s, sp.dma(slot(s), units[u], slot_sem[s], *tokens))
                st["dense"] += d
                st["issued"] += 1

        def lend():
            free.extend((NSLOT + i, list(x_free[1])) for i in range(NMORE))
            pump()

        def reclaim():
            more = [f for f in free if f[0] >= NSLOT]
            assert len(more) == NMORE
            x_free[1] = [t for _, tokens in more for t in tokens]
            free[:] = [f for f in free if f[0] < NSLOT]

        def give_back(u, tokens):
            free.append((where[u][0], list(tokens)))
            pump()

        def prep_high():
            b = st["prepped"]
            if b >= st["limit"] or b - st["released"] >= NPREP or not room(True):
                return False
            u = dense_ids[b]
            if u not in where:
                return False
            c, loaded = where[u]
            h, tokens = take(True)
            raw = slot(c)
            w_at[b] = (h, c, RINGR[:, h, :], RINGR[:, c, :])
            halves.append((b, act.do(call(act.e.activation, w_at[b][2], raw, ACT.Copy), loaded, *tokens)))
            w_left[b] = 1024
            st["prepped"] += 1
            pump()
            return True

        def prep_low():
            b, t = halves.pop(0)
            _, c, wh, wl = w_at[b]
            w_ready[b] = dve.do(call(dve.e.tensor_tensor, wl, slot(c), f32(wh), ALU.subtract), t)

        def fill_in():
            if halves:
                prep_low()

        def refill(n=2):
            for _ in range(n):
                if not prep_high():
                    break
            while len(halves) > 1:
                prep_low()

        def weights(x, n):
            b, c = divmod(x, 1024)
            while b not in w_ready:
                if not halves:
                    assert prep_high()
                prep_low()
            pe.wait(w_ready[b])
            assert c + n <= 1024
            return w_at[b][2][:, c:c + n], w_at[b][3][:, c:c + n]

        def ends_block(x, n):
            w_left[x // 1024] -= n
            return w_left[x // 1024] == 0

        def release(x, token):
            assert token[0] is pe.sem
            h, c, _, _ = w_at[x // 1024]
            free.append((h, [token]))
            free.append((c, [token]))
            st["released"] += 1
            pump()

        def next_raw():
            u = raw_ids[st["raw"]]
            st["raw"] += 1
            c, loaded = where[u]
            return u, slot(c), loaded

        bank_free = [[] for _ in range(8)]
        turn = dict(b=0)

        def next_bank(banks):
            b = banks[turn["b"] % len(banks)]
            turn["b"] += 1
            return b

        def three(o, wh, wl, xh, xl, start, stop, signal, swap=False):
            for i, (l, r) in enumerate(((wh, xh), (wh, xl), (wl, xh))):
                if swap:
                    l, r = r, l
                f = (call(pe.e.matmul, o, l, r, start=start and i == 0, stop=stop and i == 2,
                                                     skip_group_check=True))
                if signal and i == 2:
                    return pe.do(f)
                pe.run(f)

        def grid(xi, ks, outs, x_tokens, fresh=None):
            base, tokens = st["x"], [None] * len(outs)
            st["x"] += 128 * len(ks) * len(outs)

            def steps():
                for n, k in enumerate(ks):
                    for m, o in enumerate(outs):
                        x = base + 128 * (m * len(ks) + n)
                        wh, wl = weights(x, 128)
                        assert x_tokens[k] is not None
                        pe.wait(x_tokens[k])
                        full, last = ends_block(x, 128), n == len(ks) - 1
                        t = three(o, wh, wl, XH[xi][:, k, :], XL[xi][:, k, :],
                                  n == 0 and (fresh is None or fresh[m]), last, full or last)
                        if last:
                            tokens[m] = t
                        if full:
                            release(x, t)
                    yield
            return tokens, steps()

        def group(xi, ks, banks, x_tokens):
            for b in banks:
                pe.wait(*bank_free[b])
            tokens, steps = grid(xi, ks, [PS[:, b, 0:256] for b in banks], x_tokens)
            for _ in steps:
                pass
            return tokens

        def mtile(xi, ks, o, x_tokens):
            tokens, steps = grid(xi, ks, [o], x_tokens)
            for _ in steps:
                pass
            return tokens[0]

        def vtile(xi, ks, cols, per_block, banks, x_tokens):
            for n, k in enumerate(ks):
                x = st["x"] + cols * (n % per_block)
                wh, wl = weights(x, cols)
                assert x_tokens[k] is not None
                pe.wait(x_tokens[k])
                end = (n + 1) % per_block == 0 or n == len(ks) - 1
                for tt in range(2):
                    sl = slice(128 * tt, 128 * (tt + 1))
                    t = three(PS[:, banks[tt], 0:cols], wh, wl, XH[xi][:, k, sl], XL[xi][:, k, sl],
                              n == 0, n == len(ks) - 1, tt == 1, swap=True)
                if end:
                    release(x, t)
                    st["x"] += 1024
            return t

        def vtiles(xi, ks, banks):
            t = [None, None]

            def steps():
                for b in banks:
                    pe.wait(*bank_free[b], *bank_free[b + 1])
                for n in range(0, len(ks), 2):
                    for v, b in enumerate(banks):
                        for i in range(2):
                            k = ks[n + i]
                            x = st["x"] + 512 * i
                            wh, wl = weights(x, 512)
                            assert x_tok[xi][k] is not None
                            pe.wait(x_tok[xi][k])
                            for tt in range(2):
                                sl = slice(128 * tt, 128 * (tt + 1))
                                t[v] = three(PS[:, b + tt, :], wh, wl, XH[xi][:, k, sl], XL[xi][:, k, sl], n + i == 0,
                                             n + i == len(ks) - 1, tt == 1, swap=True)
                        release(x, t[v])
                        st["x"] += 1024
                    yield
            return t, steps()

        def load(name, dst, src):
            return sp.dma(dst, src, [sem(name), 0])
        t_first = load("s_gain", PRM[:, 0:32], a["prm"][:, 0:32])
        h2 = H[:, :, :].rearrange("p k t -> p (k t)")
        t_x = [load(f"s_x{i}", h2[:, 1024 * i:1024 * i + 1024], a["xT"][:, 1024 * i:1024 * i + 1024]) for i in range(2)]
        pump(4)
        t_cst = load("s_cst", CST[:, :], a["cst"])
        t_prm = load("s_prm", PRM[:, 32:NPARAM], a["prm"][:, 32:NPARAM])
        t_pos = load("s_pos", POSI[:, :], a["pos"])
        pump()
        for q in (act, dve):
            q.wait(t_first)

        def constants():
            for q in everyone:
                q.wait(t_cst, t_prm)

        ident = cst("ident", 128)
        ones = cst("ones", 128)
        eps = cst("eps", 1)

        def scr(at, n, **dims):
            return SCR[:, at:at + n]

        h_tok = [t_x[0]] * 4 + [t_x[1]] * 4
        x_tok = {0: [None] * 12, 1: [None] * 12}
        x_free = {0: [], 1: []}

        def done_with(xi, token):
            x_free[xi] = [token]
            x_tok[xi][:] = [None] * 12
        sq_tok = [None, None]
        norm = dict(acc=None, n=0, rb=0, readers=[])

        def split_into(xi, k, src, tokens, gain=None):
            xh, xl = XH[xi][:, k, :], XL[xi][:, k, :]
            if gain is None:
                t1 = act.do(call(act.e.activation, xh, src, ACT.Copy), *tokens, *x_free[xi])
                fill_in()
                t2 = dve.do(call(dve.e.tensor_tensor, xl, src, f32(xh), ALU.subtract), t1)
            else:
                t1 = act.do(call(act.e.activation, xh, src, ACT.Copy, scale=gain), *tokens, *x_free[xi])
                fill_in()
                t2 = dve.do(call(dve.e.scalar_tensor_tensor, xl, src, gain, f32(xh), ALU.mult, ALU.subtract), t1)
            x_tok[xi][k] = t2
            return t2

        def square_into(k, src, tokens):
            if k == 0:
                norm["acc"] = act.do(call(act.e.activation, ACC[:, :], src, ACT.Square), *tokens, norm["acc"],
                                     *norm["readers"])
                return
            b = k % 2
            t = act.do(call(act.e.activation, SQ[:, b, :], src, ACT.Square), *tokens, sq_tok[b])
            t = pool.do(call(pool.e.tensor_tensor, ACC[:, :], ACC[:, :], SQ[:, b, :], ALU.add), t, norm["acc"], pool.last)
            sq_tok[b] = t
            norm["acc"] = t

        nt_free = [[], [], []]

        def newton(y, y0, x, tok, tmp):
            t = dve.do(call(dve.e.tensor_tensor, tmp, y0, y0, ALU.mult), tok)
            t = dve.do(call(dve.e.tensor_tensor, tmp, tmp, x, ALU.mult), t)
            t = dve.do(call(dve.e.tensor_scalar, tmp, tmp, -0.5, 1.5, op0=ALU.mult, op1=ALU.add), t)
            return dve.do(call(dve.e.tensor_tensor, y, tmp, y0, ALU.mult), t)

        def rstd_bcast(bank, mean=1024):
            i = norm["rb"] = 1 - norm["rb"]
            o = PS[:, bank, 0:256]
            t = pe.do(call(pe.e.matmul, o, ones, ACC[:, :], start=True, stop=True), norm["acc"], *bank_free[bank])
            norm["readers"] = [t]
            y0, x, tmp = NT[:, 0, :], NT[:, 1, :], NT[:, 2, :]
            t1 = dve.do(call(dve.e.tensor_scalar, x, o, 1.0 / mean, 1e-6, op0=ALU.mult, op1=ALU.add), t, dve.last)
            t2 = act.do(call(act.e.activation, y0, x, ACT.Abs_reciprocal_sqrt), t1)
            bank_free[bank] = [t1]
            norm["t_rb"] = newton(RB[:, i, :], y0, x, t2, tmp)
            return RB[:, i, :], norm["t_rb"]

        def rstd_cols(bank, dst, mean=1024):
            for tt in range(2):
                o = PS[:, bank, tt:tt + 1]
                t = pe.do(call(pe.e.matmul, o, ACC[:, 128 * tt:128 * tt + 128], ones[:, 0:1], start=True,
                                                         stop=True, skip_group_check=True),
                          norm["acc"], *bank_free[bank])
            norm["readers"] = [t]
            x, y0, tmp = ST[:, 0, 0:2], ST[:, 0, 2:4], ST[:, 0, 4:6]
            t1 = dve.do(call(dve.e.tensor_scalar, x, PS[:, bank, 0:2], 1.0 / mean, 1e-6, op0=ALU.mult, op1=ALU.add),
                        t, dve.last)
            bank_free[bank] = [t1]
            t2 = act.do(call(act.e.activation, y0, x, ACT.Abs_reciprocal_sqrt), t1)
            norm["t_rc"] = newton(dst, y0, x, t2, tmp)
            return norm["t_rc"]

        def cols_of_rb(bank, rb, t_rb):
            for tt in range(2):
                o = PS[:, bank, 128 * tt:128 * tt + 128]
                t = pe.do(call(pe.e.transpose, o, rb[:, 128 * tt:128 * tt + 128], ident), t_rb,
                          *bank_free[bank])
            src = PS[:, bank, 0:256].rearrange("p (a b) -> p a b", a=2)[:, :, 0:1]
            dst = RC[:, 0, :].unsqueeze(2)
            t = dve.do(call(dve.e.tensor_copy, dst, src), t, dve.last)
            bank_free[bank] = [t]
            return t

        def add_residual(k, o, t, bank_release=None):
            t1 = dve.do(call(dve.e.tensor_tensor, H[:, k, :], o, H[:, k, :], ALU.add), t, h_tok[k])
            h_tok[k] = t1
            return t1

        def new_h(k, gain, split=True):
            if split:
                split_into(0, k, H[:, k, :], [h_tok[k]], gain)
            square_into(k, H[:, k, :], [h_tok[k]])

        def out_begin(ks, banks):
            outs = [PS[:, b, 256 * h:256 * h + 256] for b in banks for h in range(2)]
            tokens, steps = grid(1, ks, outs, x_tok[1], (True, False, True, False))

            def go():
                for b in banks:
                    pe.wait(*bank_free[b])
                for _ in steps:
                    first["n"] += 1
                    yield
            first = dict(ks=ks, outs=outs, tokens=tokens, steps=go(), banks=banks, n=0)
            return first

        def out_proj(first, banks, evict):
            ks, b4 = first["ks"], banks[0]
            for _ in range(len(ks) - 1 - first["n"]):
                next(first["steps"])
            pe.wait(*bank_free[b4])
            t4, fifth = grid(1, ks, [PS[:, b4, 0:256]], x_tok[1])
            for _ in range(len(ks) - 1):
                next(fifth)
            for steps in (first["steps"], fifth):
                for _ in steps:
                    pass
            for m in range(8):
                if m < 4:
                    o, t, b = first["outs"][m], first["tokens"][m | 1], first["banks"][m // 2]
                elif m == 4:
                    o, t, b = PS[:, b4, 0:256], t4[0], b4
                else:
                    b = banks[m % len(banks)]
                    pe.wait(*bank_free[b])
                    o = PS[:, b, 0:256]
                    t = mtile(1, ks, o, x_tok[1])
                if m == 7:
                    done_with(1, t)
                t1 = add_residual(m, o, t)
                bank_free[b] = [t1]
                evict(m)
                if m >= 0:
                    refill(1 if m < 7 else 2)

        def ffn_input(i):
            return lambda m: new_h(m, prm("norm_ffn", 8 * i + m))

        def ffn(i, next_gain, hook=None):
            def temp(b, o):
                return SCR[:, 512 * o + 256 * b:512 * o + 256 * b + 256]

            rb = t_rb = None
            acts = {}
            down_tok = {}
            g_free = [[], [], []]

            def gate_up(fs):
                bs = [next_bank((0, 1, 2, 3)) for _ in fs]
                for b in bs:
                    pe.wait(*bank_free[b])
                tokens, steps = grid(0, range(8), [PS[:, b, 256 * i:256 * i + 256] for b in bs for i in range(2)], x_tok[0],
                                     (True, False) * len(fs))
                for _ in steps:
                    pass
                return [(b, tokens[2 * i + 1]) for i, b in enumerate(bs)]

            def chain(f, b, tu):
                p = f % 2
                t1, sg, t2 = temp(p, 0), temp(p, 1), temp(p, 2)
                ta = dve.do(call(dve.e.tensor_tensor, t1, PS[:, b, 0:256], rb, ALU.mult), tu, t_rb)
                ts = act.do(call(act.e.activation, sg, t1, ACT.Silu), ta)
                tb = dve.do(call(dve.e.tensor_tensor, t2, PS[:, b, 256:512], rb, ALU.mult))
                bank_free[b] = [tb]
                if f < 21:
                    fill_in()
                tc = dve.do(call(dve.e.tensor_tensor, t2, sg, t2, ALU.mult), ts, tb)
                s = f % 3
                th = act.do(call(act.e.activation, GH[:, s, :], t2, ACT.Copy), tc, *g_free[s])
                prep_high()
                if f < 21:
                    fill_in()
                acts[f] = dve.do(call(dve.e.tensor_tensor, GL[:, s, :], t2, f32(GH[:, s, :]), ALU.subtract), th)

            def down(fs):
                base = st["x"]
                for f in fs:
                    pe.wait(acts[f])
                for d in range(8):
                    bank = 4 + d // 2
                    o = PS[:, bank, 256 * (d % 2):256 * (d % 2) + 256]
                    if fs[0] == 0 and d % 2 == 0:
                        pe.wait(*bank_free[bank])
                    for j, f in enumerate(fs):
                        x = base + 1024 * j + 128 * d
                        wh, wl = weights(x, 128)
                        last = f == 21
                        full = ends_block(x, 128)
                        t = three(o, wh, wl, GH[:, f % 3, :], GL[:, f % 3, :], f == 0 and d % 2 == 0, last, last or full)
                        if full:
                            release(x, t)
                            g_free[f % 3] = [t]
                    if fs[-1] == 21:
                        down_tok[d] = t
                st["x"] += 1024 * len(fs)

            for f in range(22):
                if f == 0:
                    first = gate_up((0, 1))
                    rb, t_rb = rstd_bcast(7)
                    refill()
                b, tu = first[f] if f < 2 else gate_up((f,))[0]
                if f == 21:
                    done_with(0, tu)
                if f >= 3:
                    down([f - 3])
                if hook:
                    hook(f)
                chain(f, b, tu)
                refill(3)
            down([19])
            down([20, 21])
            for d in range(8):
                bank = 4 + d // 2
                o = PS[:, bank, 256 * (d % 2):256 * (d % 2) + 256]
                t1 = add_residual(d, o, down_tok[d | 1])
                bank_free[bank] = [t1]
                if next_gain is not None:
                    new_h(d, prm(*next_gain(d)))
                else:
                    new_h(d, None, split=False)
            refill(4)

        def attention(n, unit, P_at, PT_at, width, finish, causal=True, sb=(2, 3), tb=(4, 5), ob=(6, 7), fill=None):
            heads = len(unit(0)["heads"])
            NP = 3
            n0, n1 = (128, 256) if causal else (256, 256)
            sbank = lambda u, h: sb[(heads * u + h) % len(sb)]
            tbank = lambda u, h: tb[(heads * u + h) % len(tb)]
            obank = lambda j: ob[j % len(ob)]
            fill = fill or (lambda s, i: None)
            Pb = lambda u, h: SCR[:, P_at + ((u % NP) * heads + h) * width:P_at + ((u % NP) * heads + h) * width + width]
            Tb = lambda u, h: SCR[:, PT_at + ((u % 2) * heads + h) * width:PT_at + ((u % 2) * heads + h) * width + width]
            tok = {}
            p_free = [[t for t in lasts()] for _ in range(NP)]
            t_free = [[t for t in lasts()] for _ in range(2)]

            def A(u):
                w = unit(u)
                for h, hd in enumerate(w["heads"]):
                    b = sbank(u, h)
                    pe.wait(*bank_free[b])
                    ms = hd["score"]
                    for i, (x, nn, l, r, s0, s1) in enumerate(ms):
                        f = call(pe.e.matmul, 
                            PS[:, b, x:x + nn], l, r, start=s0, stop=s1, skip_group_check=True)
                        pe.wait(*hd.get("wait", ()))
                        if i == len(ms) - 1:
                            tok["A", u, h] = pe.do(f)
                        else:
                            pe.run(f)

            def B(u):
                w = unit(u)
                for h, hd in enumerate(w["heads"]):
                    b = sbank(u, h)
                    p = Pb(u, h)
                    nb = ST[:, u % 4, 2 * h:2 * h + 2]
                    for q, (x, nn) in enumerate(((0, n0), (n0, n1))):
                        mask = cst("mask", nn, 384 - nn) if causal else cst("mask", nn)
                        sc = hd["scale"][q] if hd["scale"] is not None else -1.0
                        t = dve.do(call(dve.e.tensor_tensor_reduce, 
                            out=p[:, x:x + nn], in0=PS[:, b, x:x + nn], in1=mask, scale=sc, scalar=3e38,
                            op0=ALU.add, op1=ALU.min, accum_out=nb[:, q:q + 1]),
                            tok["A", u, h], *p_free[u % NP])
                    tok["B", u, h] = t
                    bank_free[b] = [t]

            def C(u):
                w = unit(u)
                for h, hd in enumerate(w["heads"]):
                    p = Pb(u, h)
                    for q, (x, nn) in enumerate(((0, n0), (n0, n1))):
                        t = act.do(call(act.e.activation, 
                            p[:, x:x + nn], p[:, x:x + nn], ACT.Exp, scale=-1.0,
                            bias=ST[:, u % 4, 2 * h + q:2 * h + q + 1],
                            accum_out=ST[:, u % 4, 8 + 2 * h + q:9 + 2 * h + q]), tok["B", u, h])
                    tok["C", u, h] = t

            def D(u):
                w = unit(u)
                t = dve.do(call(dve.e.reciprocal, ST[:, u % 4, 16:16 + 2 * heads], ST[:, u % 4, 8:8 + 2 * heads]),
                           *[tok["C", u, h] for h in range(heads)])
                for h, hd in enumerate(w["heads"]):
                    p, g = Pb(u, h), hd["gate"]
                    for q, (x, nn) in enumerate(((0, n0), (n0, n1))):
                        r = ST[:, u % 4, 16 + 2 * h + q:17 + 2 * h + q]
                        if g is None:
                            f = call(dve.e.tensor_scalar, p[:, x:x + nn], p[:, x:x + nn], r, None, op0=ALU.mult)
                        else:
                            f = call(dve.e.tensor_scalar, p[:, x:x + nn], p[:, x:x + nn], g[:, q:q + 1], r, op0=ALU.mult,
                                     op1=ALU.mult)
                        t2 = dve.do(f, t)
                    tok["D", u, h] = t2

            def E(u):
                order = (0, 1, 2) if causal else (0, 2, 1, 3)
                for h in range(heads):
                    b = tbank(u, h)
                    pe.wait(*bank_free[b])
                    p = Pb(u, h)
                    for i, x in enumerate(order):
                        f = call(pe.e.transpose, PS[:, b, 128 * x:128 * x + 128],
                                                                      p[:, 128 * i:128 * i + 128], ident)
                        if i == len(order) - 1:
                            t = pe.do(f, tok["D", u, h])
                        else:
                            pe.run(f, tok["D", u, h])
                    tok["E", u, h] = t
                p_free[u % NP] = [t]

            def F(u):
                for h in range(heads):
                    b = tbank(u, h)
                    d = Tb(u, h)
                    q = act if heads == 2 or u % 2 == 0 else dve
                    w = width
                    if q is act:
                        t = act.do(call(act.e.activation, d, PS[:, b, 0:w], ACT.Copy), tok["E", u, h],
                                   *t_free[u % 2])
                    else:
                        t = dve.do(call(dve.e.tensor_copy, d, PS[:, b, 0:w]), tok["E", u, h], *t_free[u % 2])
                    bank_free[b] = [t]
                    tok["F", u, h] = t

            def G(u):
                w = unit(u)
                b = obank(w["o"])
                if w["first"]:
                    pe.wait(*bank_free[b])
                if w["extra"]:
                    w["extra"](b)
                for h in range(heads):
                    pe.wait(tok["F", u, h])
                for kb in range(2):
                    for h, hd in enumerate(w["heads"]):
                        rows = slice(0, 128) if heads == 1 else slice(64 * h, 64 * h + 64)
                        q0 = 128 if (causal and kb) else 0
                        x = 256 * kb
                        v = hd["v"][kb]
                        start = w["first"] and kb == 0
                        f = call(pe.e.matmul, 
                            PS[rows, b, q0:256], v, Tb(u, h)[:, x:x + 256 - q0], start=start,
                            stop=w["last"] and kb == 1, skip_group_check=True)
                        t = pe.do(f)
                t_free[u % 2] = [t]
                if w["last"]:
                    finished.append((w["o"], b, t))

            finished = []

            def end_units():
                while finished:
                    finish(*finished.pop(0))

            for s in range(n + 3):
                if 0 <= s - 1 < n:
                    C(s - 1)
                if 0 <= s - 2 < n:
                    D(s - 2)
                if s < n:
                    A(s)
                    B(s)
                end_units()
                fill(s, 0)
                if 0 <= s - 2 < n:
                    E(s - 2)
                fill(s, 1)
                if 0 <= s - 2 < n:
                    F(s - 2)
                if 0 <= s - 3 < n:
                    G(s - 3)
                fill(s, 2)
            end_units()

        def o_split(base=0):
            def finish(j, b, t):
                o = PS[:, b, 0:256]
                bank_free[b] = [split_into(1, base + j, o, [t])]
            return finish

        def nsa(j):
            ctr = [0]

            def alloc(n):
                ctr[0] += n
                return ctr[0] - n
            q_at, ks_at, kw_at = alloc(2048), alloc(1024), alloc(1024)
            kc_at, v_at, gate_at = alloc(64), alloc(1024), alloc(192)
            hid_at, hk_at, hv_at, vc_at = alloc(256), alloc(128), alloc(256), alloc(512)
            pc_at, pp_at, pct_at = alloc(512), alloc(1024), alloc(1024)
            tmp_at = alloc(128)
            un_at = alloc(3840)
            c_at, blk_at = un_at, un_at + 1024
            P_at, PT_at = un_at, un_at + 2304
            assert ctr[0] <= NSCR, ctr
            Q = SCR[:, q_at:q_at + 2048].rearrange("p (j t) -> p j t", j=8)
            KZ = [SCR[:, x:x + 1024].rearrange("p (g t) -> p g t", g=4) for x in (ks_at, kw_at)]
            KC = SCR[:, kc_at:kc_at + 64].rearrange("p (g c) -> p g c", g=4)
            V = SCR[:, v_at:v_at + 1024].rearrange("p (b t d) -> p b t d", b=2, t=2)
            GA = SCR[:, gate_at:gate_at + 96].rearrange("p (t c) -> p t c", t=2)
            GB = SCR[:, gate_at + 96:gate_at + 192].rearrange("p (t c) -> p t c", t=2)
            C = SCR[:, c_at:c_at + 1024].rearrange("p (i t) -> p i t", i=4)
            BLK = SCR[:, blk_at:blk_at + 1920].rearrange("p (v i g c) -> p v i g c", v=2, i=16, g=4)
            HID = SCR[:, hid_at:hid_at + 256]
            HK = SCR[:, hk_at:hk_at + 128].rearrange("p (k g c) -> p k g c", k=2, g=4)
            HV = SCR[:, hv_at:hv_at + 256].rearrange("p (k g c) -> p k g c", k=2, g=4)
            VC = SCR[:, vc_at:vc_at + 512].rearrange("p (n c) -> p n c", n=4)
            PC = SCR[:, pc_at:pc_at + 512].rearrange("p (n c) -> p n c", n=32)
            PP = SCR[:, pp_at:pp_at + 1024].rearrange("p (n c) -> p n c", n=32)
            PCT = SCR[:, pct_at:pct_at + 1024].rearrange("p (n t) -> p n t", n=4)
            TMP = SCR[:, tmp_at:tmp_at + 128]

            prior = lasts()
            tz = None
            for ap in (SCR[64:128, ks_at:ks_at + 2048].rearrange("p (g t) -> p g t", g=8)[:, 0::2, :],
                       SCR[0:64, ks_at:ks_at + 2048].rearrange("p (g t) -> p g t", g=8)[:, 1::2, :],
                       SCR[:, kc_at:kc_at + 64], SCR[:, hid_at:hid_at + 256 + 128 + 256 + 512],
                       SCR[:, pp_at:pp_at + 1024]):
                tz = pool.do(call(pool.e.memset, ap, 0.0), pool.last, *prior)

            c_tok = [None] * 4
            ts = group(0, range(8), (0, 1, 2, 3), x_tok[0])
            constants()
            rb, t_rb = rstd_bcast(7)
            refill(3)
            for i in range(4):
                c_tok[i] = dve.do(call(dve.e.tensor_tensor, C[:, i, :], PS[:, i, 0:256], rb, ALU.mult), ts[i], t_rb, *prior)
                bank_free[i] = [c_tok[i]]
                refill(1)
            blk_tok = {}
            for v in range(2):
                eng = pool if v else dve
                for g in range(4):
                    rows = slice(64 * (g % 2), 64 * (g % 2) + 64)
                    for jj in range(2):
                        full = C[rows, 2 * v + g // 2, 0:256].rearrange("p (c i) -> p i c", i=16)
                        for half in range(2):
                            s2 = full[:, jj::2, half:half + 15]
                            pos = PRM[rows, PAT["cmp_pos"] + 64 * j + 32 * v + 16 * jj + 8 * half:
                                      PAT["cmp_pos"] + 64 * j + 32 * v + 16 * jj + 8 * half + 8]
                            pos = pos.unsqueeze(2).broadcast_to([64, 8, 15])
                            dst = BLK[64 * jj:64 * jj + 64, v, 8 * half:8 * half + 8, g, :]
                            blk_tok[v] = eng.do(call(eng.e.tensor_tensor, dst, s2, pos, ALU.add),
                                                c_tok[2 * v + g // 2], *([pool.last] if v else []), *prior)
            k_tok = {}
            for i in range(4):
                b = (4, 5, 0, 1)[i]
                pe.wait(*bank_free[b])
                t = mtile(0, range(8), PS[:, b, 0:256], x_tok[0])
                br, gg = i // 2, 2 * (i % 2)
                for hh in range(2):
                    rows = slice(64 * hh, 64 * hh + 64)
                    k_tok[br, gg + hh] = dve.do(call(dve.e.tensor_tensor, KZ[br][rows, gg + hh, :], PS[rows, b, 0:256],
                                                     rb[rows, :], ALU.mult), t, tz)
                bank_free[b] = [k_tok[br, gg + 1]]
                if i == 0:
                    t_rc = cols_of_rb(7, rb, t_rb)
                refill()
            q_tok = [None] * 8

            def query(i, b):
                pe.wait(*bank_free[b])
                o = PS[:, b, 0:256]
                t = mtile(0, range(8), o, x_tok[0])
                fill_in()
                q_tok[i] = dve.do(call(dve.e.scalar_tensor_tensor, Q[:, i, :], o, 0.125, rb, ALU.mult, ALU.mult), t)
                bank_free[b] = [q_tok[i]]
                refill()
                return t

            query(0, 2)
            pe.wait(blk_tok[0], blk_tok[1], *bank_free[6])
            for n in range(8):
                u, w, loaded = next_raw()
                w = w.rearrange("p (i v c) -> p i v c", i=2, v=2)
                pe.wait(loaded)
                for ii in range(2):
                    for v in range(2):
                        i = 2 * n + ii
                        l = BLK[:, v, i, :, :].rearrange("p g c -> p (g c)")
                        t = pe.do(call(pe.e.matmul, PS[64 * v:64 * v + 60, 6, 0:256], l, w[:, ii, v, :], start=i == 0,
                                       stop=i == 15, skip_group_check=True))
                give_back(u, [t])
            for v in range(2):
                ht = act.do(call(act.e.activation, HID[64 * v:64 * v + 60, :], PS[64 * v:64 * v + 60, 6, 0:256],
                                 ACT.Gelu_apprx_tanh), t, tz)
            bank_free[6] = [ht]
            query(1, 3)
            for x in range(2):
                t2 = pe.do(call(pe.e.transpose, PS[:, 6, 128 * x:128 * x + 128], HID[:, 128 * x:128 * x + 128], ident),
                           ht, *bank_free[6])
            src = PS[:, 6, 0:256].rearrange("p (k n) -> p k n", k=2)
            t3 = dve.do(call(dve.e.tensor_copy, HK[:, :, :, 0:15],
                             src[:, :, 0:60].rearrange("p k (g c) -> p k g c", g=4)), t2, tz)
            t4 = dve.do(call(dve.e.tensor_copy, HV[:, :, :, 0:15],
                             src[:, :, 64:124].rearrange("p k (g c) -> p k g c", g=4)), t2)
            bank_free[6] = [t4]
            query(2, 4)
            w2 = lambda v, k: prm("cmp_w2", 256 * j + 128 * v + 64 * k, 64)
            pe.wait(t4, *bank_free[6], *bank_free[7])
            for hh in range(2):
                for k in range(2):
                    t5 = pe.do(call(pe.e.matmul, PS[64 * hh:64 * hh + 64, 6, 0:64], w2(0, k),
                                    HK[:, k, :, :].rearrange("p g c -> p (g c)"), start=k == 0, stop=k == 1,
                                    skip_group_check=True))
            for k in range(2):
                t6 = pe.do(call(pe.e.matmul, PS[:, 7, 0:64], HV[:, k, :, :].rearrange("p g c -> p (g c)"), w2(1, k),
                                start=k == 0, stop=k == 1))
            kc = PS[:, 6, 0:64].rearrange("p (g c) -> p g c", g=4)
            for hh in range(2):
                rows = slice(64 * hh, 64 * hh + 64)
                t_kc = dve.do(call(dve.e.tensor_copy, KC[rows, hh::2, 0:15], kc[rows, hh::2, 0:15]), t5, tz)
            bank_free[6] = [t_kc]
            for pg in range(2):
                for aa in range(2):
                    for hh in range(2):
                        g, d0 = 2 * pg + hh, 64 * aa + 32 * hh
                        t_vc = act.do(call(act.e.activation, VC[d0:d0 + 32, 2 * pg + aa, 64 * hh:64 * hh + 64],
                                           PS[32 * g:32 * g + 32, 7, 0:64], ACT.Copy), t6, tz)
            bank_free[7] = [t_vc]
            query(3, 5)
            t_pct = [None] * 2

            def compressed(pg, b):
                tmp = TMP[:, 64 * pg:64 * pg + 64]
                pe.wait(*bank_free[b], t_kc)
                for tt in range(2):
                    for i in range(4):
                        pr = 4 * pg + i
                        r = KC[:, 2 * pg:2 * pg + 2, :].rearrange("p g c -> p (g c)")
                        x = 128 * tt + 32 * i
                        t = pe.do(call(pe.e.matmul, PS[:, b, x:x + 32], Q[:, pr, 128 * tt:128 * tt + 128], r, start=True,
                                       stop=True, skip_group_check=True), q_tok[pr])
                yield
                sc = PS[:, b, 0:256].rearrange("p (t n c) -> p t n c", t=2, n=8)
                p4 = PC[:, 16 * pg:16 * pg + 16, :].rearrange("p (t n) c -> p t n c", t=2)
                pc = PC[:, 16 * pg:16 * pg + 16, :]
                cm = cst("cmask", 32).rearrange("p (t c) -> p t c", t=2).unsqueeze(2).broadcast_to([128, 2, 8, 16])
                mx, sm = tmp[:, 0:16], tmp[:, 16:32]
                bc = lambda ap: ap.unsqueeze(2).broadcast_to([128, 16, 16])
                t2 = dve.do(call(dve.e.tensor_tensor, p4, sc, cm, ALU.add), t, *prior)
                bank_free[b] = [t2]
                t2 = chain(dve, t2, call(dve.e.tensor_reduce, mx, pc, AX.X, ALU.max),
                           call(dve.e.tensor_scalar, mx, mx, -1e29, None, op0=ALU.max),
                           call(dve.e.tensor_tensor, pc, pc, bc(mx), ALU.subtract))
                t3 = act.do(call(act.e.activation, pc, pc, ACT.Exp), t2)
                yield
                t3 = chain(dve, t3, call(dve.e.tensor_reduce, sm, pc, AX.X, ALU.add),
                           call(dve.e.tensor_scalar, sm, sm, 1e-30, None, op0=ALU.max),
                           call(dve.e.reciprocal, mx, sm))
                for tt in range(2):
                    m4 = tmp[:, 8 * tt:8 * tt + 8].rearrange("p (r h) -> p r h", r=4)
                    g4 = GA[:, tt, 8 * pg:8 * pg + 8].rearrange("p (h r) -> p r h", h=2)
                    t4 = dve.do(call(dve.e.tensor_tensor, m4, m4, g4, ALU.mult), t3, t_g)
                t_pp = dve.do(call(dve.e.tensor_tensor, PP[:, 16 * pg:16 * pg + 16, 0:16], pc, bc(mx), ALU.mult), t4, tz)
                yield
                pe.wait(*bank_free[b])
                for cc in range(2):
                    for tt in range(2):
                        n = 16 * pg + 8 * tt + 4 * cc
                        src = PP[:, n:n + 4, :].rearrange("p n c -> p (n c)")
                        t = pe.do(call(pe.e.transpose, PS[:, b, 256 * cc + 128 * tt:256 * cc + 128 * tt + 128], src, ident),
                                  t_pp)
                yield
                dst = PCT[:, 2 * pg:2 * pg + 2, :].rearrange("p n t -> p (n t)")
                t_pct[pg] = act.do(call(act.e.activation, dst, PS[:, b, :], ACT.Copy), t, *prior)
                bank_free[b] = [t_pct[pg]]
                yield

            for br, (cols, per) in enumerate(((304, 3), (256, 4))):
                bb = (0, 1) if br == 0 else (2, 3)
                pe.wait(*bank_free[bb[0]], *bank_free[bb[1]])
                t = vtile(0, range(8), cols, per, bb, x_tok[0])
                for tt in range(2):
                    if br == 0:
                        tg = act.do(call(act.e.activation, GB[:, tt, :], PS[:, bb[tt], 256:304], ACT.Copy,
                                         scale=RC[:, 0, tt:tt + 1]), t, t_rc, *prior)
                    v_tok = act.do(call(act.e.activation, V[:, br, tt, :], PS[:, bb[tt], 0:256], ACT.Copy,
                                        scale=RC[:, 0, tt:tt + 1]), t, t_rc, *prior)
                    bank_free[bb[tt]] = [v_tok]
                if br == 0:
                    t1 = act.do(call(act.e.activation, GB[:, :, :], GB[:, :, :], ACT.Exp, scale=-1.0), tg)
                    t1 = dve.do(call(dve.e.tensor_scalar, GB[:, :, :], GB[:, :, :], 1.0, None, op0=ALU.add), t1)
                    t_g = dve.do(call(dve.e.reciprocal, GA[:, :, :], GB[:, :, :]), t1)
                refill()
            out, later = [], []

            def fill(s, i):
                if i == 0 and s == 0:
                    later.append(compressed(0, 7))
                if i == 1 and s < 4 or i == 0 and s == 4:
                    next(later[0])
                if i == 0 and s < 8 and s % 2 == 0:
                    t = query(4 + s // 2, 3)
                    if s == 6:
                        done_with(0, t)
                if i == 0 and s == 7:
                    later.append(compressed(1, 3))
                if i == 1 and 7 <= s < 12:
                    next(later[1])
                if i == 2 and s == 15:
                    out.append(out_begin(range(8), (0, 1)))
                if s >= 16:
                    for _ in range(((2, 1, 2), (1, 0, 0), (1, 0, 0))[s - 16][i]):
                        next(out[0]["steps"])

            def unit(u):
                pr, br = u // 2, u % 2
                pg, r = pr // 4, pr % 4

                def extra(b):
                    l, rr = VC[:, 2 * pg + pr % 2, :], PCT[:, pr // 2, :]
                    pe.run(call(pe.e.matmul, PS[:, b, 0:256], l, rr, start=False, stop=False, skip_group_check=True),
                           t_pct[pg], t_vc)
                heads = []
                for h in range(2):
                    g = 2 * pg + h
                    col = 16 * (1 + br) + 4 * g + r
                    heads.append(dict(
                        score=[(0, 128, Q[:, pr, 0:128], KZ[br][:, g, 0:128], True, True),
                               (128, 256, Q[:, pr, 128:256], KZ[br][:, g, :], True, True)],
                        wait=(q_tok[pr], k_tok[br, g]), scale=None, gate=GA[:, :, col],
                        v=[V[:, br, kb, 64 * g:64 * g + 64] for kb in range(2)]))
                return dict(heads=heads, o=pr, first=br == 0, last=br == 1, extra=extra if br == 1 else None)
            pe.wait(v_tok)
            dve.wait(t_g)
            attention(16, unit, P_at, PT_at, 384, o_split(), sb=(0, 1, 2), fill=fill)
            return out[0], (2, 3, 4, 5)

        def moba():
            Q = SCR[:, 0:2048].rearrange("p (j t) -> p j t", j=8)
            KZ = SCR[:, 2048:6144].rearrange("p (h t) -> p h t", h=16)
            V = SCR[:, 6144:8192].rearrange("p (t c) -> p t c", t=2)
            prior = lasts()
            for ap in (KZ[64:128, 0::2, :], KZ[0:64, 1::2, :]):
                tz = pool.do(call(pool.e.memset, ap, 0.0), pool.last, *prior)
            q_tok, k_tok = [None] * 8, [None] * 16
            vts, steps = vtiles(0, range(8), (0, 2))
            next(steps)
            refill()
            next(steps)
            rb, t_rb = rstd_bcast(7)
            refill()
            next(steps)
            refill()
            next(steps)
            t_rc = cols_of_rb(6, rb, t_rb)
            refill()

            def proj(j, kind):
                b = kind if j else 4 + kind
                pe.wait(*bank_free[b])
                o = PS[:, b, 0:256]
                t = mtile(0, range(8), o, x_tok[0])
                fill_in()
                if kind == 0:
                    q_tok[j] = dve.do(call(dve.e.scalar_tensor_tensor, Q[:, j, :], o, 0.125, rb, ALU.mult, ALU.mult), t,
                                      t_rb, *prior)
                    bank_free[b] = [q_tok[j]]
                else:
                    for hh in range(2):
                        rows = slice(64 * hh, 64 * hh + 64)
                        k_tok[2 * j + hh] = dve.do(call(dve.e.tensor_tensor, KZ[rows, 2 * j + hh, :], PS[rows, b, 0:256],
                                                        rb[rows, :], ALU.mult), t, tz)
                    bank_free[b] = [k_tok[2 * j + 1]]
                    if j == 7:
                        done_with(0, t)
                refill()
            for n in range(2):
                for tt in range(2):
                    b = 2 * n + tt
                    v_tok = act.do(call(act.e.activation, V[:, tt, 512 * n:512 * n + 512], PS[:, b, :], ACT.Copy,
                                        scale=RC[:, 0, tt:tt + 1]), vts[n], t_rc, *prior)
                    bank_free[b] = [v_tok]
            proj(0, 0)
            proj(0, 1)
            out = []

            def fill(s, i):
                if s < 7 and i < 2:
                    proj(s + 1, i)
                if s == 7 and i == 2:
                    out.append(out_begin(range(8), (0, 1)))
                if s >= 8:
                    for _ in range(((2, 1, 1), (1, 1, 0), (1, 0, 0))[s - 8][i]):
                        next(out[0]["steps"])

            def unit(u):
                heads = [dict(score=[(0, 128, Q[:, u, 0:128], KZ[:, 2 * u + h, 0:128], True, True),
                                     (128, 256, Q[:, u, 128:256], KZ[:, 2 * u + h, :], True, True)],
                              wait=(q_tok[u], k_tok[2 * u + h]), scale=None, gate=None,
                              v=[V[:, kb, 128 * u + 64 * h:128 * u + 64 * h + 64] for kb in range(2)]) for h in range(2)]
                return dict(heads=heads, o=u, first=True, last=True, extra=None)
            attention(8, unit, 8192, 8192 + 2304, 384, o_split(), fill=fill)
            return out[0], (4, 5, 6, 7)

        def conv():
            prior = lasts()
            R2 = SCR[:, 0:256]
            Z = [SCR[:, 256 + 258 * i:256 + 258 * (i + 1)] for i in range(2)]
            Y = [SCR[:, 1024 + 256 * i:1280 + 256 * i] for i in range(2)]
            CC = [SCR[:, 1536 + 256 * i:1792 + 256 * i] for i in range(2)]
            for i in range(2):
                tz = pool.do(call(pool.e.memset, Z[i][:, 0:2], 0.0), pool.last, *prior)
            for d in range(8):
                s = d % 2
                bs = [3 * (d % 2) + i for i in range(3)]
                if d == 0:
                    ts = group(0, range(8), bs, x_tok[0])
                    rb, t_rb = rstd_bcast(7)
                    t_r2 = dve.do(call(dve.e.tensor_tensor, R2, rb, rb, ALU.mult), t_rb, *prior)
                    refill()
                else:
                    ts = []
                    for b in bs:
                        pe.wait(*bank_free[b])
                        ts.append(mtile(0, range(8), PS[:, b, 0:256], x_tok[0]))
                        refill(1)
                if d == 7:
                    out = [out_begin(range(8), (6, 7))]
                    for _ in range(6):
                        next(out[0]["steps"])
                c_, u_, b_ = (PS[:, x, 0:256] for x in bs)
                w = lambda i: prm("conv_w", 3 * d + i)
                z, y, cc = Z[s], Y[s], CC[s]
                t = dve.do(call(dve.e.tensor_tensor, cc, c_, R2, ALU.mult), ts[0], t_r2, dve.last)
                bank_free[bs[0]] = [t]
                t = dve.do(call(dve.e.tensor_tensor, z[:, 2:258], u_, cc, ALU.mult), ts[1], t, tz)
                bank_free[bs[1]] = [t]
                t = dve.do(call(dve.e.tensor_scalar, y, z[:, 0:256], w(0), None, op0=ALU.mult), t)
                t = dve.do(call(dve.e.scalar_tensor_tensor, y, z[:, 1:257], w(1), y, ALU.mult, ALU.add), t)
                t = dve.do(call(dve.e.scalar_tensor_tensor, y, z[:, 2:258], w(2), y, ALU.mult, ALU.add), t)
                t = dve.do(call(dve.e.tensor_tensor, y, y, rb, ALU.mult), t)
                t = dve.do(call(dve.e.tensor_tensor, y, b_, y, ALU.mult), t, ts[2])
                bank_free[bs[2]] = [t]
                if d == 7:
                    done_with(0, ts[2])
                split_into(1, d, y, [t])
                refill()
            return out[0], (0, 1, 2, 3)

        MEMK = SCR[:, 11776:12800].rearrange("p (h t) -> p h t", h=4)
        MEMV = SCR[:, 12800:13824].rearrange("p (t c) -> p t c", t=2)

        def chain(q, t, *ops):
            for op in ops:
                t = q.do(op, t)
            return t

        def inv_sqrt(y, x, t, tmp):
            y0 = tmp[0]
            t = act.do(call(act.e.activation, y0, x, ACT.Abs_reciprocal_sqrt), t)
            return newton(y, y0, x, t, tmp[1])

        def small(at, *shape):
            n = int(np.prod(shape))
            ap = SM[:, at:at + n]
            if len(shape) == 2:
                ap = ap.rearrange("p (a b) -> p a b", a=shape[0])
            return ap

        def squares(dst, src, junk, *tokens):
            return act.do(call(act.e.activation, junk, src, ACT.Square, accum_out=dst), *tokens)

        MT = SCR[:, 8192:10240].rearrange("p (k t) -> p k t", k=8)
        ld = {n: [sem(f"s_{n}"), 0] for n in ("memT", "a_ln", "a_ws", "a_bs")}
        mem = {}

        def load_mem():
            prior = lasts()
            mem["x"] = sp.dma(SCR[:, 8192:10240], a["memT"], ld["memT"], *prior)
            mem["ln"] = sp.dma(SCR[:, 4096:6144], a["a_ln"], ld["a_ln"])
            mem["ws"] = sp.dma(SCR[:, 6144:7168], a["a_ws"], ld["a_ws"])
            mem["bs"] = sp.dma(SCR[:, 7168:8192], a["a_bs"], ld["a_bs"])

        def mem_hook(f):
            k = f - 3
            if 0 <= k < 8:
                split_into(1, k, MT[:, k, :], [mem["x"]], prm("mem_norm", k))
                square_into(k, MT[:, k, :], [mem["x"]])
            if k == 8:
                b = next_bank((0, 1, 2, 3))
                mem["rc"] = rstd_cols(b, RC[:, 1, :])
            if f == 14:
                ws = SCR[:, 6144:7168].rearrange("p (g t) -> p g t", g=8)
                mem["ws"] = pool.do(call(pool.e.affine_select, ws, ws, [[0, 8], [1, 128]], ALU.is_ge, 0.0, base=0,
                                         channel_multiplier=-1), mem["ws"], pool.last)

        def mem_kv():
            prior = lasts()
            kv, steps = vtiles(1, range(8), (0, 2))
            next(steps)
            rb, t_rb = rstd_bcast(7)
            refill()
            next(steps)
            for k in range(8):
                h_tok[k] = dve.do(call(dve.e.scalar_tensor_tensor, H[:, k, :], H[:, k, :], prm("norm_final", k), rb,
                                       ALU.mult, ALU.mult), t_rb, h_tok[k])
                new_h(k, prm("norm1", k))
                refill(1)
            for _ in steps:
                refill(1)
            done_with(1, kv[1])
            for tt in range(2):
                t = act.do(call(act.e.activation, MEMV[:, tt, :], PS[:, 2 + tt, :], ACT.Copy, scale=RC[:, 1, tt:tt + 1]),
                           kv[1], mem["rc"], *prior)
                bank_free[2 + tt] = [t]
            mem["v"] = t
            KM = SCR[:, 2048:3072].rearrange("p (t c) -> p t c", t=2)
            JK = SCR[:, 3072:3200]
            ss, m2, y, t0, t1 = small(0, 2, 4), small(8, 2), small(10, 2, 4), small(18, 8), small(26, 8)
            for tt in range(2):
                for h in range(4):
                    t = squares(ss[:, tt, h:h + 1], PS[:, tt, 128 * h:128 * h + 128], JK, kv[0], act.last, *prior)
            m2b = m2.unsqueeze(2).broadcast_to([128, 2, 4])
            x = small(34, 2, 4)
            t = chain(dve, t, call(dve.e.tensor_tensor, m2, RC[:, 1, :], RC[:, 1, :], ALU.mult),
                      call(dve.e.tensor_tensor, x, ss, m2b, ALU.mult),
                      call(dve.e.tensor_scalar, x, x, 1.0 / 128, 1e-6, op0=ALU.mult, op1=ALU.add))
            t = inv_sqrt(small(10, 8), small(34, 8), t, (t0, t1))
            rb_ = RC[:, 1, :].unsqueeze(2).broadcast_to([128, 2, 4])
            t = dve.do(call(dve.e.tensor_tensor, y, y, rb_, ALU.mult), t)
            for tt in range(2):
                for h in range(4):
                    tk = dve.do(call(dve.e.tensor_scalar, KM[:, tt, 128 * h:128 * h + 128],
                                     PS[:, tt, 128 * h:128 * h + 128], y[:, tt, h:h + 1], None, op0=ALU.mult), t)
            bank_free[0] = bank_free[1] = [tk]
            return KM, tk

        def to_features(src, heads, dst, banks, tokens, gain=None, free=(), act_too=True):
            out_t = []
            for h in range(heads):
                b = banks[(h // 2) % len(banks)]
                if h % 2 == 0:
                    pe.wait(*bank_free[b])
                for tt in range(2):
                    t = pe.do(call(pe.e.transpose, PS[:, b, 256 * (h % 2) + 128 * tt:256 * (h % 2) + 128 * tt + 128],
                                   src[:, tt, 128 * h:128 * h + 128], ident), *tokens)
                if h % 2:
                    d = dst[:, h - 1:h + 1, :].rearrange("p h t -> p (h t)")
                    if (h // 2) % 2 and act_too:
                        t = act.do(call(act.e.activation, d, PS[:, b, :], ACT.Copy, scale=1.0 if gain is None else gain),
                                   t, *free)
                    else:
                        t = dve.do(call(dve.e.tensor_scalar, d, PS[:, b, :], 1.0 if gain is None else gain, None,
                                        op0=ALU.mult), t, *free)
                    bank_free[b] = [t]
                    out_t.append(t)
            return out_t

        def query_scales(ss, dst, n, c, mean, tokens, at):
            c2 = small(at, 2)
            x = small(at + 2, 2, n)
            xf, y0, tmp = small(at + 2, 2 * n), small(at + 2 + 2 * n, 2 * n), small(at + 2 + 4 * n, 2 * n)
            wide = lambda ap: ap.unsqueeze(2).broadcast_to([128, 2, n])
            t = dve.do(call(dve.e.tensor_tensor, c2, c, c, ALU.mult), *tokens)
            t = chain(dve, t, call(dve.e.tensor_tensor, x, ss, wide(c2), ALU.mult),
                      call(dve.e.tensor_scalar, xf, xf, 1.0 / mean, 1e-6, op0=ALU.mult, op1=ALU.add))
            t = inv_sqrt(xf, xf, t, (y0, tmp))
            t = dve.do(call(dve.e.tensor_scalar, xf, xf, -float(mean) ** -0.5, None, op0=ALU.mult), t)
            return dve.do(call(dve.e.tensor_tensor, dst, x, wide(c), ALU.mult), t)

        def mem_queries(i, banks, vt, QM, QT, tbanks, free):
            g = small(318, 1)
            tg = dve.do(call(dve.e.tensor_tensor, g, prm("mem_qn", i), prm("mem_kn", i), ALU.mult), *free)
            ta = act.do(call(act.e.activation, QM[:, 0, :], PS[:, banks[0], :], ACT.Copy), vt, *free)
            td = dve.do(call(dve.e.tensor_copy, QM[:, 1, :], PS[:, banks[1], :]), vt)
            bank_free[banks[0]], bank_free[banks[1]] = [ta], [td]

            def turned():
                return to_features(QM, 4, QT, tbanks, [ta, td, tg], gain=g)
            return [ta, td], turned

        def mem_scales(QM, JK, tokens, r, t_r, at):
            ss, ns = small(at, 2, 4), small(at + 8, 2, 4)
            for tt in range(2):
                for h in range(4):
                    ts = squares(ss[:, tt, h:h + 1], QM[:, tt, 128 * h:128 * h + 128], JK[:, 0:128], act.last, *tokens)
            return ns, query_scales(ss, ns, 4, r, 128, [ts, t_r], at + 18)

        def mem_attention(QT, tq, ns, tn, P_at, PT_at, fill, **banks):
            def unit(u):
                return dict(heads=[dict(
                    score=[(0, 256, QT[:, u, 0:128], MEMK[:, u, :], True, True),
                           (256, 256, QT[:, u, 128:256], MEMK[:, u, :], True, True)],
                    wait=(*tq, *mem["k"]), scale=(ns[:, 0, u:u + 1], ns[:, 1, u:u + 1]), gate=None,
                    v=[MEMV[:, kb, 128 * u:128 * u + 128] for kb in range(2)])], o=u, first=True, last=True, extra=None)
            pe.wait(mem["v"])
            dve.wait(tn)
            attention(4, unit, P_at, PT_at, 512, o_split(8), causal=False, fill=fill, **banks)

        MEM_FIRST = (8, 9, 10, 11, 0, 1, 2, 3, 4, 5, 6, 7)

        def gmlp(KM, t_km):
            VV = SCR[:, 0:2048].rearrange("p (t c) -> p t c", t=2)
            U = SCR[:, 2048:4096].rearrange("p (k t) -> p k t", k=8)
            LNG, LNB = SCR[:, 4096:5120], SCR[:, 5120:6144]
            WS = SCR[:, 6144:7168].rearrange("p (g t) -> p g t", g=8)
            BS = SCR[:, 7168:8192].rearrange("p (g t) -> p g t", g=8)
            QM = SCR[:, 8192:9216].rearrange("p (t c) -> p t c", t=2)
            QT = SCR[:, 9216:10240].rearrange("p (h t) -> p h t", h=4)
            JK = SCR[:, 10240:10752]
            prior = lasts()
            vs, steps = vtiles(0, range(8), (4, 6))
            next(steps)
            refill()
            rb, t_rb = rstd_bcast(2)
            next(steps)
            refill()
            next(steps)
            mem["k"] = to_features(KM, 4, MEMK, (0, 1), [t_km], free=prior)
            refill()
            next(steps)
            t_rc = cols_of_rb(3, rb, t_rb)
            refill()
            for n in range(2):
                for tt in range(2):
                    b = 4 + 2 * n + tt
                    tv = act.do(call(act.e.activation, VV[:, tt, 512 * n:512 * n + 512], PS[:, b, :], ACT.Gelu,
                                     scale=RC[:, 0, tt:tt + 1]), vs[n], t_rc, *prior)
                    bank_free[b] = [tv]
            refill()
            pe.wait(*bank_free[0], *bank_free[1])
            vt = vtile(0, range(8), 512, 2, (0, 1), x_tok[0])
            t_vn = []

            def layer_norm(tt):
                s6, mv = small(64 + 16 * tt, 12), small(76 + 16 * tt, 2)
                for n in range(2):
                    t = dve.do(call(dve.e.bn_stats, s6[:, 6 * n:6 * n + 6], VV[:, tt, 512 * n:512 * n + 512]), tv)
                t = dve.do(call(dve.e.bn_aggr, mv, s6), t)
                x, y0, tmp = small(96 + 4 * tt, 1), small(97 + 4 * tt, 1), small(98 + 4 * tt, 1)
                t = dve.do(call(dve.e.tensor_scalar, x, mv[:, 1:2], 1e-6, None, op0=ALU.add), t)
                fill_in()
                t = inv_sqrt(x, x, t, (y0, tmp))
                v = VV[:, tt, :]
                dve.wait(mem["ln"])
                t_vn.append(chain(dve, t,
                                  call(dve.e.tensor_scalar, v, v, mv[:, 0:1], x, op0=ALU.subtract, op1=ALU.mult),
                                  call(dve.e.tensor_tensor, v, v, LNG, ALU.mult),
                                  call(dve.e.tensor_tensor, v, v, LNB, ALU.add)))
            layer_norm(0)
            refill(1)
            tq, turned = mem_queries(0, (0, 1), vt, QM, QT, (0, 1), prior)
            tu = [None] * 8

            def u_tile(k):
                b = 2 + k % 2
                pe.wait(*bank_free[b])
                t = mtile(0, range(8), PS[:, b, 0:256], x_tok[0])
                fill_in()
                tu[k] = dve.do(call(dve.e.tensor_tensor, U[:, k, :], PS[:, b, 0:256], rb, ALU.mult), t, t_rb, *mem["k"])
                bank_free[b] = [tu[k]]
                if k == 7:
                    done_with(0, t)
                refill()
            u_tile(0)
            tqt = turned()
            u_tile(1)
            ns, tn = mem_scales(QM, JK, [*tq, *prior], RC[:, 0, :], t_rc, 0)
            layer_norm(1)

            def fill(s, i):
                if i == 0 and s < 6:
                    u_tile(2 + s)
            mem_attention(QT, tqt, ns, tn, 4096, 10752, fill, sb=(0, 1), tb=(4, 5), ob=(6, 7))
            for k in range(8):
                tu[k] = act.do(call(act.e.activation, U[:, k, :], U[:, k, :], ACT.Gelu), tu[k])
            first = out_begin(MEM_FIRST, (2, 3))
            pe.wait(mem["ws"])
            dve.wait(mem["bs"])

            def mix(gi):
                b = gi % 2
                pe.wait(*bank_free[b])
                for n in range(2):
                    t = pe.do(call(pe.e.matmul, PS[:, b, 128 * n:128 * n + 128], VV[:, n, 128 * gi:128 * gi + 128],
                                   WS[:, gi, :], start=True, stop=True, skip_group_check=True), t_vn[n])
                tmp = SCR[:, 8192 + 256 * (gi % 4):8448 + 256 * (gi % 4)]
                tmp3 = tmp.rearrange("p (n t) -> p n t", n=2)
                bs = BS[:, gi, :].unsqueeze(1).broadcast_to([128, 2, 128])
                t = dve.do(call(dve.e.tensor_tensor, tmp3, PS[:, b, 0:256].rearrange("p (n t) -> p n t", n=2), bs,
                                ALU.add), t, *([x_tok[1][gi - 4]] if gi >= 4 else [*tqt, tn]))
                bank_free[b] = [t]
                t = dve.do(call(dve.e.tensor_tensor, tmp, tmp, U[:, gi, :], ALU.mult), t, tu[gi])
                split_into(1, gi, tmp, [t])
            mix(0)
            mix(1)
            for k in range(8):
                next(first["steps"])
                if k + 2 < 8:
                    mix(k + 2)
                if k % 2:
                    refill(1)
            return first, (4, 5, 6, 7)

        def mla():
            reclaim()
            S = lambda at, n: SCR[:, at:at + n]
            QNT = S(0, 2048).rearrange("p (h t) -> p h t", h=8)
            QRT = S(2048, 1024).rearrange("p (h t) -> p h t", h=4)
            KNT = S(3072, 2048).rearrange("p (h t) -> p h t", h=8)
            KZR = S(5120, 2048).rearrange("p (h t) -> p h t", h=8)
            VT = S(7168, 2048).rearrange("p (t c) -> p t c", t=2)
            QM = S(0, 1024).rearrange("p (t c) -> p t c", t=2)
            QT = S(1024, 1024).rearrange("p (h t) -> p h t", h=4)
            CQ = S(5632, 1024).rearrange("p (t c) -> p t c", t=2)
            CKV = S(6656, 512).rearrange("p (t c) -> p t c", t=2)
            QI = S(7168, 1024).rearrange("p (t h c) -> p t h c", t=2, h=8)
            QIf = S(7168, 1024).rearrange("p (t c) -> p t c", t=2)
            QR = S(8192, 1024).rearrange("p (t h c) -> p t h c", t=2, h=8)
            QRf = S(8192, 1024).rearrange("p (t c) -> p t c", t=2)
            QN = S(9216, 2048).rearrange("p (t c) -> p t c", t=2)
            KR = S(11264, 128).rearrange("p (t c) -> p t c", t=2)
            KRR = S(11392, 128).rearrange("p (t c) -> p t c", t=2)
            X0H, X0L = (x[:, :, :].rearrange("p k t -> p (k t)") for x in (FH0, FL0))
            KT = X0H.rearrange("p (t c) -> p t c", t=2)
            KRH = X0L[:, 0:1024].rearrange("p (t h c) -> p t h c", t=2, h=8)
            KRf = X0L[:, 0:1024].rearrange("p (t c) -> p t c", t=2)
            TAB = [FGH[:, i, :].rearrange("p (w t c) -> p w t c", w=4, t=2) for i in range(2)]
            JK = FGL[:, 0:2, :].rearrange("p k t -> p (k t)")
            prior = lasts()
            TT = lambda o, x, y, op: call(dve.e.tensor_tensor, o, x, y, op)

            zs, steps = vtiles(0, range(8), (0, 2))
            next(steps)
            refill()
            next(steps)
            r = RC[:, 0, :]
            t_rc = rstd_cols(6, r)
            refill()
            t_tab = rope_tables(TAB, prior)
            next(steps)
            refill()
            next(steps)
            refill()
            pe.wait(*bank_free[4], *bank_free[5])
            vt = vtile(0, range(8), 320, 3, (4, 5), x_tok[0])
            done_with(0, vt)
            x0_free = list(x_free[0])
            for tt in range(2):
                t_cq = dve.do(call(dve.e.tensor_copy, CQ[:, tt, :], PS[:, tt, :]), zs[0], *prior)
                bank_free[tt] = [t_cq]

            def latent(k, tokens):
                src, name, kk = (CQ, "q_norm", k) if k < 4 else (CKV, "kv_norm", k - 4)
                b = 6 + k % 2
                pe.wait(*bank_free[b])
                for tt in range(2):
                    t = pe.do(call(pe.e.transpose, PS[:, b, 128 * tt:128 * tt + 128],
                                   src[:, tt, 128 * kk:128 * kk + 128], ident), tokens)
                bank_free[b] = [split_into(1, k, PS[:, b, 0:256], [t], prm(name, kk))]
                return t
            for k in range(4):
                t_cq_read = latent(k, t_cq)
            ss1 = small(16, 2, 3)
            for tt in range(2):
                t1 = squares(ss1[:, tt, 0:1], CQ[:, tt, :], JK, t_cq, act.last, *prior)
            tq, turned = mem_queries(1, (2, 3), zs[1], QM, QT, (2, 3), prior)
            tok = {}

            def up(name, ks, banks, dst, free):
                pe.wait(*bank_free[banks[0]], *bank_free[banks[1]])
                t = vtile(1, ks, 512, 2, banks, x_tok[1])
                fill_in()
                a_ = act.do(call(act.e.activation, dst[:, 0, :], PS[:, banks[0], :], ACT.Copy), t, *free)
                d_ = dve.do(call(dve.e.tensor_copy, dst[:, 1, :], PS[:, banks[1], :]), t, *free)
                bank_free[banks[0]], bank_free[banks[1]] = [a_], [d_]
                tok[name] = [a_, d_]
                refill()
            for tt in range(2):
                dve.do(call(dve.e.tensor_copy, CKV[:, tt, :], PS[:, 4 + tt, 0:256]), vt, *prior)
                t2 = dve.do(call(dve.e.tensor_copy, KR[:, tt, :], PS[:, 4 + tt, 256:320]))
                bank_free[4 + tt] = [t2]
            up("qr", range(4), (0, 1), QIf, prior)
            latent(4, t2)
            latent(5, t2)
            for tt in range(2):
                t1 = squares(ss1[:, tt, 1:2], CKV[:, tt, :], JK[:, 0:256], t2, act.last)
                t1 = squares(ss1[:, tt, 2:3], KR[:, tt, :], JK[:, 0:64], act.last)
            tqt = turned()
            ns, tn = mem_scales(QM, JK, tq, r, t_rc, 50)
            up("k0", (4, 5), (6, 7), KT[:, :, 0:512], x0_free)
            up("k1", (4, 5), (0, 1), KT[:, :, 512:1024], x0_free)

            def rotate(q, dst, src, heads, tab, tt, scratch, tokens):
                p = [x[:, 0:heads, :] for x in scratch]
                w = [tab[:, i, tt, :].unsqueeze(1).broadcast_to([128, heads, 32]) for i in range(4)]
                x1, x2 = src[:, :, 0:32], src[:, :, 32:64]
                strict = lambda: [q.last] if q is pool else []
                for i, xx in enumerate((x1, x2, x1, x2)):
                    t = q.do(call(q.e.tensor_tensor, p[i], xx, w[i], ALU.mult), *tokens, *strict())
                q.do(call(q.e.tensor_tensor, dst[:, :, 0:32], p[0], p[1], ALU.subtract), t)
                return q.do(call(q.e.tensor_tensor, dst[:, :, 32:64], p[2], p[3], ALU.add), t, *strict())
            RT = [[X0L[:, 1024 + 256 * i:1280 + 256 * i].rearrange("p (h c) -> p h c", h=8) for i in range(4)],
                  [S(5632 + 256 * i, 256).rearrange("p (h c) -> p h c", h=8) for i in range(4)]]
            rot = [rotate(pool, QR[:, 1], QI[:, 1], 8, TAB[0], 1, RT[1], [*tok["qr"], t_tab, t_cq_read, t1])]
            r2, x, y0, tmp, c = small(24, 2), small(26, 2, 2), small(30, 4), small(34, 4), small(38, 2, 2)
            xf = small(26, 4)
            wide = lambda ap, n: ap.unsqueeze(2).broadcast_to([128, 2, n])
            one = lambda o, x, s1, o0: call(dve.e.tensor_scalar, o, x, s1, None, op0=o0)

            def latent_factors():
                t = dve.do(TT(r2, r, r, ALU.mult), t_rc, t1)
                t = chain(dve, t, TT(x, ss1[:, :, 0:2], wide(r2, 2), ALU.mult),
                          one(x[:, :, 0:1], x[:, :, 0:1], 1.0 / 512, ALU.mult),
                          one(x[:, :, 1:2], x[:, :, 1:2], 1.0 / 256, ALU.mult), one(xf, xf, 1e-6, ALU.add))
                t = inv_sqrt(xf, xf, t, (y0, tmp))
                t = dve.do(TT(c, x, wide(r, 2), ALU.mult), t)
                dve.do(call(dve.e.tensor_copy, cq.unsqueeze(2), c[:, :, 0:1]), t)
                tok["c"] = dve.do(call(dve.e.tensor_copy, ckv.unsqueeze(2), c[:, :, 1:2]), t)
            cq, ckv = small(42, 2), small(44, 2)
            ssn, ssr, ssq, ssk = small(128, 2, 8), small(144, 2, 8), small(160, 2, 8), small(176, 2, 8)
            fk, fr = small(192, 2, 8), small(208, 2, 8)
            nsq = small(224, 2, 8)

            def head_squares(name, ss, src, n, tt, hs, tokens):
                for h in hs:
                    t = squares(ss[:, tt, h:h + 1], src[:, tt, n * h:n * h + n], JK[:, 0:n], *tokens, act.last)
                tok[name] = t

            def key_factors():
                c2, kx, ky = small(240, 2), small(242, 2, 8), small(258, 2)
                kxf, k0, k1 = small(242, 16), small(260, 16), small(276, 16)
                t = dve.do(TT(c2, ckv, ckv, ALU.mult), tok["c"], tok["ssk"])
                t = chain(dve, t, TT(kx, ssk, wide(c2, 8), ALU.mult),
                          TT(ky.unsqueeze(2), ss1[:, :, 2:3], r2.unsqueeze(2), ALU.mult),
                          TT(kx, kx, wide(ky, 8), ALU.add),
                          call(dve.e.tensor_scalar, kxf, kxf, 1.0 / 192, 1e-6, op0=ALU.mult, op1=ALU.add))
                t = inv_sqrt(kxf, kxf, t, (k0, k1))
                tok["f"] = chain(dve, t, TT(fk, kx, wide(ckv, 8), ALU.mult), TT(fr, kx, wide(r, 8), ALU.mult))

            def scale_keys(tt):
                k3 = KT[:, tt, :].rearrange("p (h c) -> p h c", h=8)
                tok["kt", tt] = dve.do(TT(k3, k3, fk[:, tt, :].unsqueeze(2).broadcast_to([128, 8, 128]), ALU.mult),
                                       tok["f"], *tok["k0"], *tok["k1"])

            def key_rotary(tt):
                tr = rotate(dve, KRR[:, tt, :].unsqueeze(1), KR[:, tt, :].unsqueeze(1), 1, TAB[1], tt,
                            [y[:, 4 * tt:4 * tt + 1, :] for y in RT[0]], [t_tab, rot[-1]])
                tok["kr"] = dve.do(TT(KRH[:, tt], KRR[:, tt, :].unsqueeze(1).broadcast_to([128, 8, 64]),
                                      fr[:, tt, :].unsqueeze(2).broadcast_to([128, 8, 64]), ALU.mult), tr, tok["f"])
            v = []

            def value(n, bb):
                pe.wait(*bank_free[bb[0]], *bank_free[bb[1]])
                v.append((bb, vtile(1, (4, 5), 512, 2, bb, x_tok[1])))
                refill()

            def values(n):
                bb, t = v[n]
                for tt in range(2):
                    tok["v"] = act.do(call(act.e.activation, VT[:, tt, 512 * n:512 * n + 512], PS[:, bb[tt], :], ACT.Copy,
                                           scale=ckv[:, tt:tt + 1]), t, tok["c"], *tok["qrt"])
                    bank_free[bb[tt]] = [tok["v"]]

            def fill(s, i):
                if (s, i) == (0, 0):
                    up("qn0", range(4), (6, 7), QN[:, :, 0:512], prior)
                    rot.append(rotate(dve, QR[:, 0], QI[:, 0], 8, TAB[0], 0, RT[0], [*tok["qr"], t_tab, *x0_free]))
                if (s, i) == (1, 0):
                    up("qn1", range(4), (0, 1), QN[:, :, 512:1024], prior)
                    latent_factors()
                if s < 4 and i == 1:
                    head_squares("ssk", ssk, KT, 128, s // 2, range(4 * (s % 2), 4 * (s % 2) + 4), [*tok["k0"], *tok["k1"]])
                if (s, i) == (2, 0):
                    value(0, (6, 7))
                    tok["qrt"] = to_features(QRf, 4, QRT, (0, 1), rot, free=prior)
                if (s, i) == (3, 0):
                    value(1, (0, 1))
                    values(0)
                if (s, i) == (4, 0):
                    key_factors()
                    values(1)
                    scale_keys(0)
                if (s, i) == (4, 2):
                    scale_keys(1)
                if (s, i) == (5, 0):
                    key_rotary(0)
                if (s, i) == (5, 2):
                    key_rotary(1)
                if s < 2 and i == 2:
                    head_squares("ssr", ssr, QIf, 64, s, range(8), tok["qr"])
            mem_attention(QT, tqt, ns, tn, 3072, 4608, fill, sb=(2, 3), tb=(4,), ob=(5,))
            x_free[1] = [v[1][1]]
            done = [pe.last, act.last, dve.last]
            for ap in (KZR[64:128, 0::2, :], KZR[0:64, 1::2, :]):
                t_z = pool.do(call(pool.e.memset, ap, 0.0), pool.last, *done)
            gp = small(46, 1)
            t_gp = dve.do(TT(gp, prm("qn_nope"), prm("kn_nope"), ALU.mult), *prior)
            t_knt = to_features(KT, 8, KNT, (0, 1), [tok["kt", 0], tok["kt", 1]], free=done)
            first = out_begin(MEM_FIRST, (2, 3))
            next(first["steps"])
            next(first["steps"])
            t_qn = to_features(QN, 8, QNT, (6, 7), [*tok["qn0"], *tok["qn1"], t_gp], gain=gp, free=done)
            for tt in range(2):
                head_squares("ssn", ssn, QN, 128, tt, range(8), [*tok["qn0"], *tok["qn1"]])
            next(first["steps"])
            tz = []
            for pr in range(4):
                b = 4 + pr % 2
                pe.wait(*bank_free[b])
                for tt in range(2):
                    t = pe.do(call(pe.e.transpose, PS[:, b, 128 * tt:128 * tt + 128], KRf[:, tt, 128 * pr:128 * pr + 128],
                                   ident), tok["kr"])
                for hh in range(2):
                    rows = slice(64 * hh, 64 * hh + 64)
                    tz.append(dve.do(call(dve.e.tensor_copy, KZR[rows, 2 * pr + hh, :], PS[rows, b, 0:256]), t, t_z))
                bank_free[b] = tz[-2:]
            x_free[0] = [t, *t_knt]
            next(first["steps"])
            refill()
            t_ssq = dve.do(TT(ssq, ssn, ssr, ALU.add), tok["ssn"], tok["ssr"])
            t_nsq = query_scales(ssq, nsq, 8, cq, 192, [t_ssq, tok["c"]], 242)
            pe.wait(tok["v"], *tz, *t_qn, *tok["qrt"], *t_knt)
            dve.wait(t_nsq)

            def unit(u):
                return dict(heads=[dict(
                    score=[(0, 128, QNT[:, u, 0:128], KNT[:, u, 0:128], True, False),
                           (0, 128, QRT[:, u // 2, 0:128], KZR[:, u, 0:128], False, True),
                           (128, 256, QNT[:, u, 128:256], KNT[:, u, :], True, False),
                           (128, 256, QRT[:, u // 2, 128:256], KZR[:, u, :], False, True)],
                    scale=(nsq[:, 0, u:u + 1], nsq[:, 1, u:u + 1]), gate=None,
                    v=[VT[:, kb, 128 * u:128 * u + 128] for kb in range(2)])], o=u, first=True, last=True, extra=None)

            def fill2(s, i):
                if i == 2:
                    if s >= 4:
                        next(first["steps"])
                    refill(1)
            attention(8, unit, 9216, 10368, 384, o_split(), sb=(0, 1), fill=fill2)
            return first, (4, 5, 6, 7)

        def rope_tables(TAB, prior):
            pf = small(0, 2)
            ang = ROT[:, 0:64].rearrange("p (t i) -> p t i", t=2)
            A, N, NH, TMP = (ROT[:, 64 * i:64 * i + 64] for i in range(4))
            SIN, COS = ROT[:, 256:320], ROT[:, 320:384]
            two_pi = 2 * np.pi
            C1 = 6.28125
            C2 = float(np.floor((two_pi - C1) * 2 ** 20) / 2 ** 20)
            C3 = float(two_pi - C1 - C2)
            M = 12582912.0
            t = dve.do(call(dve.e.tensor_copy, pf, POSI[:, :]), t_pos, *prior)
            for tt in range(2):
                t = dve.do(call(dve.e.tensor_scalar, ang[:, tt, :], cst("inv", 32), pf[:, tt:tt + 1], None,
                                op0=ALU.mult), t)
            stt = lambda o, x, s, y: call(dve.e.scalar_tensor_tensor, o, x, s, y, ALU.mult, ALU.add)
            ts = lambda o, x, s1, s2, o0, o1: call(dve.e.tensor_scalar, o, x, s1, s2, op0=o0, op1=o1)
            one = lambda o, x, s1, o0: call(dve.e.tensor_scalar, o, x, s1, None, op0=o0)
            t = chain(
                dve, t,
                ts(N, A, 1.0 / two_pi, M, ALU.mult, ALU.add), one(N, N, M, ALU.subtract),
                ts(NH, N, 1.0 / 4096, M, ALU.mult, ALU.add), ts(NH, NH, M, 4096.0, ALU.subtract, ALU.mult),
                call(dve.e.tensor_tensor, TMP, N, NH, ALU.subtract),
                stt(A, NH, -C1, A), stt(A, TMP, -C1, A), stt(A, NH, -C2, A), stt(A, TMP, -C2, A), stt(A, N, -C3, A),
                one(N, A, np.pi / 2, ALU.add), one(TMP, N, np.pi, ALU.is_gt), stt(N, TMP, -two_pi, N),
                ts(A, A, -3.1415925, 3.1415925, ALU.max, ALU.min), ts(N, N, -3.1415925, 3.1415925, ALU.max, ALU.min))
            act.do(call(act.e.activation, SIN, A, ACT.Sin), t)
            t = act.do(call(act.e.activation, COS, N, ACT.Sin), t)
            for tab, name in zip(TAB, ("qn_rope", "kn_rope")):
                g = prm(name, 0, 64).rearrange("p (h c) -> p h c", h=2)
                for w, (gi, f) in enumerate(((0, COS), (1, SIN), (0, SIN), (1, COS))):
                    t2 = dve.do(call(dve.e.tensor_tensor, tab[:, w, :, :], f.rearrange("p (t i) -> p t i", t=2),
                                     g[:, gi, :].unsqueeze(1).broadcast_to([128, 2, 32]), ALU.mult), t, *prior)
            return t2

        HG = SCR[:, 0:2048].rearrange("p (k t) -> p k t", k=8)
        hg_tok = [None] * 8

        def out_proj_moe(li, first, banks):
            prior = lasts()

            def evict(m):
                hg_tok[m] = act.do(call(act.e.activation, HG[:, m, :], H[:, m, :], ACT.Copy,
                                        scale=prm("norm2", 8 * li + m)), h_tok[m], *prior)
                square_into(m, H[:, m, :], [h_tok[m]])
            out_proj(first, banks, evict)

        def overflow(li, CW, POSX, t_flag, prior):
            q = {n: Queue(f"s_over{li}_{n}", e) for n, e in (("sp", nc.sync), ("pe", nc.tensor), ("act", nc.scalar),
                                                             ("dve", nc.vector))}
            osp, ope, oact, odve = (q[n] for n in ("sp", "pe", "act", "dve"))
            o_load = [sem(f"s_over{li}_w"), 0]
            W = SCR[:, 4096:6144].rearrange("p (u c) -> p u c", u=4)
            Y = SCR[:, 6144:8192].rearrange("p (t c) -> p t c", t=2)
            A = SCR[:, 8192:8704].rearrange("p (t c) -> p t c", t=2)
            AT = SCR[:, 8704:9216].rearrange("p (k t) -> p k t", k=2)
            CWO = SCR[:, 11392:11456].rearrange("p (t e) -> p t e", t=2)
            r = RC[:, 0, :]
            src = a["moe"][li].rearrange("(g u h) p (e c) -> g h e p u c", u=12, h=2, e=2)
            odve.do(call(odve.e.memset, SCR[:, 6144:8192], 0.0))
            t_y = odve.do(call(odve.e.scalar_tensor_tensor, CWO, POSX, 31.5, CW, ALU.is_ge, ALU.mult))
            t_w = t_av = t_down = None
            for e in range(32):
                for hf in range(2):
                    ld_ = osp.dma(W, src[e // 4, e % 4 // 2, e % 2, :, 4 * hf:4 * hf + 4, :], o_load, t_w, ope.last)
                    for tt in range(2):
                        for k in range(4):
                            t_w = ope.do(call(ope.e.matmul, PS[:, 1 + tt, :], HG[:, 4 * hf + k, 128 * tt:128 * tt + 128],
                                              W[:, k, :], start=hf == 0 and k == 0, stop=hf == 1 and k == 3,
                                              skip_group_check=True), ld_, t_av)
                for tt in range(2):
                    t = oact.do(call(oact.e.activation, A[:, tt, :], PS[:, 1 + tt, 0:256], ACT.Silu, scale=r[:, tt:tt + 1]),
                                t_w, t_down)
                    t = odve.do(call(odve.e.scalar_tensor_tensor, A[:, tt, :], PS[:, 1 + tt, 256:512], r[:, tt:tt + 1],
                                     A[:, tt, :], ALU.mult, ALU.mult), t)
                    t_av = odve.do(call(odve.e.tensor_scalar, A[:, tt, :], A[:, tt, :], CWO[:, tt, e:e + 1], None,
                                        op0=ALU.mult), t, t_y)
                for tt in range(2):
                    for k in range(2):
                        t = ope.do(call(ope.e.transpose, PS[:, 3, 256 * k + 128 * tt:256 * k + 128 * tt + 128],
                                        A[:, tt, 128 * k:128 * k + 128], ident), t_av)
                t_at = oact.do(call(oact.e.activation, AT.rearrange("p k t -> p (k t)"), PS[:, 3, :], ACT.Copy), t)
                ld_ = osp.dma(W, src[e // 4, e % 4 // 2, e % 2, :, 8:12, :], o_load, t_w)
                for tt in range(2):
                    for n in range(2):
                        b = (4, 6, 7, 3)[2 * tt + n]
                        for k in range(2):
                            t_down = ope.do(call(ope.e.matmul, PS[:, b, :], AT[:, k, 128 * tt:128 * tt + 128],
                                                 W[:, 2 * n + k, :], start=k == 0, stop=k == 1, skip_group_check=True),
                                            ld_, t_at, t_y)
                for tt in range(2):
                    for n in range(2):
                        y = Y[:, tt, 512 * n:512 * n + 512]
                        t_y = odve.do(call(odve.e.tensor_tensor, y, PS[:, (4, 6, 7, 3)[2 * tt + n], :], y, ALU.add),
                                      t_down, t_y)
                t_av = t_y
            for f in range(8):
                for tt in range(2):
                    t = ope.do(call(ope.e.transpose, PS[:, 1 + f // 2, 256 * (f % 2) + 128 * tt:256 * (f % 2) + 128 * tt + 128],
                                    Y[:, tt, 128 * f:128 * f + 128], ident), t_y)
            for f in range(4):
                h2 = H[:, 2 * f:2 * f + 2, :].rearrange("p k t -> p (k t)")
                odve.do(call(odve.e.tensor_tensor, h2, PS[:, 1 + f, :], h2, ALU.add), t)
            ends = [x.last for x in (ope, oact, odve)]
            for n, main in (("sp", sp), ("pe", pe), ("act", act), ("dve", dve)):
                q[n].wait(*ends)

                def emit(n=n, e=main.e, ops=q[n].ops):
                    with e.register(f"over{li}_{n}") as flag:
                        e.reg_load(flag, FLAG[0:1, li:li + 1])
                        with e.If_ne(flag, 0):
                            for op in ops:
                                op()
                main.wait(t_flag, *prior)
                main.ops.append(emit)

        def moe(li):
            XN = SCR[:, 2048:4096].rearrange("p (t c) -> p t c", t=2)
            XE = [SCR[:, 4096 + 1024 * i:5120 + 1024 * i].rearrange("p (k s) -> p k s", k=8) for i in range(2)]
            S = [SCR[:, 6144 + 256 * i:6400 + 256 * i].rearrange("p (t s) -> p t s", t=2) for i in range(2)]
            SW = [SCR[:, 6656 + 256 * i:6912 + 256 * i].rearrange("p (t s) -> p t s", t=2) for i in range(2)]
            SWT = [SCR[:, 7168 + 256 * i:7424 + 256 * i] for i in range(2)]
            SG = [SCR[:, 7680 + 256 * i:7936 + 256 * i] for i in range(2)]
            AV = [SCR[:, 8192 + 256 * i:8448 + 256 * i] for i in range(2)]
            AT = [SCR[:, 8704 + 256 * i:8960 + 256 * i].rearrange("p (k s) -> p k s", k=2) for i in range(2)]
            OE = [SCR[:, 9216 + 1024 * i:10240 + 1024 * i] for i in range(2)]
            POSX = SCR[:, 11264:11328].rearrange("p (t e) -> p t e", t=2)
            CW = SCR[:, 11328:11392].rearrange("p (t e) -> p t e", t=2)
            r = RC[:, 0, :]
            prior = lasts()
            lend()
            u, w, loaded = next_raw()
            pe.wait(loaded, *bank_free[0])
            for k in range(8):
                t = pe.do(call(pe.e.matmul, PS[:, 0, 0:256], w[:, 128 * k:128 * k + 128], HG[:, k, :], start=k == 0,
                               stop=k == 7), hg_tok[k])
            give_back(u, [t])
            LT = SCR[:, 9216:9472]
            t_lt = act.do(call(act.e.activation, LT, PS[:, 0, 0:256], ACT.Copy), t, *prior)
            bank_free[0] = [t_lt]
            t_rc = rstd_cols(5, RC[:, 0, :])
            t_xn = []
            for tt in range(2):
                for kk in range(2):
                    b = 1 + 2 * tt + kk
                    pe.wait(*bank_free[b])
                    for k in range(4):
                        t = pe.do(call(pe.e.transpose, PS[:, b, 128 * k:128 * k + 128],
                                       HG[:, 4 * kk + k, 128 * tt:128 * tt + 128], ident), hg_tok[4 * kk + k])
                    if tt == 0 and kk == 0:
                        for t2 in range(2):
                            t_l = pe.do(call(pe.e.transpose, PS[:, 0, 128 * t2:128 * t2 + 128],
                                             LT[:, 128 * t2:128 * t2 + 128], ident), t_lt)
                    x = act.do(call(act.e.activation, XN[:, tt, 512 * kk:512 * kk + 512], PS[:, b, :], ACT.Copy,
                                    scale=r[:, tt:tt + 1]), t, t_rc, *prior)
                    bank_free[b] = [x]
                    t_xn.append(x)
            at = [9472]

            def new(*shape):
                n = int(np.prod(shape))
                ap = SCR[:, at[0]:at[0] + n]
                at[0] += n
                assert at[0] <= 11264
                if len(shape) == 2:
                    ap = ap.rearrange("p (a b) -> p a b", a=shape[0])
                return ap
            TT = lambda o, x, y, op: call(dve.e.tensor_tensor, o, x, y, op)
            TS = lambda o, x, s1, s2, o0, o1: call(dve.e.tensor_scalar, o, x, s1, s2, op0=o0, op1=o1)
            RED = lambda o, x, op: call(dve.e.tensor_reduce, o, x, AX.X, op)
            STT = lambda o, x, s, y, o0, o1: call(dve.e.scalar_tensor_tensor, o, x, s, y, o0, o1)
            wide = lambda ap, n: ap.unsqueeze(2).broadcast_to([128, 2, n])
            iota = lambda n: cst("iota", n).unsqueeze(1).broadcast_to([128, 2, n])
            L = new(2, 36)
            t = t_rc
            for tt in range(2):
                t = dve.do(STT(L[:, tt, :], PS[:, 0, 128 * tt:128 * tt + 36], r[:, tt:tt + 1],
                               prm("r_bias", 36 * li, 36), ALU.mult, ALU.add), t, t_l, *prior)
            bank_free[0] = [t]
            gm, eq, oh_g, gi, d4 = new(2), new(2, 4), new(2, 4), new(2), new(2, 4)
            lg = L[:, :, 0:4]
            t = chain(dve, t, RED(gm, lg, ALU.max), TT(eq, lg, wide(gm, 4), ALU.is_equal),
                      STT(eq, eq, -100.0, iota(4), ALU.mult, ALU.add), RED(gi, eq, ALU.min),
                      TT(oh_g, eq, wide(gi, 4), ALU.is_equal), TT(d4, lg, wide(gm, 4), ALU.subtract))
            t_ge = act.do(call(act.e.activation, d4, d4, ACT.Exp), t)
            pen, E1, E2 = new(2, 4), new(2, 32), new(2, 32)
            m1, m2, i1, i2 = new(2), new(2), new(2), new(2)
            q1, q2, o1, o2 = new(2, 32), new(2, 32), new(2, 32), new(2, 32)
            el4 = lambda ap: ap.rearrange("p t (g e) -> p t g e", g=4)
            t = chain(dve, t, TS(pen, oh_g, 1e30, -1e30, ALU.mult, ALU.add),
                      TT(el4(E1), el4(L[:, :, 4:36]), pen.unsqueeze(3).broadcast_to([128, 2, 4, 8]), ALU.add),
                      RED(m1, E1, ALU.max), TT(q1, E1, wide(m1, 32), ALU.is_equal),
                      STT(q1, q1, -100.0, iota(32), ALU.mult, ALU.add), RED(i1, q1, ALU.min),
                      TT(o1, q1, wide(i1, 32), ALU.is_equal), STT(E2, o1, -2e30, E1, ALU.mult, ALU.add),
                      RED(m2, E2, ALU.max), TT(q2, E2, wide(m2, 32), ALU.is_equal),
                      STT(q2, q2, -100.0, iota(32), ALU.mult, ALU.add), RED(i2, q2, ALU.min),
                      TT(o2, q2, wide(i2, 32), ALU.is_equal))
            mk = new(2, 32)
            t_mk = dve.do(TT(mk, o1, o2, ALU.add), t)
            before = cst("before", 128)
            pe.wait(t_mk, *bank_free[5])
            pe.run(call(pe.e.matmul, PS[:, 5, 0:32], before, mk[:, 0, :], start=True, stop=True, skip_group_check=True))
            pe.run(call(pe.e.matmul, PS[:, 5, 32:64], before, mk[:, 1, :], start=True, stop=False, skip_group_check=True))
            pe.run(call(pe.e.matmul, PS[:, 5, 32:64], ones, mk[:, 0, :], start=False, stop=True, skip_group_check=True))
            pe.run(call(pe.e.matmul, PS[:, 5, 64:96], ones, mk[:, 0, :], start=True, stop=False, skip_group_check=True))
            t_pos2 = pe.do(call(pe.e.matmul, PS[:, 5, 64:96], ones, mk[:, 1, :], start=False, stop=True,
                                skip_group_check=True))
            dd, gs, den, w1, w2 = new(2), new(2), new(2), new(2), new(2)
            t = dve.do(TT(dd, m2, m1, ALU.subtract), t_mk)
            t_e = act.do(call(act.e.activation, dd, dd, ACT.Exp), t)
            t = dve.do(RED(gs, d4, ALU.add), t_ge)
            dve.wait(t)
            t = chain(dve, t_e, STT(den, dd, 1.0, gs, ALU.add, ALU.mult), call(dve.e.reciprocal, w1, den),
                      TT(w2, w1, dd, ALU.mult), TT(o1, o1, wide(w1, 32), ALU.mult), TT(o2, o2, wide(w2, 32), ALU.mult),
                      TT(CW, o1, o2, ALU.add), TS(E2, mk, -1000.0, 1000.0, ALU.mult, ALU.add))
            t_px = dve.do(TT(POSX, E2, PS[:, 5, 0:64].rearrange("p (t e) -> p t e", t=2), ALU.add), t, t_pos2)
            cm = new(2)
            t = dve.do(RED(cm[:, 0:1], PS[:, 5, 64:96], ALU.max), t_px)
            t_flag = dve.do(call(dve.e.tensor_scalar, FLAG[:, li:li + 1], cm[:, 0:1], 32.5, None, op0=ALU.is_gt), t)
            bank_free[5] = [t]
            overflow(li, CW, POSX, t_flag, [*t_xn, *lasts(), *[t for b in bank_free for t in b]])

            tk = {}

            def places(g):
                s, i = S[g % 2], g % 2
                px = POSX[:, :, 4 * g:4 * g + 4].unsqueeze(3).broadcast_to([128, 2, 4, 32])
                cw = CW[:, :, 4 * g:4 * g + 4].unsqueeze(3).broadcast_to([128, 2, 4, 32])
                io = cst("iota", 32).unsqueeze(1).unsqueeze(1).broadcast_to([128, 2, 4, 32])
                v = lambda ap: ap.rearrange("p t (e s) -> p t e s", e=4)
                t = dve.do(TT(v(S[i]), io, px, ALU.is_equal), t_px, tk.get(("gather", g - 2)), tk.get(("turn", g - 2)),
                           dve.last)
                tk["S", g] = dve.do(TT(v(SW[i]), v(S[i]), cw, ALU.mult), t)

            def gather(g):
                for hf in range(2):
                    pe.wait(*bank_free[hf])
                    for k in range(4):
                        o = PS[:, hf, 128 * k:128 * k + 128]
                        for tt in range(2):
                            t = pe.do(call(pe.e.matmul, o, XN[:, tt, 128 * (4 * hf + k):128 * (4 * hf + k) + 128],
                                           S[g % 2][:, tt, :], start=tt == 0, stop=tt == 1, skip_group_check=True),
                                      tk["S", g], *t_xn)
                    dst = XE[g % 2][:, 4 * hf:4 * hf + 4, :].rearrange("p k s -> p (k s)")
                    before_ = tk.get(("gu", g - 2))
                    if hf:
                        t2 = dve.do(call(dve.e.tensor_copy, dst, PS[:, hf, :]), t, before_)
                    else:
                        t2 = act.do(call(act.e.activation, dst, PS[:, hf, :], ACT.Copy), t, before_)
                    bank_free[hf] = [t2]
                    tk["xe", g, hf] = t2
                tk["gather", g] = t

            def gate_up(g):
                pe.wait(*bank_free[2], tk["xe", g, 0], tk["xe", g, 1])
                for k in range(8):
                    us, e = [next_raw(), next_raw()], 0
                    for u, w, loaded in us:
                        pe.wait(loaded)
                    for e in range(4):
                        w = us[e // 2][1][:, 512 * (e % 2):512 * (e % 2) + 512]
                        t = pe.do(call(pe.e.matmul, PS[32 * e:32 * e + 32, 2, :], XE[g % 2][:, k, 32 * e:32 * e + 32],
                                       w, start=k == 0, stop=k == 7, skip_group_check=True))
                    for u, w, loaded in us:
                        give_back(u, [t])
                tk["gu", g] = t
                i = g % 2
                ts = act.do(call(act.e.activation, SG[i], PS[:, 2, 0:256], ACT.Silu), t, tk.get(("av", g - 2)))
                tk["av", g] = dve.do(TT(AV[i], SG[i], PS[:, 2, 256:512], ALU.mult), ts, tk.get(("turn", g - 2)))
                bank_free[2] = [tk["av", g]]

            def turn_(g):
                i = g % 2
                pe.wait(*bank_free[5])
                for k in range(2):
                    t = pe.do(call(pe.e.transpose, PS[:, 5, 128 * k:128 * k + 128], AV[i][:, 128 * k:128 * k + 128],
                                   ident), tk["av", g])
                for tt in range(2):
                    t = pe.do(call(pe.e.transpose, PS[:, 5, 256 + 128 * tt:384 + 128 * tt], SW[i][:, tt, :], ident),
                              tk["S", g])
                tk["turn", g] = t
                ta = act.do(call(act.e.activation, AT[i].rearrange("p k s -> p (k s)"), PS[:, 5, 0:256], ACT.Copy), t,
                            tk.get(("down", g - 2)))
                tk["sw", g] = dve.do(call(dve.e.tensor_copy, SWT[i], PS[:, 5, 256:512]), ta, tk.get(("comb", g - 2)))
                tk["at", g] = ta
                bank_free[5] = [tk["sw", g]]

            def down(g):
                i = g % 2
                pe.wait(tk["at", g])
                for n in range(2):
                    pe.wait(*bank_free[3 + n])
                    for k in range(2):
                        us = [next_raw(), next_raw()]
                        for u, w, loaded in us:
                            pe.wait(loaded)
                        for e in range(4):
                            w = us[e // 2][1][:, 512 * (e % 2):512 * (e % 2) + 512]
                            t = pe.do(call(pe.e.matmul, PS[32 * e:32 * e + 32, 3 + n, :], AT[i][:, k, 32 * e:32 * e + 32],
                                           w, start=k == 0, stop=k == 1, skip_group_check=True))
                        for u, w, loaded in us:
                            give_back(u, [t])
                    d = OE[i][:, 512 * n:512 * n + 512]
                    if n:
                        t2 = dve.do(call(dve.e.tensor_copy, d, PS[:, 3 + n, :]), t, tk.get(("comb", g - 2)))
                    else:
                        t2 = act.do(call(act.e.activation, d, PS[:, 3 + n, :], ACT.Copy), t, tk.get(("comb", g - 2)))
                    bank_free[3 + n] = [t2]
                    tk["oe", g, n] = t2
                tk["down", g] = t

            def combine(g):
                i = g % 2
                pe.wait(tk["sw", g])
                for f in range(4):
                    b = 6 + f % 2
                    pe.wait(*bank_free[b], tk["oe", g, f // 2])
                    for x in range(2):
                        t = pe.do(call(pe.e.matmul, PS[:, b, 256 * x:256 * x + 256],
                                       OE[i][:, 128 * (2 * f + x):128 * (2 * f + x) + 128], SWT[i], start=True, stop=True,
                                       skip_group_check=True))
                    h2 = H[:, 2 * f:2 * f + 2, :].rearrange("p k t -> p (k t)")
                    t2 = dve.do(TT(h2, PS[:, b, :], h2, ALU.add), t, h_tok[2 * f], h_tok[2 * f + 1])
                    h_tok[2 * f] = h_tok[2 * f + 1] = t2
                    bank_free[b] = [t2]
                    if g == 7 and li == 0:
                        prep_high()
                    if g == 7:
                        for k in (2 * f, 2 * f + 1):
                            if li == 0:
                                new_h(k, prm("norm1", 8 + k))
                            else:
                                t_out.append(sp.dma(out[:, 256 * k:256 * k + 256], H[:, k, :], o_sems[k], h_tok[k]))
                tk["comb", g] = t

            places(0)
            places(1)
            gather(0)
            for g in range(8):
                gate_up(g)
                if g >= 1:
                    combine(g - 1)
                if g < 7:
                    gather(g + 1)
                turn_(g)
                down(g)
                if g + 2 < 8:
                    places(g + 2)
                if g == 6 and li == 0:
                    st["limit"] = bounds[1]
            refill()
            combine(7)

        def start_layer(gain_name, at):
            for k in range(8):
                split_into(0, k, H[:, k, :], [h_tok[k]], prm(gain_name, at + k))
                if k < 4:
                    refill((2, 1, 1, 0)[k])
            refill(3)
            for k in range(8):
                square_into(k, H[:, k, :], [h_tok[k]])

        t_out = []
        o_sems = [[sem(f"s_out{i}"), 0] for i in range(8)]

        def program():
            start_layer("norm_mix", 0)
            for i in range(4):
                first, banks = nsa(i // 3) if i % 3 == 0 else moba() if i == 1 else conv()
                out_proj(first, banks, ffn_input(i))
                if i < 3:
                    ffn(i, lambda d, i=i: ("norm_mix", 8 * (i + 1) + d))
                else:
                    load_mem()
                    ffn(i, None, mem_hook)

            KM, t_km = mem_kv()
            first, banks = gmlp(KM, t_km)
            out_proj_moe(0, first, banks)
            moe(0)
            first, banks = mla()
            out_proj_moe(1, first, banks)
            moe(1)
            sp.wait(*t_out)

        program()

        with nc.Block() as block:
            @block.sync
            def _(e):
                for op in sp.ops:
                    op()

            @block.tensor
            def _(e):
                for op in pe.ops:
                    op()

            @block.scalar
            def _(e):
                for op in act.ops:
                    op()

            @block.vector
            def _(e):
                for op in dve.ops:
                    op()

            @block.gpsimd
            def _(e):
                for op in pool.ops:
                    op()


def by_rows(w):
    k, m = w.shape[0] // 128, w.shape[1] // 128
    t = w.reshape(k, 128, m, 128).transpose(2, 0, 1, 3).reshape(m * k // 8, 8, 128, 128)
    return t.transpose(0, 2, 1, 3).reshape(-1, 128, 1024)


def by_cols(w, per):
    k, cols = w.shape[0] // 128, w.shape[1]
    t = w.reshape(k, 128, cols)
    out = np.zeros((-(-k // per), 128, 1024), w.dtype)
    for b in range(out.shape[0]):
        for i in range(min(per, k - per * b)):
            out[b, :, cols * i:cols * i + cols] = t[per * b + i]
    return out


def beside(w):
    return np.stack([by_cols(w[:, :512], 2), by_cols(w[:, 512:], 2)], 1).reshape(-1, 128, 1024)


def columns(v):
    v = v.reshape(-1, v.shape[-1] // 128, 128)
    return v.transpose(2, 0, 1).reshape(128, -1)


def layout(x):
    x = {k: np.asarray(v) for k, v in x.items()}
    out = {"cst": CONST}

    def tokens_last(v):
        return v.reshape(256, 8, 128).transpose(2, 1, 0).reshape(128, 2048)

    out["xT"] = tokens_last(x["x"])
    out["memT"] = tokens_last(x["mem_2"])
    out["pos"] = x["positions_2"].reshape(2, 128).T

    pos = []
    for j in range(2):
        for name in ("nsa_cmp_pos_k", "nsa_cmp_pos_v"):
            p = x[name][j].reshape(16, 2, 64).transpose(2, 1, 0).reshape(64, 32)
            pos.append(np.concatenate([p, p], 0))
    w2 = []
    for j in range(2):
        for name in ("nsa_cmp_k_w2", "nsa_cmp_v_w2"):
            w2.append(x[name][j].reshape(2, 128, 64).transpose(1, 0, 2).reshape(128, 128))
    rows = lambda v: np.broadcast_to(v[None, :], (128, v.shape[0]))
    bias = [rows(np.concatenate([x["moe_b_group_2"][i], x["moe_b_expert_2"][i]])) for i in range(2)]
    prm = [columns(x["norm_mix"]), columns(x["norm_ffn"]), columns(x["norm_final"]), columns(x["mem_norm_g_2"]),
           columns(x["norm1_g_2"]), columns(x["norm2_g_2"]), columns(x["mem_qn_g_2"]), columns(x["mem_kn_g_2"]),
           x["conv_w"][0].reshape(3, 8, 128).transpose(2, 1, 0).reshape(128, 24),
           columns(x["b_q_norm_g_2"]), columns(x["b_kv_norm_g_2"]),
           columns(x["b_qn_g_2"][:, :128]), columns(x["b_kn_g_2"][:, :128]),
           rows(x["b_qn_g_2"][0, 128:]), rows(x["b_kn_g_2"][0, 128:])] + pos + w2 + bias
    out["prm"] = np.concatenate(prm, 1)

    in1, in2, wo, cmp_ = [], [], [], []
    heads = np.array([4 * (2 * p + h) + r for p in range(2) for r in range(4) for h in range(2)])
    perm = (64 * heads[:, None] + np.arange(64)[None]).reshape(-1)
    for j in range(2):
        w = x["nsa_w_in"][j]
        part = lambda i: w[:, 1024 + 256 * i:1280 + 256 * i]
        vg = np.concatenate([part(3), w[:, 2560:2608]], 1)
        q = by_rows(w[:, :1024][:, perm])
        in1.append(np.concatenate([by_rows(part(i)) for i in (0, 1, 2, 4)] + [q[:1]]))
        in2.append(np.concatenate([q[1:4], by_cols(vg, 3), by_cols(part(5), 4), q[4:]]))
        wo.append(by_rows(x["nsa_w_out"][j][perm]))
        c = np.stack([x["nsa_cmp_k_w1"][j], x["nsa_cmp_v_w1"][j]])
        cmp_.append(c.reshape(2, 8, 2, 128, 256).transpose(1, 3, 2, 0, 4).reshape(8, 128, 1024))
    out["nsa_in1"], out["nsa_in2"], out["nsa_out"], out["w_cmp"] = (np.stack(v) for v in (in1, in2, wo, cmp_))

    w = x["moba_w_in"][0]
    q, k = by_rows(w[:, :1024]), by_rows(w[:, 1024:2048])
    out["moba_in"] = np.concatenate([beside(w[:, 2048:]), np.stack([q, k], 1).reshape(16, 128, 1024)])[None]
    out["moba_out"] = by_rows(x["moba_w_out"][0])[None]
    b, c, u = (by_rows(x["conv_w_in"][0][:, 1024 * i:1024 * i + 1024]) for i in range(3))
    out["conv_in"] = np.stack([c, u, b], 1).reshape(24, 128, 1024)[None]
    out["conv_out"] = by_rows(x["conv_w_out"][0])[None]

    ffn = []
    for i in range(4):
        g, u, d = by_rows(x["ffn_w_gate"][i]), by_rows(x["ffn_w_up"][i]), x["ffn_w_down"][i].reshape(22, 128, 1024)
        seq = []
        for f in range(22):
            seq += [g[f], u[f]]
            if f >= 3:
                seq.append(d[f - 3])
        ffn.append(np.stack(seq + [d[19], d[20], d[21]]))
    out["ffn"] = np.stack(ffn)

    out["mem_kv"] = beside(x["w_mem_kv_2"])[None]
    mem_first = lambda w: np.concatenate([w[1024:], w[:1024]])
    w = x["a_w_in_2"][0]
    out["a_in"] = np.concatenate([beside(w[:, 1024:2048]), by_cols(w[:, 2048:], 2), by_rows(w[:, :1024])])[None]
    out["a_out"] = by_rows(mem_first(x["a_w_out_2"][0]))[None]
    ln = np.concatenate([x["a_ln_g_2"][0], x["a_ln_b_2"][0]])
    out["a_ln"] = np.broadcast_to(ln[None], (128, 2048))
    out["a_ws"] = x["a_w_s_2"][0].transpose(2, 0, 1).reshape(128, 1024)
    out["a_bs"] = np.broadcast_to(x["a_b_s_2"][0].reshape(1, 1024), (128, 1024))
    rt = []
    for i in range(2):
        w = np.zeros((1024, 128), np.float32)
        w[:, :4], w[:, 4:36] = x["moe_w_group_2"][i], x["moe_w_expert_2"][i]
        rt.append(by_rows(w))
    out["router"] = np.stack(rt)
    w = x["b_w_in_2"][0]
    out["b_in"] = np.concatenate([beside(np.concatenate([w[:, :512], w[:, 832:]], 1)), by_cols(w[:, 512:832], 3)])[None]
    w = x["b_w_q_up_2"][0].reshape(512, 8, 192)
    q_n, q_r = w[:, :, :128].reshape(512, 1024), w[:, :, 128:].reshape(512, 512)
    w = x["b_w_kv_up_2"][0].reshape(256, 8, 2, 128)
    k, v = w[:, :, 0].reshape(256, 1024), w[:, :, 1].reshape(256, 1024)
    ups = [q_r, k[:, :512], k[:, 512:], q_n[:, :512], q_n[:, 512:], v[:, :512], v[:, 512:]]
    out["b_up"] = np.concatenate([by_cols(w, 2) for w in ups])[None]
    out["b_out"] = by_rows(mem_first(x["b_w_out_2"][0]))[None]

    g, u = (x[n].reshape(2, 8, 4, 8, 128, 256) for n in ("moe_w_gate_2", "moe_w_up_2"))
    moe = np.empty((2, 8, 12, 128, 4, 512), np.float32)
    moe[:, :, :8, :, :, :256] = g.transpose(0, 1, 3, 4, 2, 5)
    moe[:, :, :8, :, :, 256:] = u.transpose(0, 1, 3, 4, 2, 5)
    d = x["moe_w_down_2"].reshape(2, 8, 4, 2, 128, 2, 512)
    moe[:, :, 8:] = d.transpose(0, 1, 5, 3, 4, 2, 6).reshape(2, 8, 4, 128, 4, 512)
    out["moe"] = moe.reshape(2, 96, 128, 2, 1024).transpose(0, 1, 3, 2, 4).reshape(2, 192, 128, 1024)
    return {k: np.ascontiguousarray(v) for k, v in out.items()}


def kernel(**inputs):
    import concourse.bacc as _bacc
    from concourse import mybir as _mybir
    from concourse.bass_utils import run_bass_kernel_spmd as _run

    nc = _bacc.Bacc("TRN2", target_bir_lowering=False, num_devices=1)
    arrays = layout(inputs)
    args = {n: nc.dram_tensor(n, v.shape, _mybir.dt.from_np(v.dtype), kind="ExternalInput").ap()
            for n, v in arrays.items()}
    y = nc.dram_tensor("out_0_dram", (128, 2048), _mybir.dt.float32, kind="ExternalOutput").ap()
    blocks_kernel(nc, args, y)
    r = _run(nc, [arrays], core_ids=[0])
    got = np.asarray(r.results[0]["out_0_dram"])
    return got.reshape(128, 8, 256).transpose(2, 1, 0).reshape(1, 256, 1024)
```

```python
import concourse.bass as bass
from concourse import mybir
from contextlib import ExitStack
import numpy as np


def const_table():
    p = np.arange(128)
    parts, at, n = {}, {}, 0

    def add(name, a):
        nonlocal n
        parts[name] = np.broadcast_to(np.asarray(a, np.float32), (128, np.asarray(a).shape[-1]))
        at[name] = n
        n += parts[name].shape[1]

    add("ident", np.eye(128))
    add("ones", np.ones((128, 128)))
    tri = np.where(p[None, :] <= p[:, None], 0.0, -1e30)
    add("mask", np.concatenate([np.zeros((128, 256)), tri], 1))
    c = np.arange(16)
    cm = [np.where((16 * c[None] + 31 <= p[:, None] + 128 * q) & (c[None] < 15), 0.0, -1e30) for q in range(2)]
    add("cmask", np.concatenate(cm, 1))
    add("before", (p[:, None] < p[None, :]) - 1000.0 * np.eye(128))
    add("iota", np.arange(32)[None, :] - 1000.0)
    add("inv", (10000.0 ** (-(np.arange(32) * 2.0 / 64))).astype(np.float32)[None, :])
    add("eps", np.full((128, 1), 1e-6))
    return np.ascontiguousarray(np.concatenate(list(parts.values()), 1)), at, n


CONST, CAT, NCONST = const_table()

PARAMS = [("norm_mix", 32), ("norm_ffn", 32), ("norm_final", 8), ("mem_norm", 8), ("norm1", 16), ("norm2", 16),
          ("mem_qn", 2), ("mem_kn", 2), ("conv_w", 24), ("q_norm", 4), ("kv_norm", 2), ("qn_nope", 1), ("kn_nope", 1),
          ("qn_rope", 64), ("kn_rope", 64), ("r_bias", 72)]
PAT, NPARAM = {}, 0
for _name, _n in PARAMS:
    PAT[_name] = NPARAM
    NPARAM += _n

NSLOT = 21
NSCR = 13824


def blocks_kernel(nc, a, out):
    F32, F32R, I32 = mybir.dt.float32, mybir.dt.float32r, mybir.dt.int32
    ALU, ACT, AX = mybir.AluOpType, mybir.ActivationFunctionType, mybir.AxisListType
    ctx = ExitStack()

    def sb(name, shape, dt=F32):
        return ctx.enter_context(nc.sbuf_tensor(name, shape, dt))

    def both(name, shape):
        with nc.sbuf_tensor(name, shape, F32R) as rounded:
            pass
        return rounded, sb(name + "_f", shape)

    def sem(name):
        return ctx.enter_context(nc.semaphore(name))

    def call(f, *args, **kw):
        return lambda: f(*args, **kw)

    class Queue:



        def __init__(self, name, e):
            self.sem, self.e, self.ops, self.count, self.met = sem(name), e, [], 0, {}

        def wait(self, *tokens):
            for t in tokens:
                if t is not None and self.met.get(t[0].name, 0) < t[1]:
                    self.met[t[0].name] = t[1]
                    self.ops.append(call(self.e.wait_ge, t[0], t[1]))

        def run(self, op, *tokens):
            self.wait(*tokens)
            self.ops.append(op)

        def do(self, op, *tokens):
            self.wait(*tokens)
            self.count += 1
            self.ops.append(lambda: op().then_inc(self.sem, 1))
            return (self.sem, self.count)

        @property
        def last(self):
            return (self.sem, self.count) if self.count else None

        def dma(self, dst, src, s, *tokens):
            self.wait(*tokens)
            s[1] += 16
            v = s[1]
            self.ops.append(lambda: self.e.dma_start(dst, src).then_inc(s[0], 16))
            return (s[0], v)

    with ctx:
        RINGR, RING = both("RING", [128, NSLOT, 1024])
        (XH0, FH0), (XL0, FL0), (XH1, FH1), (XL1, FL1) = (both(n, [128, k, 256]) for n, k in (
            ("XH0", 8), ("XL0", 8), ("XH1", 12), ("XL1", 12)))
        XH, XL = [XH0, XH1], [XL0, XL1]
        H = sb("H", [128, 8, 256])
        G, FG = both("G", [128, 12, 256])
        GH, GL = G[:, 0:3, :], G[:, 3:6, :]
        CST = sb("CST", [128, NCONST])
        PRM = sb("PRM", [128, NPARAM])
        RB, NT = FG[:, 6:8, :], FG[:, 8:11, :]
        RC = sb("RC", [128, 2, 2])
        SQ = sb("SQ", [128, 2, 256])
        ACC = sb("ACC", [128, 256])
        ST = sb("ST", [128, 4, 24])
        SM = sb("SM", [128, 320])
        POSI = sb("POSI", [128, 2], I32)
        FLAG = sb("FLAG", [128, 2], I32)
        SCR = sb("SCR", [128, NSCR])
        PS = ctx.enter_context(nc.psum_tensor("PS", [128, 8, 512], F32))

        pe, act, dve, pool, sp = (Queue(*n) for n in (
            ("s_pe", nc.tensor), ("s_act", nc.scalar), ("s_dve", nc.vector), ("s_pool", nc.gpsimd), ("s_sp", nc.sync)))
        everyone = (pe, act, dve, pool)


        def cst(name, n, at=0):
            return CST[:, CAT[name] + at:CAT[name] + at + n]

        def prm(name, at=0, n=1):
            return PRM[:, PAT[name] + at:PAT[name] + at + n]

        def lasts():
            return [q.last for q in everyone]

        def f32(ap):
            return ap.bitcast(F32)

        units, dense_ids, raw_ids = [], [], []

        def section(name, j, first=0, end=None):
            for b in range(a[name].shape[1])[first:end]:
                dense_ids.append(len(units))
                width = (960, 960, 640)[b] if name == "b_in" and b < 3 else 1024
                units.append(a[name][j, b][:, 0:width])

        def raws(name, j, end=None):
            for b in range(done.get((name, j), 0), end or a[name].shape[1]):
                raw_ids.append(len(units))
                units.append(a[name][j, b])
            done[name, j] = end

        done = {}
        bounds = {}
        for i in range(4):
            if i % 3 == 0:
                section("nsa_in1", i // 3)
                raws("w_cmp", i // 3)
                section("nsa_in2", i // 3)
                section("nsa_out", i // 3)
            elif i % 3 == 1:
                section("moba_in", 0)
                section("moba_out", 0)
            else:
                section("conv_in", 0)
                section("conv_out", 0)
            section("ffn", i)
        section("mem_kv", 0)
        section("a_in", 0)
        section("a_out", 0)
        bounds[0] = len(dense_ids)
        raws("router", 0)
        raws("moe", 0, 190)
        section("b_in", 0, 0, 1)
        raws("moe", 0, 192)
        ring_only = raw_ids[-4:]
        section("b_in", 0, 1)
        section("b_up", 0)
        section("b_out", 0)
        bounds[1] = len(dense_ids)
        raws("router", 1)
        raws("moe", 1)
        is_dense = [False] * len(units)
        for u in dense_ids:
            is_dense[u] = True

        flat = lambda ap: ap.rearrange("p k t -> p (k t)")
        more = dict(x0=[flat(x[:, 4 * i:4 * i + 4, :]) for i in range(2) for x in (FH0, FL0)],
                    x1=[flat(FL1[:, 8:12, :])], oe1=[flat(FH1[:, 8:12, :])], u=[SCR[:, 2048 + 1024 * i:3072 + 1024 * i] for i in range(2)],
                    v=[SCR[:, 7168 + 1024 * i:8192 + 1024 * i] for i in range(2)], p=[SCR[:, 9728:10752]],
                    g=[flat(FG[:, 0:4, :])], norm=[flat(FG[:, i:i + 4, :]) for i in (4, 8)], hg=[SCR[:, 0:1024], SCR[:, 1024:2048]],
                    mem=[SCR[:, 11776 + 1024 * i:12800 + 1024 * i] for i in range(2)],
                    q=[(flat(SQ[:, :, :]), SCR[:, 9216:9728])], xe=[SCR[:, 5120:6144]], oe=[SCR[:, 4096:5120]], av0=[SCR[:, 10752:11776]], av1=[SCR[:, 6144:7168]])
        spaces = [RING[:, i, :] for i in range(NSLOT)]
        group_of = {}
        for name, aps in more.items():
            group_of[name] = range(len(spaces), len(spaces) + len(aps))
            spaces += aps
        slot_sem = [[sem(f"s_slot{i}"), 0] for i in range(len(spaces))]
        free, lent, once = [(i, []) for i in range(NSLOT)], [], {}
        where = {}
        st = dict(issued=0, dense=0, prepped=0, released=0, limit=bounds[0], raw=0, x=0, ahead=8, lag=1)
        w_at, w_ready, w_left, halves = {}, {}, {}, []

        def columns(w, at, n):
            return w[at // 512][:, at % 512:at % 512 + n] if isinstance(w, tuple) else w[:, at:at + n]

        def pump(n=99999):
            while st["issued"] < min(n, len(units)):
                u = st["issued"]
                d = is_dense[u]
                if lent and not d and u not in ring_only:
                    s, tokens = lent.pop(0)
                else:
                    kept = min(st["ahead"] - (st["prepped"] - st["released"]), st["dense"] + d - st["prepped"])
                    if len(free) - 1 < max(kept, 0):
                        return
                    s, tokens = free.pop(0)
                w, n_cols = units[u], units[u].shape[1]
                step = 512 if isinstance(spaces[s], tuple) else 1024
                for x in range(0, n_cols, step):
                    n_here = min(step, n_cols - x)
                    t = sp.dma(columns(spaces[s], x, n_here), w[:, x:x + n_here], slot_sem[s], *tokens)
                where[u] = (s, t)
                st["dense"] += d
                st["issued"] += 1

        def lend(name, tokens, first=0, end=None):
            lent.extend((i, list(tokens)) for i in group_of[name][first:end])
            pump()

        def lend_once(name, tokens):
            once[name] = None
            lent.insert(0, (group_of[name][0], list(tokens)))
            pump()

        def reclaim(name):
            back = [f for f in lent if f[0] in group_of[name]]
            assert len(back) == len(group_of[name])
            lent[:] = [f for f in lent if f[0] not in group_of[name]]
            return [t for _, tokens in back for t in tokens]

        def give_back(u, tokens):
            s = where[u][0]
            for name in once:
                if s in group_of[name]:
                    once[name] = list(tokens)
                    return
            (free if s < NSLOT else lent).append((s, list(tokens)))
            pump()

        def prep_high():
            b = st["prepped"]
            if b >= st["limit"] or b - st["released"] >= st["ahead"] or not free:
                return False
            u = dense_ids[b]
            if u not in where:
                return False
            c, loaded = where[u]
            h, tokens = free.pop(0)
            raw = spaces[c]
            w_at[b] = (h, c, RINGR[:, h, :], RINGR[:, c, :])
            n = units[u].shape[1]
            halves.append((b, act.do(call(act.e.activation, w_at[b][2][:, 0:n], raw[:, 0:n], ACT.Copy), loaded, *tokens)))
            w_left[b] = 1024
            st["prepped"] += 1
            pump()
            return True

        def prep_low():
            b, t = halves.pop(0)
            _, c, wh, wl = w_at[b]
            q = pool if b in range(bounds[0], bounds[0] + 24, 4) else dve
            n = units[dense_ids[b]].shape[1]
            w_ready[b] = q.do(call(q.e.tensor_tensor, wl[:, 0:n], spaces[c][:, 0:n], f32(wh[:, 0:n]), ALU.subtract), t)

        def fill_in():
            if halves:
                prep_low()

        def refill(n=2):
            for _ in range(n):
                if not prep_high():
                    break
            while len(halves) > st["lag"]:
                prep_low()

        def weights(x, n):
            b, c = divmod(x, 1024)
            while b not in w_ready:
                if not halves:
                    assert prep_high()
                prep_low()
            pe.wait(w_ready[b])
            assert c + n <= 1024
            return w_at[b][2][:, c:c + n], w_at[b][3][:, c:c + n]

        def ends_block(x, n):
            w_left[x // 1024] -= n
            return w_left[x // 1024] == 0

        def release(x, token):
            assert token[0] is pe.sem
            h, c, _, _ = w_at[x // 1024]
            free.append((h, [token]))
            free.append((c, [token]))
            st["released"] += 1
            pump()

        def next_raw():
            u = raw_ids[st["raw"]]
            st["raw"] += 1
            c, loaded = where[u]
            return u, spaces[c], loaded

        bank_free = [[] for _ in range(8)]
        turn = dict(b=0)

        def next_bank(banks):
            b = banks[turn["b"] % len(banks)]
            turn["b"] += 1
            return b

        def three(o, wh, wl, xh, xl, start, stop, signal, swap=False):
            for i, (l, r) in enumerate(((wh, xh), (wh, xl), (wl, xh))):
                if swap:
                    l, r = r, l
                f = (call(pe.e.matmul, o, l, r, start=start and i == 0, stop=stop and i == 2,
                                                     skip_group_check=True))
                if signal and i == 2:
                    return pe.do(f)
                pe.run(f)

        def grid(xi, ks, outs, x_tokens, fresh=None):
            base, tokens = st["x"], [None] * len(outs)
            st["x"] += 128 * len(ks) * len(outs)

            def steps():
                for n, k in enumerate(ks):
                    for m, o in enumerate(outs):
                        x = base + 128 * (n * len(outs) + m)
                        wh, wl = weights(x, 128)
                        assert x_tokens[k] is not None
                        pe.wait(x_tokens[k])
                        full, last = ends_block(x, 128), n == len(ks) - 1
                        t = three(o, wh, wl, XH[xi][:, k, :], XL[xi][:, k, :],
                                  n == 0 and (fresh is None or fresh[m]), last, full or last)
                        if last:
                            tokens[m] = t
                        if full:
                            release(x, t)
                    yield
            return tokens, steps()

        def group(xi, ks, banks, x_tokens):
            for b in banks:
                pe.wait(*bank_free[b])
            tokens, steps = grid(xi, ks, [PS[:, b, 0:256] for b in banks], x_tokens)
            for _ in steps:
                pass
            return tokens

        def mtile(xi, ks, o, x_tokens):
            tokens, steps = grid(xi, ks, [o], x_tokens)
            for _ in steps:
                pass
            return tokens[0]

        def vtile(xi, ks, cols, per_block, banks, x_tokens, halfway=None):
            for n, k in enumerate(ks):
                if halfway and n == per_block:
                    halfway()
                x = st["x"] + cols * (n % per_block)
                wh, wl = weights(x, cols)
                assert x_tokens[k] is not None
                pe.wait(x_tokens[k])
                end = (n + 1) % per_block == 0 or n == len(ks) - 1
                for tt in range(2):
                    sl = slice(128 * tt, 128 * (tt + 1))
                    t = three(PS[:, banks[tt], 0:cols], wh, wl, XH[xi][:, k, sl], XL[xi][:, k, sl],
                              n == 0, n == len(ks) - 1, tt == 1, swap=True)
                if end:
                    release(x, t)
                    st["x"] += 1024
            return t

        def vtiles(xi, ks, banks):
            t = [None, None]

            def steps():
                for b in banks:
                    pe.wait(*bank_free[b], *bank_free[b + 1])
                for n in range(0, len(ks), 2):
                    for v, b in enumerate(banks):
                        for i in range(2):
                            k = ks[n + i]
                            x = st["x"] + 512 * i
                            wh, wl = weights(x, 512)
                            assert x_tok[xi][k] is not None
                            pe.wait(x_tok[xi][k])
                            for tt in range(2):
                                sl = slice(128 * tt, 128 * (tt + 1))
                                t[v] = three(PS[:, b + tt, :], wh, wl, XH[xi][:, k, sl], XL[xi][:, k, sl], n + i == 0,
                                             n + i == len(ks) - 1, tt == 1, swap=True)
                        release(x, t[v])
                        st["x"] += 1024
                    yield
            return t, steps()

        t = dve.do(call(dve.e.memset, SM[:, 319:320], 0.0))
        act.do(call(act.e.activation, SM[:, 318:319], SM[:, 319:320], ACT.Copy), t)

        def load(name, dst, src, *tokens):
            return sp.dma(dst, src, [sem(name), 0], *tokens)
        t_first = load("s_gain", PRM[:, 0:32], a["prm"][:, 0:32])
        h2 = H[:, :, :].rearrange("p k t -> p (k t)")
        t_x = []
        for i in range(4):
            pump(i + 1)
            t_x.append(load(f"s_x{i}", h2[:, 512 * i:512 * i + 512], a["xT"][:, 512 * i:512 * i + 512]))
        t_cst = load("s_cst", CST[:, :], a["cst"])
        t_prm = load("s_prm", PRM[:, 32:NPARAM], a["prm"][:, 32:NPARAM])
        CMP = SCR[:, 13056:13376]
        t_cmp = [load("s_cmp0", CMP, a["cmp"][0])]
        t_pos = load("s_pos", POSI[:, :], a["pos"])
        pump()
        for q in (act, dve):
            q.wait(t_first)

        def constants():
            for q in everyone:
                q.wait(t_cst, t_prm)

        ident = cst("ident", 128)
        ones = cst("ones", 128)
        eps = cst("eps", 1)

        def scr(at, n, **dims):
            return SCR[:, at:at + n]

        h_tok = [t_x[k // 2] for k in range(8)]
        x_tok = {0: [None] * 12, 1: [None] * 12}
        x_free = {0: [], 1: []}

        def done_with(xi, token):
            x_free[xi] = [token]
            x_tok[xi][:] = [None] * 12
        sq_tok = [None, None]
        norm = dict(acc=None, rb=0, readers=[])

        def split_into(xi, k, src, tokens, gain=None):
            xh, xl = XH[xi][:, k, :], XL[xi][:, k, :]
            if gain is None:
                t1 = act.do(call(act.e.activation, xh, src, ACT.Copy), *tokens, *x_free[xi])
                fill_in()
                t2 = dve.do(call(dve.e.tensor_tensor, xl, src, f32(xh), ALU.subtract), t1)
            else:
                t1 = act.do(call(act.e.activation, xh, src, ACT.Copy, scale=gain), *tokens, *x_free[xi])
                fill_in()
                t2 = dve.do(call(dve.e.scalar_tensor_tensor, xl, src, gain, f32(xh), ALU.mult, ALU.subtract), t1)
            x_tok[xi][k] = t2
            return t2

        def square_into(k, src, tokens, q=pool):
            if k == 0:
                norm["acc"] = act.do(call(act.e.activation, ACC[:, :], src, ACT.Square), *tokens, norm["acc"],
                                     *norm["readers"])
                return
            b = k % 2
            t = act.do(call(act.e.activation, SQ[:, b, :], src, ACT.Square), *tokens, sq_tok[b])
            t = q.do(call(q.e.tensor_tensor, ACC[:, :], ACC[:, :], SQ[:, b, :], ALU.add), t, norm["acc"],
                     pool.last if q is pool else None)
            sq_tok[b] = t
            norm["acc"] = t

        nt_free = [[], [], []]

        def newton(y, y0, x, tok, tmp):
            t = dve.do(call(dve.e.tensor_tensor, tmp, y0, y0, ALU.mult), tok)
            t = dve.do(call(dve.e.tensor_tensor, tmp, tmp, x, ALU.mult), t)
            t = dve.do(call(dve.e.tensor_scalar, tmp, tmp, -0.5, 1.5, op0=ALU.mult, op1=ALU.add), t)
            return dve.do(call(dve.e.tensor_tensor, y, tmp, y0, ALU.mult), t)

        def rstd_bcast(bank, mean=1024):
            i = norm["rb"] = 1 - norm["rb"]
            o = PS[:, bank, 0:256]
            t = pe.do(call(pe.e.matmul, o, ones, ACC[:, :], start=True, stop=True), norm["acc"], *bank_free[bank])
            norm["readers"] = [t]
            y0, x, tmp = NT[:, 0, :], NT[:, 1, :], NT[:, 2, :]
            t1 = dve.do(call(dve.e.tensor_scalar, x, o, 1.0 / mean, 1e-6, op0=ALU.mult, op1=ALU.add), t, dve.last)
            t2 = act.do(call(act.e.activation, y0, x, ACT.Abs_reciprocal_sqrt), t1)
            bank_free[bank] = [t1]
            norm["t_rb"] = newton(RB[:, i, :], y0, x, t2, tmp)
            return RB[:, i, :], norm["t_rb"]

        def rstd_cols(bank, dst, mean=1024):
            for tt in range(2):
                o = PS[:, bank, tt:tt + 1]
                t = pe.do(call(pe.e.matmul, o, ACC[:, 128 * tt:128 * tt + 128], ones[:, 0:1], start=True,
                                                         stop=True, skip_group_check=True),
                          norm["acc"], *bank_free[bank])
            norm["readers"] = [t]
            x, y0, tmp = ST[:, 0, 0:2], ST[:, 0, 2:4], ST[:, 0, 4:6]
            t1 = dve.do(call(dve.e.tensor_scalar, x, PS[:, bank, 0:2], 1.0 / mean, 1e-6, op0=ALU.mult, op1=ALU.add),
                        t, dve.last)
            bank_free[bank] = [t1]
            t2 = act.do(call(act.e.activation, y0, x, ACT.Abs_reciprocal_sqrt), t1)
            norm["t_rc"] = newton(dst, y0, x, t2, tmp)
            return norm["t_rc"]

        def cols_of_rb(bank, rb, t_rb):
            for tt in range(2):
                o = PS[:, bank, 128 * tt:128 * tt + 128]
                t = pe.do(call(pe.e.transpose, o, rb[:, 128 * tt:128 * tt + 128], ident), t_rb,
                          *bank_free[bank])
            src = PS[:, bank, 0:256].rearrange("p (a b) -> p a b", a=2)[:, :, 0:1]
            dst = RC[:, 0, :].unsqueeze(2)
            t = dve.do(call(dve.e.tensor_copy, dst, src), t, dve.last)
            bank_free[bank] = [t]
            return t

        def add_residual(k, o, t, bank_release=None):
            t1 = dve.do(call(dve.e.tensor_tensor, H[:, k, :], o, H[:, k, :], ALU.add), t, h_tok[k])
            h_tok[k] = t1
            return t1

        def new_h(k, gain, split=True):
            if split:
                split_into(0, k, H[:, k, :], [h_tok[k]], gain)
            square_into(k, H[:, k, :], [h_tok[k]])

        def out_begin(ks, banks):
            outs = [PS[:, b, 256 * h:256 * h + 256] for b in banks for h in range(2)]
            tokens, steps = grid(1, ks, outs, x_tok[1], (True, False, True, False))

            def go():
                for b in banks:
                    pe.wait(*bank_free[b])
                for _ in steps:
                    first["n"] += 1
                    yield
            first = dict(ks=ks, outs=outs, tokens=tokens, steps=go(), banks=banks, n=0)
            return first

        def out_proj(first, banks, evict):
            ks, b4 = first["ks"], banks[0]
            while first["n"] < len(ks) - 1:
                next(first["steps"])
                if first["n"] % 2 == 0:
                    refill(1)
            pe.wait(*bank_free[b4])
            t4, fifth = grid(1, ks, [PS[:, b4, 0:256]], x_tok[1])
            for _ in range(len(ks) - 1):
                next(fifth)
            refill(1)
            for steps in (first["steps"], fifth):
                for _ in steps:
                    pass
            for m in range(8):
                if m < 4:
                    o, t, b = first["outs"][m], first["tokens"][m | 1], first["banks"][m // 2]
                elif m == 4:
                    o, t, b = PS[:, b4, 0:256], t4[0], b4
                else:
                    b = banks[m % len(banks)]
                    pe.wait(*bank_free[b])
                    o = PS[:, b, 0:256]
                    t = mtile(1, ks, o, x_tok[1])
                if m == 7:
                    done_with(1, t)
                t1 = add_residual(m, o, t)
                bank_free[b] = [t1]
                evict(m)
                if m >= 0:
                    refill(1 if m < 7 else 2)

        def ffn_input(i):
            return lambda m: new_h(m, prm("norm_ffn", 8 * i + m))

        def ffn(i, next_gain, hook=None):
            def temp(b, o):
                return SCR[:, 512 * o + 256 * b:512 * o + 256 * b + 256]

            rb = t_rb = None
            acts = {}
            down_tok = {}
            g_free = [[], [], []]

            def gate_up(fs):
                bs = [next_bank((0, 1, 2, 3)) for _ in fs]
                for b in bs:
                    pe.wait(*bank_free[b])
                tokens, steps = grid(0, range(8), [PS[:, b, 256 * i:256 * i + 256] for b in bs for i in range(2)], x_tok[0],
                                     (True, False) * len(fs))
                for _ in steps:
                    pass
                return [(b, tokens[2 * i + 1]) for i, b in enumerate(bs)]

            def chain(f, b, tu):
                p = f % 2
                t1, sg, t2 = temp(p, 0), temp(p, 1), temp(p, 2)
                ta = dve.do(call(dve.e.tensor_tensor, t1, PS[:, b, 0:256], rb, ALU.mult), tu, t_rb)
                ts = act.do(call(act.e.activation, sg, t1, ACT.Silu), ta)
                tb = dve.do(call(dve.e.tensor_tensor, t2, PS[:, b, 256:512], rb, ALU.mult))
                bank_free[b] = [tb]
                if f < 21:
                    fill_in()
                tc = dve.do(call(dve.e.tensor_tensor, t2, sg, t2, ALU.mult), ts, tb)
                s = f % 3
                th = act.do(call(act.e.activation, GH[:, s, :], t2, ACT.Copy), tc, *g_free[s])
                prep_high()
                if f < 21:
                    fill_in()
                acts[f] = dve.do(call(dve.e.tensor_tensor, GL[:, s, :], t2, f32(GH[:, s, :]), ALU.subtract), th)

            def down(fs):
                base = st["x"]
                for f in fs:
                    pe.wait(acts[f])
                for d in range(8):
                    bank = 4 + d // 2
                    o = PS[:, bank, 256 * (d % 2):256 * (d % 2) + 256]
                    if fs[0] == 0 and d % 2 == 0:
                        pe.wait(*bank_free[bank])
                    for j, f in enumerate(fs):
                        x = base + 1024 * j + 128 * d
                        wh, wl = weights(x, 128)
                        last = f == 21
                        full = ends_block(x, 128)
                        t = three(o, wh, wl, GH[:, f % 3, :], GL[:, f % 3, :], f == 0 and d % 2 == 0, last, last or full)
                        if full:
                            release(x, t)
                            g_free[f % 3] = [t]
                    if fs[-1] == 21:
                        down_tok[d] = t
                st["x"] += 1024 * len(fs)

            for f in range(22):
                if f == 0:
                    first = gate_up((0, 1))
                    rb, t_rb = rstd_bcast(7)
                    refill()
                b, tu = first[f] if f < 2 else gate_up((f,))[0]
                if f == 21:
                    done_with(0, tu)
                if f >= 3:
                    down([f - 3])
                if hook:
                    hook(f)
                chain(f, b, tu)
                refill(3)
            down([19])
            down([20, 21])
            for d in range(8):
                bank = 4 + d // 2
                o = PS[:, bank, 256 * (d % 2):256 * (d % 2) + 256]
                t1 = add_residual(d, o, down_tok[d | 1])
                bank_free[bank] = [t1]
                if next_gain is not None:
                    new_h(d, prm(*next_gain(d)))
                else:
                    new_h(d, None, split=False)
            refill(4)

        def attention(n, unit, P_at, PT_at, width, finish, causal=True, sb=(2, 3), tb=(4, 5), ob=(6, 7), fill=None,
                      free=None):
            heads = len(unit(0)["heads"])
            NP = 3
            n0, n1 = (128, 256) if causal else (256, 256)
            sbank = lambda u, h: sb[(heads * u + h) % len(sb)]
            tbank = lambda u, h: tb[(heads * u + h) % len(tb)]
            obank = lambda j: ob[j % len(ob)]
            fill = fill or (lambda s, i: None)
            places = lambda at, n: at if isinstance(at, list) else [SCR[:, at + width * i:at + width * i + width] for i in range(n)]
            P, PT = places(P_at, NP * heads), places(PT_at, 2 * heads)
            Pb = lambda u, h: P[(u % NP) * heads + h]
            Tb = lambda u, h: PT[(u % 2) * heads + h]
            tok = {}
            free = lasts() if free is None else free
            p_free, t_free = [free] * NP, [free] * 2

            def A(u):
                hs = unit(u)["heads"]
                n = len(hs[0]["score"])
                for h, hd in enumerate(hs):
                    pe.wait(*bank_free[sbank(u, h)], *hd.get("wait", ()))
                for i in range(n):
                    for h, hd in enumerate(hs):
                        x, nn, l, r, s0, s1 = hd["score"][i]
                        f = call(pe.e.matmul, PS[:, sbank(u, h), x:x + nn], l, r, start=s0, stop=s1,
                                 skip_group_check=True)
                        if i == n - 1:
                            tok["A", u, h] = pe.do(f)
                        else:
                            pe.run(f)

            def B(u):
                w = unit(u)
                for h, hd in enumerate(w["heads"]):
                    b = sbank(u, h)
                    p = Pb(u, h)
                    nb = ST[:, u % 4, 2 * h:2 * h + 2]
                    for q, (x, nn) in enumerate(((0, n0), (n0, n1))):
                        mask = cst("mask", nn, 384 - nn) if causal else cst("mask", nn)
                        sc = hd["scale"][q] if hd["scale"] is not None else -1.0
                        t = dve.do(call(dve.e.tensor_tensor_reduce, 
                            out=p[:, x:x + nn], in0=PS[:, b, x:x + nn], in1=mask, scale=sc, scalar=3e38,
                            op0=ALU.add, op1=ALU.min, accum_out=nb[:, q:q + 1]),
                            tok["A", u, h], *p_free[u % NP])
                    tok["B", u, h] = t
                    bank_free[b] = [t]

            def C(u):
                w = unit(u)
                for h, hd in enumerate(w["heads"]):
                    p = Pb(u, h)
                    for q, (x, nn) in enumerate(((0, n0), (n0, n1))):
                        t = act.do(call(act.e.activation, 
                            p[:, x:x + nn], p[:, x:x + nn], ACT.Exp, scale=-1.0,
                            bias=ST[:, u % 4, 2 * h + q:2 * h + q + 1],
                            accum_out=ST[:, u % 4, 8 + 2 * h + q:9 + 2 * h + q]), tok["B", u, h])
                    tok["C", u, h] = t

            def D(u):
                w = unit(u)
                t = dve.do(call(dve.e.reciprocal, ST[:, u % 4, 16:16 + 2 * heads], ST[:, u % 4, 8:8 + 2 * heads]),
                           *[tok["C", u, h] for h in range(heads)])
                for h, hd in enumerate(w["heads"]):
                    p, g = Pb(u, h), hd["gate"]
                    for q, (x, nn) in enumerate(((0, n0), (n0, n1))):
                        r = ST[:, u % 4, 16 + 2 * h + q:17 + 2 * h + q]
                        if g is None:
                            f = call(dve.e.tensor_scalar, p[:, x:x + nn], p[:, x:x + nn], r, None, op0=ALU.mult)
                        else:
                            f = call(dve.e.tensor_scalar, p[:, x:x + nn], p[:, x:x + nn], g[:, q:q + 1], r, op0=ALU.mult,
                                     op1=ALU.mult)
                        t2 = dve.do(f, t)
                    tok["D", u, h] = t2

            def E(u):
                order = (0, 1, 2) if causal else (0, 2, 1, 3)
                for h in range(heads):
                    b = tbank(u, h)
                    pe.wait(*bank_free[b])
                    p = Pb(u, h)
                    for i, x in enumerate(order):
                        f = call(pe.e.transpose, PS[:, b, 128 * x:128 * x + 128],
                                                                      p[:, 128 * i:128 * i + 128], ident)
                        if i == len(order) - 1:
                            t = pe.do(f, tok["D", u, h])
                        else:
                            pe.run(f, tok["D", u, h])
                    tok["E", u, h] = t
                p_free[u % NP] = [t]

            def F(u):
                for h in range(heads):
                    b = tbank(u, h)
                    d = Tb(u, h)
                    q = act if heads == 2 or u % 2 == 0 else dve
                    w = width
                    if q is act:
                        t = act.do(call(act.e.activation, d, PS[:, b, 0:w], ACT.Copy), tok["E", u, h],
                                   *t_free[u % 2])
                    else:
                        t = dve.do(call(dve.e.tensor_copy, d, PS[:, b, 0:w]), tok["E", u, h], *t_free[u % 2])
                    bank_free[b] = [t]
                    tok["F", u, h] = t

            def G(u):
                w = unit(u)
                b = obank(w["o"])
                if w["first"]:
                    pe.wait(*bank_free[b])
                if w["extra"]:
                    w["extra"](b)
                for h in range(heads):
                    pe.wait(tok["F", u, h])
                for kb in range(2):
                    for h, hd in enumerate(w["heads"]):
                        rows = slice(0, 128) if heads == 1 else slice(64 * h, 64 * h + 64)
                        q0 = 128 if (causal and kb) else 0
                        x = 256 * kb
                        v = hd["v"][kb]
                        start = w["first"] and kb == 0
                        f = call(pe.e.matmul, 
                            PS[rows, b, q0:256], v, Tb(u, h)[:, x:x + 256 - q0], start=start,
                            stop=w["last"] and kb == 1, skip_group_check=True)
                        t = pe.do(f)
                t_free[u % 2] = [t]
                if w["last"]:
                    finished.append((w["o"], b, t))

            finished = []

            def end_units():
                while finished:
                    finish(*finished.pop(0))

            for s in range(n + 3):
                if 0 <= s - 1 < n:
                    C(s - 1)
                if 0 <= s - 2 < n:
                    D(s - 2)
                if s < n:
                    A(s)
                    B(s)
                end_units()
                fill(s, 0)
                if 0 <= s - 2 < n:
                    E(s - 2)
                fill(s, 1)
                if 0 <= s - 2 < n:
                    F(s - 2)
                if 0 <= s - 3 < n:
                    G(s - 3)
                fill(s, 2)
            end_units()

        def o_split(base=0):
            def finish(j, b, t):
                o = PS[:, b, 0:256]
                bank_free[b] = [split_into(1, base + j, o, [t])]
            return finish

        nsa_done = []

        def nsa(j):
            ctr = [0]

            def alloc(n):
                ctr[0] += n
                return ctr[0] - n
            q_at, ks_at, kw_at = alloc(2048), alloc(512), alloc(512)
            kc_at, v_at, gate_at = alloc(64), alloc(1024), alloc(192)
            hid_at, hk_at, hv_at, vc_at = alloc(256), alloc(128), alloc(256), alloc(512)
            pc_at, pp_at, pct_at = alloc(512), alloc(1024), alloc(1024)
            tmp_at = alloc(128)
            un_at = alloc(3840)
            c_at, blk_at = un_at, un_at + 1024
            P_at, PT_at = un_at, un_at + 2304
            assert ctr[0] <= 13056, ctr
            Q = SCR[:, q_at:q_at + 2048].rearrange("p (j t) -> p j t", j=8)
            K = [SCR[:, x:x + 512].rearrange("p (g t) -> p g t", g=2) for x in (ks_at, kw_at)]
            KC = SCR[:, kc_at:kc_at + 64].rearrange("p (g c) -> p g c", g=4)
            V = SCR[:, v_at:v_at + 1024].rearrange("p (b t d) -> p b t d", b=2, t=2)
            GA = SCR[:, gate_at:gate_at + 96].rearrange("p (t c) -> p t c", t=2)
            GB = SCR[:, gate_at + 96:gate_at + 192].rearrange("p (t c) -> p t c", t=2)
            C = SCR[:, c_at:c_at + 1024].rearrange("p (i t) -> p i t", i=4)
            BLK = SCR[:, blk_at:blk_at + 1920].rearrange("p (v i g c) -> p v i g c", v=2, i=16, g=4)
            HID = SCR[:, hid_at:hid_at + 256]
            HK = SCR[:, hk_at:hk_at + 128].rearrange("p (k g c) -> p k g c", k=2, g=4)
            HV = SCR[:, hv_at:hv_at + 256].rearrange("p (k g c) -> p k g c", k=2, g=4)
            VC = SCR[:, vc_at:vc_at + 512].rearrange("p (n c) -> p n c", n=4)
            PC = SCR[:, pc_at:pc_at + 512].rearrange("p (n c) -> p n c", n=32)
            PP = SCR[:, pp_at:pp_at + 1024].rearrange("p (n c) -> p n c", n=32)
            PCT = SCR[:, pct_at:pct_at + 1024].rearrange("p (n t) -> p n t", n=4)
            TMP = SCR[:, tmp_at:tmp_at + 128]

            prior = lasts()
            tz = None
            for ap in (SCR[:, kc_at:kc_at + 64], SCR[:, hid_at:hid_at + 256 + 128 + 256 + 512],
                       SCR[:, pp_at:pp_at + 1024]):
                tz = pool.do(call(pool.e.memset, ap, 0.0), pool.last, *prior)

            c_tok = [None] * 4
            ts = group(0, range(8), (0, 1, 2, 3), x_tok[0])
            constants()
            rb, t_rb = rstd_bcast(7)
            refill(1)
            for i in range(4):
                c_tok[i] = dve.do(call(dve.e.tensor_tensor, C[:, i, :], PS[:, i, 0:256], rb, ALU.mult), ts[i], t_rb, *prior)
                bank_free[i] = [c_tok[i]]
                refill(1 if i else 3)
            blk_tok = {}
            for q in (pool, dve):
                q.wait(t_cmp[j])
            for v in range(2):
                for g in range(4):
                    eng = pool if v and g < 3 else dve
                    rows = slice(64 * (g % 2), 64 * (g % 2) + 64)
                    for jj in range(2):
                        full = C[rows, 2 * v + g // 2, 0:256].rearrange("p (c i) -> p i c", i=16)
                        for half in range(2):
                            s2 = full[:, jj::2, half:half + 15]
                            x = 32 * v + 16 * jj + 8 * half
                            pos = CMP[rows, x:x + 8].unsqueeze(2).broadcast_to([64, 8, 15])
                            dst = BLK[64 * jj:64 * jj + 64, v, 8 * half:8 * half + 8, g, :]
                            blk_tok[v, eng.sem.name] = eng.do(
                                call(eng.e.tensor_tensor, dst, s2, pos, ALU.add), c_tok[2 * v + g // 2],
                                *([pool.last] if eng is pool else []), *prior)
            k_tok = {}
            for i in range(4):
                b = (4, 5, 0, 1)[i]
                pe.wait(*bank_free[b])
                t = mtile(0, range(8), PS[:, b, 0:256], x_tok[0])
                br = i // 2
                k_tok[br, i % 2] = dve.do(call(dve.e.tensor_tensor, K[br][:, i % 2, :], PS[:, b, 0:256], rb, ALU.mult), t,
                                          *prior)
                bank_free[b] = [k_tok[br, i % 2]]
                if i == 1:
                    t_rc = cols_of_rb(7, rb, t_rb)
                refill()
            q_tok = [None] * 8

            def query_halves(i, b):
                pe.wait(*bank_free[b])
                o = PS[:, b, 0:256]
                ts, steps = grid(0, range(8), [o], x_tok[0])
                for _ in range(4):
                    next(steps)
                yield
                for _ in steps:
                    pass
                fill_in()
                q_tok[i] = dve.do(call(dve.e.scalar_tensor_tensor, Q[:, i, :], o, 0.125, rb, ALU.mult, ALU.mult), ts[0])
                bank_free[b] = [q_tok[i]]
                if i != 4:
                    refill()
                if i == 7:
                    done_with(0, ts[0])

            def query(i, b):
                for _ in query_halves(i, b):
                    pass

            query(0, 2)
            pe.wait(*blk_tok.values(), *bank_free[6])
            for n in range(8):
                u, w, loaded = next_raw()
                w = w.rearrange("p (i v c) -> p i v c", i=2, v=2)
                pe.wait(loaded)
                for ii in range(2):
                    for v in range(2):
                        i = 2 * n + ii
                        l = BLK[:, v, i, :, :].rearrange("p g c -> p (g c)")
                        t = pe.do(call(pe.e.matmul, PS[64 * v:64 * v + 60, 6, 0:256], l, w[:, ii, v, :], start=i == 0,
                                       stop=i == 15, skip_group_check=True))
                give_back(u, [t])
            for v in range(2):
                ht = act.do(call(act.e.activation, HID[64 * v:64 * v + 60, :], PS[64 * v:64 * v + 60, 6, 0:256],
                                 ACT.Gelu_apprx_tanh), t, tz)
            bank_free[6] = [ht]
            query(1, 3)
            for x in range(2):
                t2 = pe.do(call(pe.e.transpose, PS[:, 6, 128 * x:128 * x + 128], HID[:, 128 * x:128 * x + 128], ident),
                           ht, *bank_free[6])
            src = PS[:, 6, 0:256].rearrange("p (k n) -> p k n", k=2)
            t3 = dve.do(call(dve.e.tensor_copy, HK[:, :, :, 0:15],
                             src[:, :, 0:60].rearrange("p k (g c) -> p k g c", g=4)), t2, tz)
            t4 = dve.do(call(dve.e.tensor_copy, HV[:, :, :, 0:15],
                             src[:, :, 64:124].rearrange("p k (g c) -> p k g c", g=4)), t2)
            bank_free[6] = [t4]
            query(2, 4)
            w2 = lambda v, k: CMP[:, 64 + 128 * v + 64 * k:128 + 128 * v + 64 * k]
            pe.wait(t_cmp[j], t4, *bank_free[6], *bank_free[7])
            for hh in range(2):
                for k in range(2):
                    t5 = pe.do(call(pe.e.matmul, PS[64 * hh:64 * hh + 64, 6, 0:64], w2(0, k),
                                    HK[:, k, :, :].rearrange("p g c -> p (g c)"), start=k == 0, stop=k == 1,
                                    skip_group_check=True))
            for k in range(2):
                t6 = pe.do(call(pe.e.matmul, PS[:, 7, 0:64], HV[:, k, :, :].rearrange("p g c -> p (g c)"), w2(1, k),
                                start=k == 0, stop=k == 1))
            kc = PS[:, 6, 0:64].rearrange("p (g c) -> p g c", g=4)
            for hh in range(2):
                rows = slice(64 * hh, 64 * hh + 64)
                t_kc = dve.do(call(dve.e.tensor_copy, KC[rows, hh::2, 0:15], kc[rows, hh::2, 0:15]), t5, tz)
            bank_free[6] = [t_kc]
            for pg in range(2):
                for aa in range(2):
                    for hh in range(2):
                        g, d0 = 2 * pg + hh, 64 * aa + 32 * hh
                        t_vc = act.do(call(act.e.activation, VC[d0:d0 + 32, 2 * pg + aa, 64 * hh:64 * hh + 64],
                                           PS[32 * g:32 * g + 32, 7, 0:64], ACT.Copy), t6, tz)
            bank_free[7] = [t_vc]
            query(3, 5)
            t_pct = [None] * 2

            def compressed(pg, b):
                tmp = TMP[:, 64 * pg:64 * pg + 64]
                pe.wait(*bank_free[b], t_kc)
                for tt in range(2):
                    for i in range(4):
                        pr = 4 * pg + i
                        r = KC[:, 2 * pg:2 * pg + 2, :].rearrange("p g c -> p (g c)")
                        x = 128 * tt + 32 * i
                        t = pe.do(call(pe.e.matmul, PS[:, b, x:x + 32], Q[:, pr, 128 * tt:128 * tt + 128], r, start=True,
                                       stop=True, skip_group_check=True), q_tok[pr])
                yield
                sc = PS[:, b, 0:256].rearrange("p (t n c) -> p t n c", t=2, n=8)
                p4 = PC[:, 16 * pg:16 * pg + 16, :].rearrange("p (t n) c -> p t n c", t=2)
                pc = PC[:, 16 * pg:16 * pg + 16, :]
                cm = cst("cmask", 32).rearrange("p (t c) -> p t c", t=2).unsqueeze(2).broadcast_to([128, 2, 8, 16])
                mx, sm = tmp[:, 0:16], tmp[:, 16:32]
                bc = lambda ap: ap.unsqueeze(2).broadcast_to([128, 16, 16])
                t2 = dve.do(call(dve.e.tensor_tensor, p4, sc, cm, ALU.add), t, *prior)
                bank_free[b] = [t2]
                t2 = chain(dve, t2, call(dve.e.tensor_reduce, mx, pc, AX.X, ALU.max),
                           call(dve.e.tensor_scalar, mx, mx, -1e29, None, op0=ALU.max))
                t2 = pool.do(call(pool.e.tensor_tensor, pc, pc, bc(mx), ALU.subtract), t2, pool.last)
                t3 = act.do(call(act.e.activation, pc, pc, ACT.Exp), t2)
                yield
                t3 = chain(dve, t3, call(dve.e.tensor_reduce, sm, pc, AX.X, ALU.add),
                           call(dve.e.tensor_scalar, sm, sm, 1e-30, None, op0=ALU.max),
                           call(dve.e.reciprocal, mx, sm))
                for tt in range(2):
                    m4 = tmp[:, 8 * tt:8 * tt + 8].rearrange("p (r h) -> p r h", r=4)
                    g4 = GA[:, tt, 8 * pg:8 * pg + 8].rearrange("p (h r) -> p r h", h=2)
                    t4 = dve.do(call(dve.e.tensor_tensor, m4, m4, g4, ALU.mult), t3, t_g)
                t_pp = pool.do(call(pool.e.tensor_tensor, PP[:, 16 * pg:16 * pg + 16, 0:16], pc, bc(mx), ALU.mult), t4,
                               pool.last, tz)
                yield
                pe.wait(*bank_free[b])
                for cc in range(2):
                    for tt in range(2):
                        n = 16 * pg + 8 * tt + 4 * cc
                        src = PP[:, n:n + 4, :].rearrange("p n c -> p (n c)")
                        t = pe.do(call(pe.e.transpose, PS[:, b, 256 * cc + 128 * tt:256 * cc + 128 * tt + 128], src, ident),
                                  t_pp)
                yield
                dst = PCT[:, 2 * pg:2 * pg + 2, :].rearrange("p n t -> p (n t)")
                t_pct[pg] = act.do(call(act.e.activation, dst, PS[:, b, :], ACT.Copy), t, *prior)
                bank_free[b] = [t_pct[pg]]
                yield

            for br, (cols, per) in enumerate(((304, 3), (256, 4))):
                bb = (0, 1) if br == 0 else (2, 3)
                pe.wait(*bank_free[bb[0]], *bank_free[bb[1]])
                t = vtile(0, range(8), cols, per, bb, x_tok[0])
                for tt in range(2):
                    if br == 0:
                        tg = act.do(call(act.e.activation, GB[:, tt, :], PS[:, bb[tt], 256:304], ACT.Copy,
                                         scale=RC[:, 0, tt:tt + 1]), t, t_rc, *prior)
                    v_tok = act.do(call(act.e.activation, V[:, br, tt, :], PS[:, bb[tt], 0:256], ACT.Copy,
                                        scale=RC[:, 0, tt:tt + 1]), t, t_rc, *prior)
                    bank_free[bb[tt]] = [v_tok]
                if br == 0:
                    t1 = act.do(call(act.e.activation, GB[:, :, :], GB[:, :, :], ACT.Exp, scale=-1.0), tg)
                    t1 = dve.do(call(dve.e.tensor_scalar, GB[:, :, :], GB[:, :, :], 1.0, None, op0=ALU.add), t1)
                    t_g = dve.do(call(dve.e.reciprocal, GA[:, :, :], GB[:, :, :]), t1)
                refill()
            out, later, halves_of = [], [], []

            def fill(s, i):
                if i == 0 and s == 0:
                    later.append(compressed(0, 7))
                if i == 2 and s == 2:
                    pe.wait(v_tok)
                if i == 1 and s < 4 or i == 0 and s == 4:
                    next(later[0])
                if i == 0 and s < 8:
                    if s % 2 == 0:
                        halves_of.append(query_halves(4 + s // 2, 3))
                    next(halves_of[-1], None)
                if i == 2 and s == 7:
                    fill_in()
                if i == 0 and s == 8:
                    later.append(compressed(1, 3))
                if (s, i) in ((8, 0), (8, 1), (10, 1), (11, 1), (12, 1)):
                    next(later[1])
                if i == 2 and s == 15:
                    out.append(out_begin(range(8), (0, 1)))
                if s >= 16:
                    for _ in range(((2, 1, 2), (1, 0, 0), (1, 0, 0))[s - 16][i]):
                        next(out[0]["steps"])

            def unit(u):
                pr, br = u // 2, u % 2
                pg, r = pr // 4, pr % 4

                def extra(b):
                    l, rr = VC[:, 2 * pg + pr % 2, :], PCT[:, pr // 2, :]
                    pe.run(call(pe.e.matmul, PS[:, b, 0:256], l, rr, start=False, stop=False, skip_group_check=True),
                           t_pct[pg], t_vc)
                heads = []
                for h in range(2):
                    g = 2 * pg + h
                    col = 16 * (1 + br) + 4 * g + r
                    rows = slice(64 * h, 64 * h + 64)
                    heads.append(dict(
                        score=[(0, 128, Q[rows, pr, 0:128], K[br][rows, pg, 0:128], True, True),
                               (128, 256, Q[rows, pr, 128:256], K[br][rows, pg, :], True, True)],
                        wait=(q_tok[pr], k_tok[br, pg]), scale=None, gate=GA[:, :, col],
                        v=[V[:, br, kb, 64 * g:64 * g + 64] for kb in range(2)]))
                return dict(heads=heads, o=pr, first=br == 0, last=br == 1, extra=extra if br == 1 else None)
            dve.wait(t_g)
            attention(16, unit, P_at, PT_at, 384, o_split(), sb=(0, 1, 2), fill=fill)
            nsa_done[:] = lasts()
            return out[0], (2, 3, 4, 5)

        def moba():
            Q = SCR[:, 0:2048].rearrange("p (j t) -> p j t", j=8)
            K = SCR[:, 2048:4096].rearrange("p (j t) -> p j t", j=8)
            V = SCR[:, 6144:8192].rearrange("p (t c) -> p t c", t=2)
            prior = lasts()
            q_tok, k_tok = [None] * 8, [None] * 8
            vts, steps = vtiles(0, range(8), (0, 2))
            next(steps)
            refill()
            next(steps)
            rb, t_rb = rstd_bcast(7)
            refill()
            next(steps)
            refill()
            next(steps)
            t_rc = cols_of_rb(6, rb, t_rb)
            refill()

            def proj(j, kind):
                b = kind if j else 4 + kind
                pe.wait(*bank_free[b])
                o = PS[:, b, 0:256]
                t = mtile(0, range(8), o, x_tok[0])
                fill_in()
                if kind == 0:
                    q_tok[j] = dve.do(call(dve.e.scalar_tensor_tensor, Q[:, j, :], o, 0.125, rb, ALU.mult, ALU.mult), t,
                                      t_rb, *prior)
                    bank_free[b] = [q_tok[j]]
                else:
                    k_tok[j] = dve.do(call(dve.e.tensor_tensor, K[:, j, :], o, rb, ALU.mult), t, t_rb, *prior)
                    bank_free[b] = [k_tok[j]]
                    if j == 7:
                        done_with(0, t)
                refill()
            for n in range(2):
                for tt in range(2):
                    b = 2 * n + tt
                    v_tok = act.do(call(act.e.activation, V[:, tt, 512 * n:512 * n + 512], PS[:, b, :], ACT.Copy,
                                        scale=RC[:, 0, tt:tt + 1]), vts[n], t_rc, *prior)
                    bank_free[b] = [v_tok]
            proj(0, 0)
            proj(0, 1)
            proj(1, 0)
            out = []

            def fill(s, i):
                if s < 7 and i < 2 and s + 1 + i < 8:
                    proj(s + 1 + i, 1 - i)
                if s == 7 and i == 2:
                    out.append(out_begin(range(8), (0, 1)))
                if s >= 8:
                    for _ in range(((2, 1, 1), (1, 1, 0), (1, 0, 0))[s - 8][i]):
                        next(out[0]["steps"])

            def unit(u):
                rows = lambda ap, h: ap[64 * h:64 * h + 64]
                heads = [dict(score=[(0, 128, rows(Q[:, u, 0:128], h), rows(K[:, u, 0:128], h), True, True),
                                     (128, 256, rows(Q[:, u, 128:256], h), rows(K[:, u, :], h), True, True)],
                              wait=(q_tok[u], k_tok[u]), scale=None, gate=None,
                              v=[V[:, kb, 128 * u + 64 * h:128 * u + 64 * h + 64] for kb in range(2)]) for h in range(2)]
                return dict(heads=heads, o=u, first=True, last=True, extra=None)
            attention(8, unit, 8192, 8192 + 2304, 384, o_split(), fill=fill)
            return out[0], (4, 5, 6, 7)

        def conv():
            prior = lasts()
            t_cmp.append(load("s_cmp1", CMP, a["cmp"][1], *nsa_done))
            R2 = SCR[:, 0:256]
            Z = [SCR[:, 256 + 258 * i:256 + 258 * (i + 1)] for i in range(2)]
            Y = [SCR[:, 1024 + 256 * i:1280 + 256 * i] for i in range(2)]
            CC = [SCR[:, 1536 + 256 * i:1792 + 256 * i] for i in range(2)]
            for i in range(2):
                tz = pool.do(call(pool.e.memset, Z[i][:, 0:2], 0.0), pool.last, *prior)
            for d in range(8):
                s = d % 2
                bs = [3 * (d % 2) + i for i in range(3)]
                if d == 0:
                    ts = group(0, range(8), bs, x_tok[0])
                    rb, t_rb = rstd_bcast(7)
                    t_r2 = dve.do(call(dve.e.tensor_tensor, R2, rb, rb, ALU.mult), t_rb, *prior)
                    refill()
                else:
                    ts = []
                    for b in bs:
                        pe.wait(*bank_free[b])
                        ts.append(mtile(0, range(8), PS[:, b, 0:256], x_tok[0]))
                        refill(1)
                if d == 7:
                    out = [out_begin(range(8), (6, 7))]
                    for _ in range(6):
                        next(out[0]["steps"])
                c_, u_, b_ = (PS[:, x, 0:256] for x in bs)
                w = lambda i: prm("conv_w", 3 * d + i)
                z, y, cc = Z[s], Y[s], CC[s]
                t = dve.do(call(dve.e.tensor_tensor, cc, c_, R2, ALU.mult), ts[0], t_r2, dve.last)
                bank_free[bs[0]] = [t]
                t = dve.do(call(dve.e.tensor_tensor, z[:, 2:258], u_, cc, ALU.mult), ts[1], t, tz)
                bank_free[bs[1]] = [t]
                t = dve.do(call(dve.e.tensor_scalar, y, z[:, 0:256], w(0), None, op0=ALU.mult), t)
                t = dve.do(call(dve.e.scalar_tensor_tensor, y, z[:, 1:257], w(1), y, ALU.mult, ALU.add), t)
                t = dve.do(call(dve.e.scalar_tensor_tensor, y, z[:, 2:258], w(2), y, ALU.mult, ALU.add), t)
                t = dve.do(call(dve.e.tensor_tensor, y, y, rb, ALU.mult), t)
                t = dve.do(call(dve.e.tensor_tensor, y, b_, y, ALU.mult), t, ts[2])
                bank_free[bs[2]] = [t]
                if d == 7:
                    done_with(0, ts[2])
                split_into(1, d, y, [t])
                refill()
            return out[0], (0, 1, 2, 3)

        MEMK = SCR[:, 11776:12800].rearrange("p (h t) -> p h t", h=4)
        MEMV = SCR[:, 12800:13824].rearrange("p (t c) -> p t c", t=2)

        def chain(q, t, *ops):
            for op in ops:
                t = q.do(op, t)
            return t

        def inv_sqrt(y, x, t, tmp):
            y0 = tmp[0]
            t = act.do(call(act.e.activation, y0, x, ACT.Abs_reciprocal_sqrt), t)
            return newton(y, y0, x, t, tmp[1])

        def small(at, *shape):
            n = int(np.prod(shape))
            ap = SM[:, at:at + n]
            if len(shape) == 2:
                ap = ap.rearrange("p (a b) -> p a b", a=shape[0])
            return ap

        def squares(dst, src, junk, *tokens):
            return act.do(call(act.e.activation, junk, src, ACT.Square, accum_out=dst), *tokens)

        MT = SCR[:, 8192:10240].rearrange("p (k t) -> p k t", k=8)
        ld = {n: [sem(f"s_{n}"), 0] for n in ("memT", "a_ln", "a_ws", "a_bs")}
        mem = {}

        def load_mem():
            prior = lasts()
            mem["x"] = sp.dma(SCR[:, 8192:10240], a["memT"], ld["memT"], *prior)
            mem["ln"] = sp.dma(SCR[:, 4096:6144], a["a_ln"], ld["a_ln"])
            mem["ws"] = sp.dma(SCR[:, 6144:7168], a["a_ws"], ld["a_ws"])
            mem["bs"] = sp.dma(SCR[:, 7168:8192], a["a_bs"], ld["a_bs"])

        def mem_hook(f):
            k = f - 3
            if 0 <= k < 8:
                split_into(1, k, MT[:, k, :], [mem["x"]], prm("mem_norm", k))
                square_into(k, MT[:, k, :], [mem["x"]])
            if k == 8:
                b = next_bank((0, 1, 2, 3))
                mem["rc"] = rstd_cols(b, RC[:, 1, :])
            if f == 14:
                ws = SCR[:, 6144:7168].rearrange("p (g t) -> p g t", g=8)
                mem["ws"] = pool.do(call(pool.e.affine_select, ws, ws, [[0, 8], [1, 128]], ALU.is_ge, 0.0, base=0,
                                         channel_multiplier=-1), mem["ws"], pool.last)

        def mem_kv():
            prior = lasts()
            kv, steps = vtiles(1, range(8), (0, 2))
            next(steps)
            rb, t_rb = rstd_bcast(7)
            refill()
            next(steps)
            for k in range(8):
                h_tok[k] = dve.do(call(dve.e.scalar_tensor_tensor, H[:, k, :], H[:, k, :], prm("norm_final", k), rb,
                                       ALU.mult, ALU.mult), t_rb, h_tok[k])
                new_h(k, prm("norm1", k))
                refill(1)
            for _ in steps:
                refill(1)
            done_with(1, kv[1])
            for tt in range(2):
                t = act.do(call(act.e.activation, MEMV[:, tt, :], PS[:, 2 + tt, :], ACT.Copy, scale=RC[:, 1, tt:tt + 1]),
                           kv[1], mem["rc"], *prior)
                bank_free[2 + tt] = [t]
            mem["v"] = t
            KM = SCR[:, 2048:3072].rearrange("p (t c) -> p t c", t=2)
            JK = SCR[:, 3072:3200]
            ss, m2, y, t0, t1 = small(0, 2, 4), small(8, 2), small(10, 2, 4), small(18, 8), small(26, 8)
            for tt in range(2):
                for h in range(4):
                    t = squares(ss[:, tt, h:h + 1], PS[:, tt, 128 * h:128 * h + 128], JK, kv[0], act.last, *prior)
            m2b = m2.unsqueeze(2).broadcast_to([128, 2, 4])
            x = small(34, 2, 4)
            t = chain(dve, t, call(dve.e.tensor_tensor, m2, RC[:, 1, :], RC[:, 1, :], ALU.mult),
                      call(dve.e.tensor_tensor, x, ss, m2b, ALU.mult),
                      call(dve.e.tensor_scalar, x, x, 1.0 / 128, 1e-6, op0=ALU.mult, op1=ALU.add))
            t = inv_sqrt(small(10, 8), small(34, 8), t, (t0, t1))
            rb_ = RC[:, 1, :].unsqueeze(2).broadcast_to([128, 2, 4])
            t = dve.do(call(dve.e.tensor_tensor, y, y, rb_, ALU.mult), t)
            for tt in range(2):
                for h in range(4):
                    tk = dve.do(call(dve.e.tensor_scalar, KM[:, tt, 128 * h:128 * h + 128],
                                     PS[:, tt, 128 * h:128 * h + 128], y[:, tt, h:h + 1], None, op0=ALU.mult), t)
            bank_free[0] = bank_free[1] = [tk]
            return KM, tk

        def to_features(src, heads, dst, banks, tokens, gain=None, free=(), engines=(dve, act)):
            out_t = []
            for h in range(heads):
                b = banks[(h // 2) % len(banks)]
                if h % 2 == 0:
                    pe.wait(*bank_free[b])
                for tt in range(2):
                    t = pe.do(call(pe.e.transpose, PS[:, b, 256 * (h % 2) + 128 * tt:256 * (h % 2) + 128 * tt + 128],
                                   src[:, tt, 128 * h:128 * h + 128], ident), *tokens)
                if h % 2:
                    d = dst[:, h - 1:h + 1, :].rearrange("p h t -> p (h t)")
                    if engines[h // 2 % 2] is act:
                        t = act.do(call(act.e.activation, d, PS[:, b, :], ACT.Copy, scale=1.0 if gain is None else gain),
                                   t, *free)
                    else:
                        t = dve.do(call(dve.e.tensor_scalar, d, PS[:, b, :], 1.0 if gain is None else gain, None,
                                        op0=ALU.mult), t, *free)
                    bank_free[b] = [t]
                    out_t.append(t)
            return out_t

        def query_scales(ss, dst, n, c, mean, tokens, at):
            c2 = small(at, 2)
            x = small(at + 2, 2, n)
            xf, y0, tmp = small(at + 2, 2 * n), small(at + 2 + 2 * n, 2 * n), small(at + 2 + 4 * n, 2 * n)
            wide = lambda ap: ap.unsqueeze(2).broadcast_to([128, 2, n])
            t = dve.do(call(dve.e.tensor_tensor, c2, c, c, ALU.mult), *tokens)
            t = chain(dve, t, call(dve.e.tensor_tensor, x, ss, wide(c2), ALU.mult),
                      call(dve.e.tensor_scalar, xf, xf, 1.0 / mean, 1e-6, op0=ALU.mult, op1=ALU.add))
            t = inv_sqrt(xf, xf, t, (y0, tmp))
            t = dve.do(call(dve.e.tensor_scalar, xf, xf, -float(mean) ** -0.5, None, op0=ALU.mult), t)
            return dve.do(call(dve.e.tensor_tensor, dst, x, wide(c), ALU.mult), t)

        def mem_queries(i, banks, vt, QM, QT, tbanks, free):
            g = small(318, 1)
            tg = dve.do(call(dve.e.tensor_tensor, g, prm("mem_qn", i), prm("mem_kn", i), ALU.mult), *free)
            ta = act.do(call(act.e.activation, QM[:, 0, :], PS[:, banks[0], :], ACT.Copy), vt, *free)
            td = dve.do(call(dve.e.tensor_copy, QM[:, 1, :], PS[:, banks[1], :]), vt)
            bank_free[banks[0]], bank_free[banks[1]] = [ta], [td]

            def turned():
                return to_features(QM, 4, QT, tbanks, [ta, td, tg], gain=g)
            return [ta, td], turned

        def mem_scales(QM, JK, tokens, r, t_r, at):
            ss, ns = small(at, 2, 4), small(at + 8, 2, 4)
            for tt in range(2):
                for h in range(4):
                    ts = squares(ss[:, tt, h:h + 1], QM[:, tt, 128 * h:128 * h + 128], JK[:, 0:128], act.last, *tokens)
            return ns, query_scales(ss, ns, 4, r, 128, [ts, t_r], at + 18)

        def mem_attention(QT, tq, ns, tn, P_at, PT_at, fill, **more_):
            def unit(u):
                return dict(heads=[dict(
                    score=[(0, 256, QT[:, u, 0:128], MEMK[:, u, :], True, True),
                           (256, 256, QT[:, u, 128:256], MEMK[:, u, :], True, True)],
                    wait=(*tq, *mem["k"]), scale=(ns[:, 0, u:u + 1], ns[:, 1, u:u + 1]), gate=None,
                    v=[MEMV[:, kb, 128 * u:128 * u + 128] for kb in range(2)])], o=u, first=True, last=True, extra=None)
            pe.wait(mem["v"])
            dve.wait(tn)
            attention(4, unit, P_at, PT_at, 512, o_split(8), causal=False, fill=fill, **more_)

        MEM_FIRST = (8, 9, 10, 11, 0, 1, 2, 3, 4, 5, 6, 7)

        def gmlp(KM, t_km):
            VV = SCR[:, 0:2048].rearrange("p (t c) -> p t c", t=2)
            U = SCR[:, 2048:4096].rearrange("p (k t) -> p k t", k=8)
            LNG, LNB = SCR[:, 4096:5120], SCR[:, 5120:6144]
            WS = SCR[:, 6144:7168].rearrange("p (g t) -> p g t", g=8)
            BS = SCR[:, 7168:8192].rearrange("p (g t) -> p g t", g=8)
            QM = SCR[:, 8192:9216].rearrange("p (t c) -> p t c", t=2)
            QT = SCR[:, 9216:10240].rearrange("p (h t) -> p h t", h=4)
            JK = SCR[:, 10240:10752]
            prior = lasts()
            lend_once("av0", prior)
            vs, steps = vtiles(0, range(8), (4, 6))
            next(steps)
            refill()
            rb, t_rb = rstd_bcast(2)
            next(steps)
            refill()
            next(steps)
            mem["k"] = to_features(KM, 4, MEMK, (0, 1), [t_km], free=prior)
            refill()
            next(steps)
            t_rc = cols_of_rb(3, rb, t_rb)
            refill()
            for n in range(2):
                for tt in range(2):
                    b = 4 + 2 * n + tt
                    tv = act.do(call(act.e.activation, VV[:, tt, 512 * n:512 * n + 512], PS[:, b, :], ACT.Gelu,
                                     scale=RC[:, 0, tt:tt + 1]), vs[n], t_rc, *prior)
                    bank_free[b] = [tv]
            refill()
            pe.wait(*bank_free[0], *bank_free[1])
            vt = vtile(0, range(8), 512, 2, (0, 1), x_tok[0])
            s6, mv = small(64, 2, 12), small(88, 2, 2)
            for tt in range(2):
                for n in range(2):
                    t = dve.do(call(dve.e.bn_stats, s6[:, tt, 6 * n:6 * n + 6], VV[:, tt, 512 * n:512 * n + 512]), tv)
            for tt in range(2):
                t = dve.do(call(dve.e.bn_aggr, mv[:, tt, :], s6[:, tt, :]), t)
            x, y0, tmp = small(96, 2), small(98, 2), small(100, 2)
            t = dve.do(call(dve.e.tensor_scalar, x.unsqueeze(2), mv[:, :, 1:2], 1e-6, None, op0=ALU.add), t)
            fill_in()
            t_ln = inv_sqrt(x, x, t, (y0, tmp))
            pool.wait(mem["ln"])
            t_vn = []

            def layer_norm(tt):
                v = VV[:, tt, :]
                t = dve.do(call(dve.e.tensor_scalar, v, v, mv[:, tt, 0:1], x[:, tt:tt + 1], op0=ALU.subtract, op1=ALU.mult),
                           t_ln)
                t_vn.append(chain(pool, t, call(pool.e.tensor_tensor, v, v, LNG, ALU.mult),
                                  call(pool.e.tensor_tensor, v, v, LNB, ALU.add)))
            layer_norm(0)
            refill(1)
            tq, turned = mem_queries(0, (0, 1), vt, QM, QT, (0, 1), prior)
            tu = [None] * 8

            def u_tile(k):
                b = 2 + k % 2
                pe.wait(*bank_free[b])
                t = mtile(0, range(8), PS[:, b, 0:256], x_tok[0])
                fill_in()
                tu[k] = dve.do(call(dve.e.tensor_tensor, U[:, k, :], PS[:, b, 0:256], rb, ALU.mult), t, t_rb, *mem["k"])
                bank_free[b] = [tu[k]]
                if k == 7:
                    done_with(0, t)
                    lend("x0", [t])
                    lend("g", [tu[k]])
                    lend("norm", [tu[k]])
                refill()
            u_tile(0)
            layer_norm(1)
            tqt = turned()
            ns, tn = mem_scales(QM, JK, [*tq, *prior], RC[:, 0, :], t_rc, 0)
            lend("v", [*tqt, act.last, dve.last, pe.last], 1, 2)
            u_tile(1)

            def fill(s, i):
                if i == 0 and s < 6:
                    u_tile(2 + s)
                if (s, i) == (2, 2):
                    lend_once("xe", [t_vn[1]])
                    lend_once("oe", [t_vn[1]])
            st["ahead"] = 5
            P = [flat(x[:, 2 * i:2 * i + 2, :]) for i in range(3) for x in (FH1, FL1)]
            mem_attention(QT, tqt, ns, tn, P[0:3], P[3:5], fill, sb=(0, 1), tb=(4, 5), ob=(6, 7), free=x_free[1])
            x_free[1] = [pe.last, act.last, dve.last]
            lend("p", x_free[1])
            for k in range(8):
                tu[k] = act.do(call(act.e.activation, U[:, k, :], U[:, k, :], ACT.Gelu), tu[k])
            first = out_begin(MEM_FIRST, (2, 3))
            pe.wait(mem["ws"])
            dve.wait(mem["bs"])

            def mix(gi):
                b = gi % 2
                pe.wait(*bank_free[b])
                for n in range(2):
                    t = pe.do(call(pe.e.matmul, PS[:, b, 128 * n:128 * n + 128], VV[:, n, 128 * gi:128 * gi + 128],
                                   WS[:, gi, :], start=True, stop=True, skip_group_check=True), t_vn[n])
                tmp = SCR[:, 9216 + 256 * (gi % 2):9472 + 256 * (gi % 2)]
                tmp3 = tmp.rearrange("p (n t) -> p n t", n=2)
                bs = BS[:, gi, :].unsqueeze(1).broadcast_to([128, 2, 128])
                t = dve.do(call(dve.e.tensor_tensor, tmp3, PS[:, b, 0:256].rearrange("p (n t) -> p n t", n=2), bs,
                                ALU.add), t, *([x_tok[1][gi - 2]] if gi >= 2 else []))
                bank_free[b] = [t]
                t = dve.do(call(dve.e.tensor_tensor, tmp, tmp, U[:, gi, :], ALU.mult), t, tu[gi])
                split_into(1, gi, tmp, [t])
            mix(0)
            mix(1)
            for k in range(8):
                next(first["steps"])
                if k + 2 < 8:
                    mix(k + 2)
                if k % 2:
                    refill(1)
                if k == 5:
                    lend_once("av1", [pe.last])
                    lend("v", [dve.last], 0, 1)
                    lend("u", [dve.last])
            return first, (4, 5, 6, 7)

        def mla(rest_of_moe):
            st["ahead"] = 8
            st["lag"] = 2
            for name in ("x1", "g", "hg", "u", "v", "p", "q"):
                reclaim(name)
            x_free[1] = lasts()
            S = lambda at, n: SCR[:, at:at + n]
            QNT = S(0, 2048).rearrange("p (h t) -> p h t", h=8)
            QRT = S(2048, 1024).rearrange("p (h t) -> p h t", h=4)
            KNT = S(3072, 2048).rearrange("p (h t) -> p h t", h=8)
            KRT = S(6144, 1024).rearrange("p (h t) -> p h t", h=4)
            VT = S(7168, 2048).rearrange("p (n t c) -> p n t c", n=2, t=2)
            QM = S(0, 1024).rearrange("p (t c) -> p t c", t=2)
            QT = S(1024, 1024).rearrange("p (h t) -> p h t", h=4)
            CQ = S(5632, 1024).rearrange("p (t c) -> p t c", t=2)
            CKV = S(6656, 512).rearrange("p (t c) -> p t c", t=2)
            QI = S(7168, 1024).rearrange("p (t h c) -> p t h c", t=2, h=8)
            QIf = S(7168, 1024).rearrange("p (t c) -> p t c", t=2)
            QR = S(8192, 1024).rearrange("p (t h c) -> p t h c", t=2, h=8)
            QRf = S(8192, 1024).rearrange("p (t c) -> p t c", t=2)
            QN = S(9216, 2048).rearrange("p (t c) -> p t c", t=2)
            KR = S(11264, 128).rearrange("p (t c) -> p t c", t=2)
            KRR = S(11392, 128).rearrange("p (t c) -> p t c", t=2)
            X0H, X0L = (x[:, :, :].rearrange("p k t -> p (k t)") for x in (FH0, FL0))
            KT = X0H.rearrange("p (t c) -> p t c", t=2)
            KRH = X0L[:, 0:1024].rearrange("p (t h c) -> p t h c", t=2, h=8)
            KRf = X0L[:, 0:1024].rearrange("p (t c) -> p t c", t=2)
            TAB = [FG[:, i, :].rearrange("p (w t c) -> p w t c", w=4, t=2) for i in range(2)]
            JK = FG[:, 2:4, :].rearrange("p k t -> p (k t)")
            prior = lasts()
            TT = lambda o, x, y, op: call(dve.e.tensor_tensor, o, x, y, op)

            flat2 = lambda ap: ap.rearrange("p k t -> p (k t)")
            gp = small(46, 1)
            t_gp = dve.do(TT(gp, prm("qn_nope"), prm("kn_nope"), ALU.mult), *prior)
            pe.wait(*bank_free[2], *bank_free[5])
            refill(3)
            vt = vtile(0, range(8), 320, 3, (2, 5), x_tok[0], rest_of_moe)
            refill(4)
            for k in range(4):
                square_into(k, H[:, k, :], [h_tok[k]])
            zs, steps = vtiles(0, range(8), (0, 3))
            next(steps)
            refill(3)
            for k in range(4, 8):
                square_into(k, H[:, k, :], [h_tok[k]])
            for tt, b in enumerate((2, 5)):
                dve.do(call(dve.e.tensor_copy, CKV[:, tt, :], PS[:, b, 0:256]), vt, *prior)
                t_kr = dve.do(call(dve.e.tensor_copy, KR[:, tt, :], PS[:, b, 256:320]))
                bank_free[b] = [t_kr]
            t_tab = rope_tables(TAB, FG[:, 2, :], FG[:, 3, :], prior)
            next(steps)
            refill(3)
            r = RC[:, 0, :]
            t_rc = rstd_cols(6, r)

            def latent(k, tokens, b):
                src, name, kk = (CQ, "q_norm", k) if k < 4 else (CKV, "kv_norm", k - 4)
                pe.wait(*bank_free[b])
                for tt in range(2):
                    t = pe.do(call(pe.e.transpose, PS[:, b, 128 * tt:128 * tt + 128],
                                   src[:, tt, 128 * kk:128 * kk + 128], ident), *tokens)
                bank_free[b] = [split_into(1, k, PS[:, b, 0:256], [t], prm(name, kk))]
                return t
            ss1 = small(16, 2, 3)
            for tt in range(2):
                t1 = squares(ss1[:, tt, 1:2], CKV[:, tt, :], JK[:, 0:256], t_kr, t_tab, act.last, *prior)
                t1 = squares(ss1[:, tt, 2:3], KR[:, tt, :], JK[:, 0:64], act.last)
            next(steps)
            latent(4, [t_kr], 6)
            t_ckv_read = latent(5, [t_kr], 7)
            refill(3)
            next(steps)
            done_with(0, zs[1])
            x0_free = list(x_free[0])
            tok = {}

            def up(name, ks, banks, dst, free, n=2):
                pe.wait(*bank_free[banks[0]], *bank_free[banks[1]])
                t = vtile(1, ks, 512, 2, banks, x_tok[1])
                fill_in()
                a_ = act.do(call(act.e.activation, dst[:, 0, :], PS[:, banks[0], :], ACT.Copy), t, *free)
                d_ = dve.do(call(dve.e.tensor_copy, dst[:, 1, :], PS[:, banks[1], :]), t, *free)
                bank_free[banks[0]], bank_free[banks[1]] = [a_], [d_]
                tok[name] = [a_, d_]
                tok[name, "pe"] = t
                refill(n)
            tcq = [dve.do(call(dve.e.tensor_copy, CQ[:, 0, :], PS[:, 0, :]), zs[0], *prior),
                   act.do(call(act.e.activation, CQ[:, 1, :], PS[:, 1, :], ACT.Copy), zs[0], *prior)]
            bank_free[0], bank_free[1] = tcq[0:1], tcq[1:2]
            tq, turned = mem_queries(1, (3, 4), zs[1], QM, QT, (3, 4), prior)
            up("k0", (4, 5), (2, 5), KT[:, :, 0:512], x0_free, 0)
            latent(0, tcq, 0)
            latent(1, tcq, 1)
            tqt = turned()
            refill(1)
            up("k1", (4, 5), (6, 7), KT[:, :, 512:1024], x0_free, 0)
            latent(2, tcq, 0)
            t_cq_read = latent(3, tcq, 1)
            refill(1)
            refill(1)
            ns, tn = mem_scales(QM, JK, tq, r, t_rc, 50)
            for tt in range(2):
                t1 = squares(ss1[:, tt, 0:1], CQ[:, tt, :], JK, *tcq, act.last, *prior)

            ssn, ssr, ssq, ssk = small(128, 2, 8), small(144, 2, 8), small(160, 2, 8), small(176, 2, 8)
            fk, fr = small(192, 2, 8), small(208, 2, 8)
            nsq = small(224, 2, 8)

            def pool_squares(src, scratch, *tokens):
                return pool.do(call(pool.e.tensor_tensor, scratch, src, src, ALU.mult), pool.last, *tokens)

            def reduce_heads(dst, scratch, n, t):
                return dve.do(call(dve.e.tensor_reduce, dst, scratch.rearrange("p (h c) -> p h c", c=n), AX.X, ALU.add), t)
            t_sk = [pool_squares(KT[:, tt, :], S(3072 + 1024 * tt, 1024), *tok["k0"], *tok["k1"], *prior) for tt in range(2)]

            def key_squares():
                for tt in range(2):
                    tok["ssk"] = reduce_heads(ssk[:, tt, :], S(3072 + 1024 * tt, 1024), 128, t_sk[tt])

            def rotate(q, dst, src, heads, tab, tt, scratch, tokens):
                p = [x[:, 0:heads, :] for x in scratch]
                w = [tab[:, i, tt, :].unsqueeze(1).broadcast_to([128, heads, 32]) for i in range(4)]
                x1, x2 = src[:, :, 0:32], src[:, :, 32:64]
                strict = lambda: [q.last] if q is pool else []
                for i, xx in enumerate((x1, x2, x1, x2)):
                    t = q.do(call(q.e.tensor_tensor, p[i], xx, w[i], ALU.mult), *tokens, *strict())
                q.do(call(q.e.tensor_tensor, dst[:, :, 0:32], p[0], p[1], ALU.subtract), t)
                return q.do(call(q.e.tensor_tensor, dst[:, :, 32:64], p[2], p[3], ALU.add), t, *strict())
            RT = [[S(11520 + 64 * i, 64).rearrange("p (h c) -> p h c", h=2) for i in range(4)],
                  [S(5632 + 256 * i, 256).rearrange("p (h c) -> p h c", h=8) for i in range(4)]]
            t_sr, rot = [], []

            def query_rotary():
                for tt in range(2):
                    t_sr.append(pool_squares(QIf[:, tt, :], S((5120, 6656)[tt], 512), *tok["qr"], t_ckv_read, t1))
                for tt in range(2):
                    rot.append(rotate(pool, QR[:, tt], QI[:, tt], 8, TAB[0], tt, RT[1], [*tok["qr"], t_tab, t_cq_read, t1]))
            r2, x, y0, tmp, c = small(24, 2), small(26, 2, 2), small(30, 4), small(34, 4), small(38, 2, 2)
            xf = small(26, 4)
            wide = lambda ap, n: ap.unsqueeze(2).broadcast_to([128, 2, n])
            one = lambda o, x, s1, o0: call(dve.e.tensor_scalar, o, x, s1, None, op0=o0)
            cq, ckv = small(42, 2), small(44, 2)

            def latent_factors():
                t = dve.do(TT(r2, r, r, ALU.mult), t_rc, t1)
                t = chain(dve, t, TT(x, ss1[:, :, 0:2], wide(r2, 2), ALU.mult),
                          one(x[:, :, 0:1], x[:, :, 0:1], 1.0 / 512, ALU.mult),
                          one(x[:, :, 1:2], x[:, :, 1:2], 1.0 / 256, ALU.mult), one(xf, xf, 1e-6, ALU.add))
                t = inv_sqrt(xf, xf, t, (y0, tmp))
                t = dve.do(TT(c, x, wide(r, 2), ALU.mult), t)
                dve.do(call(dve.e.tensor_copy, cq.unsqueeze(2), c[:, :, 0:1]), t)
                tok["c"] = dve.do(call(dve.e.tensor_copy, ckv.unsqueeze(2), c[:, :, 1:2]), t)

            def key_factors():
                c2, kx, ky = small(240, 2), small(242, 2, 8), small(258, 2)
                kxf, k0, k1 = small(242, 16), small(260, 16), small(276, 16)
                dve.wait(tok["ssk"])
                t = dve.do(TT(c2, ckv, ckv, ALU.mult), tok["c"])
                t = chain(dve, t, TT(kx, ssk, wide(c2, 8), ALU.mult),
                          TT(ky.unsqueeze(2), ss1[:, :, 2:3], r2.unsqueeze(2), ALU.mult),
                          TT(kx, kx, wide(ky, 8), ALU.add),
                          call(dve.e.tensor_scalar, kxf, kxf, 1.0 / 192, 1e-6, op0=ALU.mult, op1=ALU.add))
                t = inv_sqrt(kxf, kxf, t, (k0, k1))
                tok["f"] = chain(dve, t, TT(fk, kx, wide(ckv, 8), ALU.mult), TT(fr, kx, wide(r, 8), ALU.mult))

            def scale_keys(tt):
                k3 = KT[:, tt, :].rearrange("p (h c) -> p h c", h=8)
                f = fk[:, tt, :].unsqueeze(2).broadcast_to([128, 8, 128])
                tok["kt", tt] = pool.do(call(pool.e.tensor_tensor, k3, k3, f, ALU.mult), tok["f"], pool.last)

            def key_rotary(tt):
                tr = rotate(dve, KRR[:, tt, :].unsqueeze(1), KR[:, tt, :].unsqueeze(1), 1, TAB[1], tt,
                            [y[:, tt:tt + 1, :] for y in RT[0]], [t_tab, *x0_free, t1])
                tok["kr"] = dve.do(TT(KRH[:, tt], KRR[:, tt, :].unsqueeze(1).broadcast_to([128, 8, 64]),
                                      fr[:, tt, :].unsqueeze(2).broadcast_to([128, 8, 64]), ALU.mult), tr, tok["f"])

            def rotary_squares():
                for tt in range(2):
                    tok["ssr"] = reduce_heads(ssr[:, tt, :], S((5120, 6656)[tt], 512), 64, t_sr[tt])

            def query_squares(tt):
                for h in range(8):
                    tok["ssn"] = squares(ssn[:, tt, h:h + 1], QN[:, tt, 128 * h:128 * h + 128], JK[:, 0:128], act.last,
                                         *tok["qn0"], *tok["qn1"])
            v = []

            def value(n, bb):
                pe.wait(*bank_free[bb[0]], *bank_free[bb[1]])
                v.append((bb, vtile(1, (4, 5), 512, 2, bb, x_tok[1])))
                refill()

            def values(n):
                bb, t = v[n]
                for tt in range(2):
                    tok["v"] = act.do(call(act.e.activation, VT[:, n, tt, :], PS[:, bb[tt], :], ACT.Copy,
                                           scale=ckv[:, tt:tt + 1]), t, tok["c"], *tok["qrt"])
                    bank_free[bb[tt]] = [tok["v"]]
            tkr, first = [], []

            def rotary_keys(pr):
                b = 6 + pr % 2
                pe.wait(*bank_free[b])
                for tt in range(2):
                    t = pe.do(call(pe.e.transpose, PS[:, b, 128 * tt:128 * tt + 128], KRf[:, tt, 128 * pr:128 * pr + 128],
                                   ident), tok["kr"])
                o = PS[:, b, 0:256]
                if pr % 2:
                    t_kr_ = act.do(call(act.e.activation, KRT[:, pr, :], o, ACT.Copy), t, tok["ssr"], rot[-1])
                else:
                    t_kr_ = dve.do(call(dve.e.tensor_copy, KRT[:, pr, :], o), t, tok["ssr"], rot[-1])
                tkr.append(t_kr_)
                bank_free[b] = [t_kr_]
                tok["krt"] = t

            def scales():
                t = dve.do(TT(ssq, ssn, ssr, ALU.add), tok["ssn"], tok["ssr"])
                tok["nsq"] = query_scales(ssq, nsq, 8, cq, 192, [t, tok["c"]], 242)

            def queries(n, banks, engines=(dve, act)):
                tok["qnt", n] = to_features(QN[:, :, 512 * n:512 * n + 512], 4, QNT[:, 4 * n:4 * n + 4, :], banks,
                                            [*tok[f"qn{n}"], t_gp], gain=gp, free=[*tqt, tn], engines=engines)

            def keys(n, banks):
                tok["knt", n] = to_features(KT[:, :, 512 * n:512 * n + 512], 4, KNT[:, 4 - 4 * n:8 - 4 * n, :], banks,
                                            [tok["kt", 0], tok["kt", 1]], free=[tok["ssk"]])

            def rotary_queries(banks):
                tok["qrt"] = to_features(QRf, 4, QRT, banks, rot, free=prior)

            def begin():
                first.append(out_begin(MEM_FIRST, (2, 3)))

            def step():
                next(first[0]["steps"])

            def lend_g():
                lend("g", [act.last, dve.last, pool.last])

            def lend_av0():
                lend_once("av0", [pe.last, act.last, dve.last])
            plan = {
                (0, 0): [(latent_factors,), (up, "qr", range(4), (0, 1), QIf, prior), (query_rotary,)],
                (1, 0): [(key_squares,), (up, "qn0", range(4), (6, 7), QN[:, :, 0:512], prior), (key_factors,)],
                (2, 0): [(up, "qn1", range(4), (0, 1), QN[:, :, 512:1024], prior), (scale_keys, 0)],
                (3, 0): [(value, 0, (6, 7)), (scale_keys, 1), (queries, 0, (0, 1))],
                (4, 0): [(rotary_queries, (0, 1)), (values, 0), (query_squares, 0), (key_rotary, 0), (rotary_squares,),
                         (key_rotary, 1)],
                (4, 2): [(value, 1, (0, 1)), (keys, 0, (6, 7))],
                (5, 0): [(query_squares, 1), (lend_g,), (begin,), (step,)],
                (6, 0): [(values, 1), (rotary_keys, 0), (step,), (scales,)],
                "end": [(rotary_keys, 1), (step,)]}

            def fill(s, i):
                for f, *args in plan.get((s, i), ()):
                    f(*args)
            st["ahead"] = 6
            x1_free = x_free[1]
            P = [X0L[:, 1024:1536], X0L[:, 1536:2048]] + [flat2(x[:, 6:8, :]) for x in (FH1, FL1)] + [flat2(SQ[:, :, :])]
            mem_attention(QT, tqt, ns, tn, P[0:3], P[3:5], fill, sb=(2, 3), tb=(4,), ob=(5,),
                          free=[*x0_free, *x1_free, t_rc])
            x_free[1] = [pe.last, act.last, dve.last]
            lend("mem", x_free[1])
            for f, *args in plan["end"]:
                f(*args)
            refill()

            def unit(u):
                rows = slice(64 * (u % 2), 64 * (u % 2) + 64)
                return dict(heads=[dict(
                    score=[(0, 128, QNT[:, u, 0:128], KNT[:, (u + 4) % 8, 0:128], True, False),
                           (0, 128, QRT[rows, u // 2, 0:128], KRT[rows, u // 2, 0:128], False, True),
                           (128, 256, QNT[:, u, 128:256], KNT[:, (u + 4) % 8, :], True, False),
                           (128, 256, QRT[rows, u // 2, 128:256], KRT[rows, u // 2, :], False, True)],
                    scale=(nsq[:, 0, u:u + 1], nsq[:, 1, u:u + 1]), gate=None,
                    wait=(*tok["qnt", u // 4], *tok["qrt"], *tok["knt", u // 4], *tkr[0:u // 2 + 1]),
                    v=[VT[:, u // 4, kb, 128 * (u % 4):128 * (u % 4) + 128] for kb in range(2)])], o=u, first=True, last=True, extra=None)

            dve.wait(tok["nsq"])
            pe.wait(tok["v"])
            first = first[0]

            plan2 = {
                (0, 0): [(queries, 1, (6, 7)), (lend_av0,)],
                (1, 0): [(keys, 1, (6, 7))],
                (2, 0): [(rotary_keys, 2)],
                (2, 2): [(rotary_keys, 3)]}

            def fill2(s, i):
                for f, *args in plan2.get((s, i), ()):
                    f(*args)
                if (s, i) == (0, 0):
                    lend("x0", x_free[1], 3, 4)
                    lend_once("xe", [rot[-1], tok["ssr"], pool.last])
                if (s, i) == (2, 0):
                    lend("x0", [pe.last, act.last, dve.last], 0, 1)
                    lend("x0", [pe.last, act.last, dve.last], 2, 3)
                if (s, i) == (3, 0):
                    lend("x0", [pe.last, act.last, dve.last], 1, 2)
                if (s, i) == (4, 0):
                    lend_once("oe", [pe.last])
                    lend("hg", [pe.last], 0, 1)
                if (s, i) == (8, 0):
                    lend("hg", [pe.last], 1, 2)
                    lend_once("av1", [pe.last])
                    lend("u", [pe.last])
                if i == 2 and s >= 4 and s != 8 or (s, i) == (10, 0):
                    next(first["steps"])
                if i == 2:
                    refill(1)
            st["ahead"] = 4
            st["lag"] = 1
            P = [S(9216 + 384 * i, 384) for i in range(4)] + [flat(SQ[:, :, :])[:, 0:384]]
            attention(8, unit, P[0:3], P[3:5], 384, o_split(), sb=(0, 1), fill=fill2)
            lend("p", [pe.last])
            return first, (4, 5, 6, 7)

        def rope_tables(TAB, R1, R2, prior):
            pf = small(0, 2)
            A, N, NH, TMP = (R1[:, 64 * i:64 * i + 64] for i in range(4))
            ang = A.rearrange("p (t i) -> p t i", t=2)
            SIN, COS = R2[:, 0:64], R2[:, 64:128]
            two_pi = 2 * np.pi
            C1 = 6.28125
            C2 = float(np.floor((two_pi - C1) * 2 ** 20) / 2 ** 20)
            C3 = float(two_pi - C1 - C2)
            M = 12582912.0
            t = dve.do(call(dve.e.tensor_copy, pf, POSI[:, :]), t_pos, *prior)
            for tt in range(2):
                t = dve.do(call(dve.e.tensor_scalar, ang[:, tt, :], cst("inv", 32), pf[:, tt:tt + 1], None,
                                op0=ALU.mult), t)
            stt = lambda o, x, s, y: call(dve.e.scalar_tensor_tensor, o, x, s, y, ALU.mult, ALU.add)
            ts = lambda o, x, s1, s2, o0, o1: call(dve.e.tensor_scalar, o, x, s1, s2, op0=o0, op1=o1)
            one = lambda o, x, s1, o0: call(dve.e.tensor_scalar, o, x, s1, None, op0=o0)
            t = chain(
                dve, t,
                ts(N, A, 1.0 / two_pi, M, ALU.mult, ALU.add), one(N, N, M, ALU.subtract),
                ts(NH, N, 1.0 / 4096, M, ALU.mult, ALU.add), ts(NH, NH, M, 4096.0, ALU.subtract, ALU.mult),
                call(dve.e.tensor_tensor, TMP, N, NH, ALU.subtract),
                stt(A, NH, -C1, A), stt(A, TMP, -C1, A), stt(A, NH, -C2, A), stt(A, TMP, -C2, A), stt(A, N, -C3, A),
                one(N, A, np.pi / 2, ALU.add), one(TMP, N, np.pi, ALU.is_gt), stt(N, TMP, -two_pi, N),
                ts(A, A, -3.1415925, 3.1415925, ALU.max, ALU.min), ts(N, N, -3.1415925, 3.1415925, ALU.max, ALU.min))
            act.do(call(act.e.activation, SIN, A, ACT.Sin), t)
            t = act.do(call(act.e.activation, COS, N, ACT.Sin), t)
            for tab, name in zip(TAB, ("qn_rope", "kn_rope")):
                g = prm(name, 0, 64).rearrange("p (h c) -> p h c", h=2)
                for w, (gi, f) in enumerate(((0, COS), (1, SIN), (0, SIN), (1, COS))):
                    t2 = dve.do(call(dve.e.tensor_tensor, tab[:, w, :, :], f.rearrange("p (t i) -> p t i", t=2),
                                     g[:, gi, :].unsqueeze(1).broadcast_to([128, 2, 32]), ALU.mult), t, *prior)
            return t2

        HGS = [SCR[:, x:x + 2048].rearrange("p (k t) -> p k t", k=8) for x in (0, 7168)]
        XNORM = flat(FH1[:, 0:8, :]).rearrange("p (t c) -> p t c", t=2)
        hg_tok = [None] * 8

        def out_proj_moe(li, first, banks):
            prior, HG = lasts(), HGS[li]
            act.do(call(act.e.activation, small(319, 1), ones[:, 0:1], ACT.Abs_reciprocal_sqrt), *prior)

            def evict(m):
                if m == 7:
                    square_into(m, H[:, m, :], [h_tok[m]], dve)
                hg_tok[m] = act.do(call(act.e.activation, HG[:, m, :], H[:, m, :], ACT.Copy,
                                        scale=prm("norm2", 8 * li + m)), h_tok[m], *prior)
                if m < 7:
                    square_into(m, H[:, m, :], [h_tok[m]])
            out_proj(first, banks, evict)

        def overflow(li, CW, POSX, t_flag, prior):
            q = {n: Queue(f"s_over{li}_{n}", e) for n, e in (("sp", nc.sync), ("pe", nc.tensor), ("act", nc.scalar),
                                                             ("dve", nc.vector))}
            osp, ope, oact, odve = (q[n] for n in ("sp", "pe", "act", "dve"))
            o_load = [sem(f"s_over{li}_w"), 0]
            XN = XNORM
            W = SCR[:, 4096:6144].rearrange("p (v u c) -> p v u c", v=2, u=2)
            Y = [SCR[:, x:x + 1024] for x in (6144, 10752)]
            A, AT = FL1[:, 4:6, :], FL1[:, 6:8, :]
            HT = [FL1[:, 0:4, :], FH1[:, 8:12, :]]
            CWO = SM[:, 128:192].rearrange("p (t e) -> p t e", t=2)
            pairs = a["moe"][li].rearrange("(g v u h) p (e c) -> g h e v p u c", v=6, u=2, h=2, e=2)
            quarters = a["moe"][li].rearrange("(g v u h) p (e c) -> g h e v p u c", v=6, u=2, h=2, e=4)

            def fetch(e, at, *tokens):
                for v in range(2):
                    if at < 4:
                        t = osp.dma(W[:, v], pairs[e // 4, e % 4 // 2, e % 2, at + v], o_load, *tokens)
                        continue
                    for k in range(2):
                        t = osp.dma(W[:, v, k, :].rearrange("p (u c) -> p u c", u=2), quarters[e // 4, k, e % 4, at + v],
                                    o_load, *tokens)
                return t
            for tt in range(2):
                odve.do(call(odve.e.memset, Y[tt], 0.0))
            t_y = odve.do(call(odve.e.scalar_tensor_tensor, CWO, POSX, 31.5 - 1000, CW, ALU.is_ge, ALU.mult))
            for f in range(4):
                for k in (2 * f, 2 * f + 1):
                    for tt in range(2):
                        t = ope.do(call(ope.e.transpose, PS[:, 1 + f, 256 * (k % 2) + 128 * tt:256 * (k % 2) + 128 * tt + 128],
                                        XN[:, tt, 128 * k:128 * k + 128], ident))
                t_w = oact.do(call(oact.e.activation, flat(HT[f // 2][:, f % 2 * 2:f % 2 * 2 + 2, :]), PS[:, 1 + f, :],
                                   ACT.Copy), t)
            ope.wait(t_w)
            t_w = t_av = t_down = None
            for e in range(32):
                for hf in range(2):
                    ld_ = fetch(e, 2 * hf, t_w, ope.last)
                    for tt in range(2):
                        for k in range(4):
                            t_w = ope.do(call(ope.e.matmul, PS[:, 1 + tt, :], HT[hf][:, k, 128 * tt:128 * tt + 128],
                                              W[:, k // 2, k % 2, :], start=hf == 0 and k == 0, stop=hf == 1 and k == 3,
                                              skip_group_check=True), ld_, t_av)
                for tt in range(2):
                    t = oact.do(call(oact.e.activation, A[:, tt, :], PS[:, 1 + tt, 0:256], ACT.Silu), t_w, t_down)
                    t = odve.do(call(odve.e.tensor_tensor, A[:, tt, :], PS[:, 1 + tt, 256:512], A[:, tt, :],
                                     ALU.mult), t)
                    t_av = odve.do(call(odve.e.tensor_scalar, A[:, tt, :], A[:, tt, :], CWO[:, tt, e:e + 1], None,
                                        op0=ALU.mult), t, t_y)
                for tt in range(2):
                    for k in range(2):
                        t = ope.do(call(ope.e.transpose, PS[:, 3, 256 * k + 128 * tt:256 * k + 128 * tt + 128],
                                        A[:, tt, 128 * k:128 * k + 128], ident), t_av)
                t_at = oact.do(call(oact.e.activation, flat(AT), PS[:, 3, :], ACT.Copy), t)
                ld_ = fetch(e, 4, t_w)
                for tt in range(2):
                    for n in range(2):
                        b = (4, 6, 7, 3)[2 * tt + n]
                        for k in range(2):
                            t_down = ope.do(call(ope.e.matmul, PS[:, b, :], AT[:, k, 128 * tt:128 * tt + 128],
                                                 W[:, n, k, :], start=k == 0, stop=k == 1, skip_group_check=True),
                                            ld_, t_at, t_y)
                for tt in range(2):
                    for n in range(2):
                        y = Y[tt][:, 512 * n:512 * n + 512]
                        t_y = odve.do(call(odve.e.tensor_tensor, y, PS[:, (4, 6, 7, 3)[2 * tt + n], :], y, ALU.add),
                                      t_down, t_y)
                t_av = t_y
            for f in range(8):
                for tt in range(2):
                    t = ope.do(call(ope.e.transpose, PS[:, 1 + f // 2, 256 * (f % 2) + 128 * tt:256 * (f % 2) + 128 * tt + 128],
                                    Y[tt][:, 128 * f:128 * f + 128], ident), t_y)
            for f in range(4):
                h2 = H[:, 2 * f:2 * f + 2, :].rearrange("p k t -> p (k t)")
                odve.do(call(odve.e.tensor_tensor, h2, PS[:, 1 + f, :], h2, ALU.add), t)
            ends = [x.last for x in (ope, oact, odve)]
            for n, main in (("sp", sp), ("pe", pe), ("act", act), ("dve", dve)):
                q[n].wait(*ends)

                def emit(n=n, e=main.e, ops=q[n].ops):
                    with e.register(f"over{li}_{n}") as flag:
                        e.reg_load(flag, FLAG[0:1, li:li + 1])
                        with e.If_ne(flag, 0):
                            for op in ops:
                                op()
                main.wait(t_flag, *prior)
                main.ops.append(emit)

        def moe(li):
            HG, XN, XE = HGS[li], XNORM, [flat(FL1[:, 0:4, :]), SCR[:, 5120:6144]]
            XE = [ap.rearrange("p (k s) -> p k s", k=8) for ap in XE]
            S, SW = ([FL1[:, 4 + 2 * j + i, :].rearrange("p (t s) -> p t s", t=2) for i in range(2)] for j in range(2))
            SWT, SG, AV, AT = ([SCR[:, x + 256 * i:x + 256 * i + 256] for x in (10752, 6144)] for i in range(4))
            AT = [ap.rearrange("p (k s) -> p k s", k=2) for ap in AT]
            OE = [SCR[:, 4096:5120], flat(FH1[:, 8:12, :])]
            POSX, CW = (SM[:, x:x + 64].rearrange("p (t e) -> p t e", t=2) for x in (0, 64))
            r = RC[:, 0, :]
            prior = lasts()
            lend_once("oe1", x_free[1])
            lend("x1", x_free[1])
            lend("q", [norm["acc"]])
            u, w, loaded = next_raw()
            pe.wait(loaded, *bank_free[0])
            for k in range(8):
                if k == 3:
                    t_rc = rstd_cols(5, RC[:, 0, :])
                for tt in range(2):
                    t_l = pe.do(call(pe.e.matmul, PS[:, 0, 64 * tt:64 * tt + 36], HG[:, k, 128 * tt:128 * tt + 128],
                                     columns(w, 36 * k, 36), start=k == 0 and tt == 0, stop=k == 7,
                                     skip_group_check=True), hg_tok[k])
            give_back(u, [t_l])
            t_xn = []
            for tt in range(2):
                for kk in range(2):
                    b = 1 + 2 * tt + kk
                    pe.wait(*bank_free[b])
                    for k in range(4):
                        t = pe.do(call(pe.e.transpose, PS[:, b, 128 * k:128 * k + 128],
                                       HG[:, 4 * kk + k, 128 * tt:128 * tt + 128], ident), hg_tok[4 * kk + k])
                    x = act.do(call(act.e.activation, XN[:, tt, 512 * kk:512 * kk + 512], PS[:, b, :], ACT.Copy,
                                    scale=r[:, tt:tt + 1]), t, t_rc, *prior)
                    bank_free[b] = [x]
                    t_xn.append(x)
            t_turned = t
            lend(("hg", "v")[li], [t_turned])
            at = [0]

            def new(*shape):
                n = int(np.prod(shape))
                ap = flat(FL1[:, 5:8, :])[:, at[0]:at[0] + n]
                at[0] += n
                assert at[0] <= 768
                if len(shape) == 2:
                    ap = ap.rearrange("p (a b) -> p a b", a=shape[0])
                return ap
            TT = lambda o, x, y, op: call(dve.e.tensor_tensor, o, x, y, op)
            TS = lambda o, x, s1, s2, o0, o1: call(dve.e.tensor_scalar, o, x, s1, s2, op0=o0, op1=o1)
            RED = lambda o, x, op: call(dve.e.tensor_reduce, o, x, AX.X, op)
            STT = lambda o, x, s, y, o0, o1: call(dve.e.scalar_tensor_tensor, o, x, s, y, o0, o1)
            wide = lambda ap, n: ap.unsqueeze(2).broadcast_to([128, 2, n])
            iota = lambda n: cst("iota", n).unsqueeze(1).broadcast_to([128, 2, n])
            L = new(2, 36)
            t = t_rc
            for tt in range(2):
                t = dve.do(STT(L[:, tt, :], PS[:, 0, 64 * tt:64 * tt + 36], r[:, tt:tt + 1],
                               prm("r_bias", 36 * li, 36), ALU.mult, ALU.add), t, t_l, *prior)
            bank_free[0] = [t]
            gm, eq, gi, d4, sel = new(2), new(2, 4), new(2), new(2, 4), new(2, 4)
            m1, m2, i1, i2 = new(2, 4), new(2, 4), new(2, 4), new(2)
            q1, o1, o2, E2, ip, mk = (new(2, 32) for _ in range(6))
            q2 = q1
            el4 = lambda ap: ap.rearrange("p t (g e) -> p t g e", g=4)
            over = lambda ap: ap.unsqueeze(3).broadcast_to([128, 2, 4, 8])
            lg, le = L[:, :, 0:4], el4(L[:, :, 4:36])
            steps = [RED(m1, le, ALU.max), TT(el4(q1), le, over(m1), ALU.is_equal),
                     STT(q1, q1, -100.0, iota(32), ALU.mult, ALU.add), RED(i1, el4(q1), ALU.min),
                     TT(el4(o1), el4(q1), over(i1), ALU.is_equal), STT(el4(E2), el4(o1), -2e30, le, ALU.mult, ALU.add),
                     RED(m2, el4(E2), ALU.max), TT(el4(q2), el4(E2), over(m2), ALU.is_equal)]
            between = [RED(gm, lg, ALU.max), TT(eq, lg, wide(gm, 4), ALU.is_equal),
                       STT(eq, eq, -100.0, iota(4), ALU.mult, ALU.add), RED(gi, eq, ALU.min),
                       TT(sel, eq, wide(gi, 4), ALU.is_equal),
                       STT(el4(ip), over(sel), -1000.0, el4(iota(32)), ALU.mult, ALU.add)]
            tg = t
            for n, op in enumerate(steps):
                t = dve.do(op, t)
                if n < len(between):
                    tg = dve.do(between[n], tg)
            t_o1 = dve.do(TT(el4(o1), el4(o1), over(sel), ALU.mult), tg)
            t_o2 = chain(dve, t, STT(q2, q2, -100.0, ip, ALU.mult, ALU.add), RED(i2, q2, ALU.min),
                         TT(o2, q2, wide(i2, 32), ALU.is_equal))
            before, PP = cst("before", 128), PS[:, 5, 0:64].rearrange("p (t e) -> p t e", t=2)
            pe.wait(*bank_free[5], *bank_free[6])
            for o, t in ((o1, t_o1), (o2, t_o2)):
                pe.run(call(pe.e.matmul, PS[:, 5, 0:64], before, o.rearrange("p a e -> p (a e)"), start=o is o1,
                            stop=False, skip_group_check=True), t)
                t_pp = pe.do(call(pe.e.matmul, PS[:, 5, 32:64], ones, o[:, 0, :], start=False, stop=o is o2,
                                  skip_group_check=True))
            d8, dd, gs, den, w1, w2 = new(2, 4), new(2), new(2), new(2), new(2), new(2)
            cm = new(2)
            tk = {}

            def weights_and_flag():
                t_d4 = dve.do(TT(d4, lg, wide(gm, 4), ALU.subtract))
                t_ge = act.do(call(act.e.activation, d4, d4, ACT.Exp), t_d4)
                t_mk = dve.do(TT(mk, o1, o2, ALU.add))
                pe.wait(t_mk)
                for tt in range(2):
                    t_cnt = pe.do(call(pe.e.matmul, PS[:, 6, 0:32], ones, mk[:, tt, :], start=tt == 0, stop=tt == 1))
                t = dve.do(TT(d8, m2, m1, ALU.subtract))
                t = chain(dve, t, TT(d8, d8, sel, ALU.mult), RED(dd, d8, ALU.add))
                t_e = act.do(call(act.e.activation, dd, dd, ACT.Exp), t)
                t_gs = dve.do(RED(gs, d4, ALU.add), t_ge)
                dve.wait(t_gs)
                t = chain(dve, t_e, STT(den, dd, 1.0, gs, ALU.add, ALU.mult), call(dve.e.reciprocal, w1, den),
                          TT(w2, w1, dd, ALU.mult))
                t1 = dve.do(TT(o1, o1, wide(w1, 32), ALU.mult), t)
                t2 = dve.do(TT(o2, o2, wide(w2, 32), ALU.mult))
                tk["cw"] = dve.do(TT(CW, o1, o2, ALU.add), t1, t2)
                t = dve.do(RED(cm[:, 0:1], PS[:, 6, 0:32], ALU.max), t_cnt)
                bank_free[6] = [t]
                return dve.do(call(dve.e.tensor_scalar, FLAG[:, li:li + 1], cm[:, 0:1], 32.5, None, op0=ALU.is_gt), t)

            def places(g):
                i = g % 2
                px = (POSX if g else PP)[:, :, 4 * g:4 * g + 4].unsqueeze(3).broadcast_to([128, 2, 4, 32])
                cw = CW[:, :, 4 * g:4 * g + 4].unsqueeze(3).broadcast_to([128, 2, 4, 32])
                io = cst("iota", 32).unsqueeze(1).unsqueeze(1).broadcast_to([128, 2, 4, 32])
                v = lambda ap: ap.rearrange("p t (e s) -> p t e s", e=4)
                t = dve.do(TT(v(S[i]), io, px, ALU.is_equal), tk["px"], tk.get(("gather", g - 2)), tk.get(("turn", g - 2)),
                           dve.last)
                tk["S", g] = t

                def weighted():
                    tk["SW", g] = dve.do(TT(v(SW[i]), v(S[i]), cw, ALU.mult), t, tk["cw"])
                return weighted

            def gather(g):
                for hf in range(2):
                    pe.wait(*bank_free[hf])
                    for k in range(4):
                        o = PS[:, hf, 128 * k:128 * k + 128]
                        for tt in range(2):
                            t = pe.do(call(pe.e.matmul, o, XN[:, tt, 128 * (4 * hf + k):128 * (4 * hf + k) + 128],
                                           S[g % 2][:, tt, :], start=tt == 0, stop=tt == 1, skip_group_check=True),
                                      tk["S", g], *t_xn)
                    dst = XE[g % 2][:, 4 * hf:4 * hf + 4, :].rearrange("p k s -> p (k s)")
                    before_ = [tk["gu", g - 2]] if g >= 2 else once["xe"]
                    if hf:
                        t2 = dve.do(call(dve.e.tensor_copy, dst, PS[:, hf, :]), t, *before_)
                    else:
                        t2 = act.do(call(act.e.activation, dst, PS[:, hf, :], ACT.Copy), t, *before_)
                    bank_free[hf] = [t2]
                    tk["xe", g, hf] = t2
                tk["gather", g] = t

            def gather_first():
                for n, (b, ks) in enumerate(((0, (0,)), (1, (1, 2)), (3, (3, 4)), (4, (5, 6, 7)))):
                    pe.wait(*bank_free[b])
                    for j, k in enumerate(ks):
                        for tt in range(2):
                            t = pe.do(call(pe.e.matmul, PS[:, b, 128 * j:128 * j + 128], XN[:, tt, 128 * k:128 * k + 128],
                                           S[0][:, tt, :], start=tt == 0, stop=tt == 1, skip_group_check=True),
                                      tk["S", 0], *t_xn)
                    dst = XE[0][:, ks[0]:ks[-1] + 1, :].rearrange("p k s -> p (k s)")
                    src = PS[:, b, 0:128 * len(ks)]
                    if n % 2:
                        t2 = act.do(call(act.e.activation, dst, src, ACT.Copy), t)
                    else:
                        t2 = dve.do(call(dve.e.tensor_copy, dst, src), t)
                    bank_free[b] = [t2]
                    for k in ks:
                        tk["xe", 0, k] = t2
                    yield
                tk["gather", 0] = t

            def gate_up(g):
                pe.wait(*bank_free[2])
                for k in range(8):
                    if g == 0:
                        next(first_tokens, None)
                    pe.wait(tk["xe", g, k // 4 if g else k])
                    us, e = [next_raw(), next_raw()], 0
                    for u, w, loaded in us:
                        pe.wait(loaded)
                    for e in range(4):
                        w = columns(us[e // 2][1], 512 * (e % 2), 512)
                        t = pe.do(call(pe.e.matmul, PS[32 * e:32 * e + 32, 2, :], XE[g % 2][:, k, 32 * e:32 * e + 32],
                                       w, start=k == 0, stop=k == 7, skip_group_check=True))
                        if e % 2:
                            give_back(us[e // 2][0], [t])
                    if (g, k) == (0, 4):
                        tk["flag"] = weights_and_flag()
                        weighted()
                        places(1)()
                    if g == 7 and k in (1, 3, 5):
                        combine(6, ((0,), (1,), (2, 3))[k // 2])
                tk["gu", g] = t
                i = g % 2
                if g < 2:
                    act.wait(*once[f"av{g}"])
                    dve.wait(*once[f"av{g}"])
                ts = act.do(call(act.e.activation, SG[i], PS[:, 2, 0:256], ACT.Silu), t, tk.get(("av", g - 2)))
                tk["av", g] = dve.do(TT(AV[i], SG[i], PS[:, 2, 256:512], ALU.mult), ts, tk.get(("turn", g - 2)))
                bank_free[2] = [tk["av", g]]

            def turn_(g):
                i = g % 2
                pe.wait(*bank_free[5])
                for k in range(2):
                    t = pe.do(call(pe.e.transpose, PS[:, 5, 128 * k:128 * k + 128], AV[i][:, 128 * k:128 * k + 128],
                                   ident), tk["av", g])
                for tt in range(2):
                    t = pe.do(call(pe.e.transpose, PS[:, 5, 256 + 128 * tt:384 + 128 * tt], SW[i][:, tt, :], ident),
                              tk["SW", g])
                tk["turn", g] = t
                ta = act.do(call(act.e.activation, AT[i].rearrange("p k s -> p (k s)"), PS[:, 5, 0:256], ACT.Copy), t,
                            tk.get(("down", g - 2)))
                tk["sw", g] = dve.do(call(dve.e.tensor_copy, SWT[i], PS[:, 5, 256:512]), ta, tk.get(("comb", g - 2)))
                tk["at", g] = ta
                bank_free[5] = [tk["sw", g]]

            def down(g):
                i = g % 2
                pe.wait(tk["at", g])
                for c in range(4):
                    b, x = ((3, 4, 0, 1)[c], 0) if g == 7 else (3 + c // 2, 256 * (c % 2))
                    if x == 0:
                        pe.wait(*bank_free[b])
                    for k in range(2):
                        u, w, loaded = next_raw()
                        pe.wait(loaded)
                        for e in range(4):
                            t = pe.do(call(pe.e.matmul, PS[32 * e:32 * e + 32, b, x:x + 256],
                                           AT[i][:, k, 32 * e:32 * e + 32], columns(w, 256 * e, 256), start=k == 0,
                                           stop=k == 1, skip_group_check=True))
                        give_back(u, [t])
                    if g < 7 and c % 2 == 0:
                        continue
                    n, q = x + 256, dve if c >= 2 else act
                    d = OE[i][:, 256 * c + 256 - n:256 * c + 256]
                    if g < 2:
                        q.wait(*once[("oe", "oe1")[g]])
                    tokens = (t, tk.get(("comb", g - 2)))
                    if q is dve:
                        t2 = dve.do(call(dve.e.tensor_copy, d, PS[:, b, 0:n]), *tokens)
                    else:
                        t2 = act.do(call(act.e.activation, d, PS[:, b, 0:n], ACT.Copy), *tokens)
                    bank_free[b] = [t2]
                    tk["oe", g, c] = t2
                    if g < 7:
                        tk["oe", g, c - 1] = t2
                    yield
                tk["down", g] = t

            def combine(g, fs=range(4)):
                i = g % 2
                pe.wait(tk["sw", g])
                for f in fs:
                    if (g, f) == (7, 3) and li:
                        t = last_features(i)
                        break
                    b = 6 + f % 2
                    pe.wait(*bank_free[b], tk["oe", g, f])
                    for x in range(2):
                        t = pe.do(call(pe.e.matmul, PS[:, b, 256 * x:256 * x + 256],
                                       OE[i][:, 128 * (2 * f + x):128 * (2 * f + x) + 128], SWT[i], start=True, stop=True,
                                       skip_group_check=True))
                    h2 = H[:, 2 * f:2 * f + 2, :].rearrange("p k t -> p (k t)")
                    t2 = dve.do(TT(h2, PS[:, b, :], h2, ALU.add), t, h_tok[2 * f], h_tok[2 * f + 1])
                    h_tok[2 * f] = h_tok[2 * f + 1] = t2
                    bank_free[b] = [t2]
                    if g == 7 and li:
                        t_out.append(sp.dma(out[:, 512 * f:512 * f + 512], h2, o_sems[f], t2))
                if g == 7 and not li:
                    for k in range(2 * fs[0], 2 * fs[-1] + 2):
                        split_into(0, k, H[:, k, :], [h_tok[k]], prm("norm1", 8 + k))
                tk["comb", g] = t

            tk["px"] = t_pp
            def last_features(i):
                pe.wait(tk["oe", 7, 3])
                for k in (6, 7):
                    pe.wait(*bank_free[k])
                    t = pe.do(call(pe.e.matmul, PS[:, k, 0:256], OE[i][:, 128 * k:128 * k + 128], SWT[i], start=True,
                                   stop=True))
                    t2 = dve.do(call(dve.e.tensor_tensor, H[:, k, :], PS[:, k, 0:256], H[:, k, :], ALU.add), t, h_tok[k])
                    t_out.append(sp.dma(out[:, 256 * k:256 * k + 256], H[:, k, :], o_sems[k], t2))
                return t

            weighted = places(0)
            tk["px"] = dve.do(call(dve.e.tensor_copy, POSX, PP), t_pp)
            bank_free[5] = [tk["px"]]
            first_tokens = gather_first()
            next(first_tokens)
            for g in range(8):
                gate_up(g)
                if g >= 1 and g not in (4, 7):
                    combine(g - 1)
                if g < 7 and g != 3:
                    gather(g + 1)
                turn_(g)
                if g == 7:
                    break
                for _ in down(g):
                    pass
                if g + 2 < 8 and g not in (2, 3):
                    places(g + 2)()
                if g == 3:
                    combine(3)
                    overflow(li, CW, POSX, tk["flag"], [*lasts(), *[t for b in bank_free for t in b]])
                    places(4)()
                    gather(4)
                    places(5)()
                if g == 6 and li == 0:
                    st["limit"] = bounds[1]
            quarters = down(7)
            next(quarters)
            next(quarters)
            if li == 0:
                x_free[0] = reclaim("x0")
            combine(7, (0,))
            next(quarters)
            if li == 0:
                refill(1)
                fill_in()
            combine(7, (1, 2))
            for _ in quarters:
                pass
            rest = call(combine, 7, (3,))
            if li:
                rest()
            return rest

        def start_layer(gain_name, at):
            refill(1)
            for k in range(8):
                split_into(0, k, H[:, k, :], [h_tok[k]], prm(gain_name, at + k))
                if k % 2:
                    refill(1)
            refill(3)
            sq = SCR[:, 0:2048]
            t = None
            for i in range(2):
                x = slice(1024 * i, 1024 * i + 1024)
                t = pool.do(call(pool.e.tensor_tensor, sq[:, x], h2[:, x], h2[:, x], ALU.mult), *h_tok[4 * i:4 * i + 4])
            for n in (1024, 512, 256):
                to = sq[:, 0:n] if n > 256 else ACC[:, :]
                t = pool.do(call(pool.e.tensor_tensor, to, sq[:, 0:n], sq[:, n:2 * n], ALU.add), t)
            norm["acc"] = t

        t_out = []
        o_sems = [[sem(f"s_out{i}"), 0] for i in range(8)]

        def program():
            start_layer("norm_mix", 0)
            for i in range(4):
                first, banks = nsa(i // 3) if i % 3 == 0 else moba() if i == 1 else conv()
                out_proj(first, banks, ffn_input(i))
                if i < 3:
                    ffn(i, lambda d, i=i: ("norm_mix", 8 * (i + 1) + d))
                else:
                    load_mem()
                    ffn(i, None, mem_hook)

            KM, t_km = mem_kv()
            first, banks = gmlp(KM, t_km)
            out_proj_moe(0, first, banks)
            rest_of_moe = moe(0)
            first, banks = mla(rest_of_moe)
            out_proj_moe(1, first, banks)
            moe(1)
            sp.wait(*t_out)

        program()

        with nc.Block() as block:
            @block.sync
            def _(e):
                for op in sp.ops:
                    op()

            @block.tensor
            def _(e):
                for op in pe.ops:
                    op()

            @block.scalar
            def _(e):
                for op in act.ops:
                    op()

            @block.vector
            def _(e):
                for op in dve.ops:
                    op()

            @block.gpsimd
            def _(e):
                for op in pool.ops:
                    op()


def by_rows(w):
    k, m = w.shape[0] // 128, w.shape[1] // 128
    t = w.reshape(k, 128, m, 128).transpose(2, 0, 1, 3).reshape(m * k // 8, 8, 128, 128)
    return t.transpose(0, 2, 1, 3).reshape(-1, 128, 1024)


def by_steps(w):
    k, m = w.shape[0] // 128, w.shape[1] // 128
    t = w.reshape(k, 128, m, 128).transpose(0, 2, 1, 3).reshape(m * k // 8, 8, 128, 128)
    return t.transpose(0, 2, 1, 3).reshape(-1, 128, 1024)


def by_out(w):
    return np.concatenate([by_steps(w[:, :512]), by_rows(w[:, 512:])])


def by_cols(w, per):
    k, cols = w.shape[0] // 128, w.shape[1]
    t = w.reshape(k, 128, cols)
    out = np.zeros((-(-k // per), 128, 1024), w.dtype)
    for b in range(out.shape[0]):
        for i in range(min(per, k - per * b)):
            out[b, :, cols * i:cols * i + cols] = t[per * b + i]
    return out


def beside(w):
    return np.stack([by_cols(w[:, :512], 2), by_cols(w[:, 512:], 2)], 1).reshape(-1, 128, 1024)


def columns(v):
    v = v.reshape(-1, v.shape[-1] // 128, 128)
    return v.transpose(2, 0, 1).reshape(128, -1)


def layout(x):
    x = {k: np.asarray(v) for k, v in x.items()}
    out = {"cst": CONST}

    def tokens_last(v):
        return v.reshape(256, 8, 128).transpose(2, 1, 0).reshape(128, 2048)

    out["xT"] = tokens_last(x["x"])
    out["memT"] = tokens_last(x["mem_2"])
    out["pos"] = x["positions_2"].reshape(2, 128).T

    pos = []
    for j in range(2):
        for name in ("nsa_cmp_pos_k", "nsa_cmp_pos_v"):
            p = x[name][j].reshape(16, 2, 64).transpose(2, 1, 0).reshape(64, 32)
            pos.append(np.concatenate([p, p], 0))
    w2 = []
    for j in range(2):
        for name in ("nsa_cmp_k_w2", "nsa_cmp_v_w2"):
            w2.append(x[name][j].reshape(2, 128, 64).transpose(1, 0, 2).reshape(128, 128))
    out["cmp"] = np.stack([np.concatenate(pos[2 * j:2 * j + 2] + w2[2 * j:2 * j + 2], 1) for j in range(2)])
    rows = lambda v: np.broadcast_to(v[None, :], (128, v.shape[0]))
    bias = [rows(np.concatenate([x["moe_b_group_2"][i], x["moe_b_expert_2"][i]])) for i in range(2)]
    prm = [columns(x["norm_mix"]), columns(x["norm_ffn"]), columns(x["norm_final"]), columns(x["mem_norm_g_2"]),
           columns(x["norm1_g_2"]), columns(x["norm2_g_2"]), columns(x["mem_qn_g_2"]), columns(x["mem_kn_g_2"]),
           x["conv_w"][0].reshape(3, 8, 128).transpose(2, 1, 0).reshape(128, 24),
           columns(x["b_q_norm_g_2"]), columns(x["b_kv_norm_g_2"]),
           columns(x["b_qn_g_2"][:, :128]), columns(x["b_kn_g_2"][:, :128]),
           rows(x["b_qn_g_2"][0, 128:]), rows(x["b_kn_g_2"][0, 128:])] + bias
    out["prm"] = np.concatenate(prm, 1)

    in1, in2, wo, cmp_ = [], [], [], []
    heads = np.array([4 * (2 * p + h) + r for p in range(2) for r in range(4) for h in range(2)])
    perm = (64 * heads[:, None] + np.arange(64)[None]).reshape(-1)
    for j in range(2):
        w = x["nsa_w_in"][j]
        part = lambda i: w[:, 1024 + 256 * i:1280 + 256 * i]
        vg = np.concatenate([part(3), w[:, 2560:2608]], 1)
        q = by_rows(w[:, :1024][:, perm])
        first = by_steps(np.concatenate([part(0), part(1)], 1))
        in1.append(np.concatenate([first, by_rows(part(2)), by_rows(part(4)), q[:1]]))
        in2.append(np.concatenate([q[1:4], by_cols(vg, 3), by_cols(part(5), 4), q[4:]]))
        wo.append(by_out(x["nsa_w_out"][j][perm]))
        c = np.stack([x["nsa_cmp_k_w1"][j], x["nsa_cmp_v_w1"][j]])
        cmp_.append(c.reshape(2, 8, 2, 128, 256).transpose(1, 3, 2, 0, 4).reshape(8, 128, 1024))
    out["nsa_in1"], out["nsa_in2"], out["nsa_out"], out["w_cmp"] = (np.stack(v) for v in (in1, in2, wo, cmp_))

    w = x["moba_w_in"][0]
    q, k = by_rows(w[:, :1024]), by_rows(w[:, 1024:2048])
    pairs = np.concatenate([q[:1], np.stack([k[:7], q[1:]], 1).reshape(14, 128, 1024), k[7:]])
    out["moba_in"] = np.concatenate([beside(w[:, 2048:]), pairs])[None]
    out["moba_out"] = by_out(x["moba_w_out"][0])[None]
    b, c, u = (by_rows(x["conv_w_in"][0][:, 1024 * i:1024 * i + 1024]) for i in range(3))
    first = by_steps(np.concatenate([x["conv_w_in"][0][:, 1024 * i:1024 * i + 128] for i in (1, 2, 0)], 1))
    out["conv_in"] = np.concatenate([first, np.stack([c, u, b], 1).reshape(24, 128, 1024)[3:]])[None]
    out["conv_out"] = by_out(x["conv_w_out"][0])[None]

    ffn = []
    for i in range(4):
        gu = np.stack([x["ffn_w_gate"][i].reshape(1024, 22, 128), x["ffn_w_up"][i].reshape(1024, 22, 128)], 2)
        d = x["ffn_w_down"][i].reshape(22, 1, 128, 1024)
        seq = [by_steps(gu[:, :2].reshape(1024, 512))]
        for f in range(2, 22):
            seq.append(by_steps(gu[:, f].reshape(1024, 256)))
            if f >= 3:
                seq.append(d[f - 3])
        ffn.append(np.concatenate(seq + [d[19], d[20], d[21]]))
    out["ffn"] = np.stack(ffn)

    out["mem_kv"] = beside(x["w_mem_kv_2"])[None]
    mem_first = lambda w: np.concatenate([w[1024:], w[:1024]])
    w = x["a_w_in_2"][0]
    out["a_in"] = np.concatenate([beside(w[:, 1024:2048]), by_cols(w[:, 2048:], 2), by_rows(w[:, :1024])])[None]
    out["a_out"] = by_out(mem_first(x["a_w_out_2"][0]))[None]
    ln = np.concatenate([x["a_ln_g_2"][0], x["a_ln_b_2"][0]])
    out["a_ln"] = np.broadcast_to(ln[None], (128, 2048))
    out["a_ws"] = x["a_w_s_2"][0].transpose(2, 0, 1).reshape(128, 1024)
    out["a_bs"] = np.broadcast_to(x["a_b_s_2"][0].reshape(1, 1024), (128, 1024))
    rt = []
    for i in range(2):
        w = np.concatenate([x["moe_w_group_2"][i], x["moe_w_expert_2"][i]], 1)
        rt.append(w.reshape(8, 128, 36).transpose(1, 0, 2).reshape(1, 128, 288))
    out["router"] = np.stack(rt)
    w = x["b_w_in_2"][0]
    out["b_in"] = np.concatenate([by_cols(w[:, 512:832], 3), beside(np.concatenate([w[:, :512], w[:, 832:]], 1))])[None]
    w = x["b_w_q_up_2"][0].reshape(512, 8, 192)
    q_n, q_r = w[:, :, :128].reshape(512, 1024), w[:, :, 128:].reshape(512, 512)
    w = x["b_w_kv_up_2"][0].reshape(256, 8, 2, 128)
    k, v = w[:, :, 0].reshape(256, 1024), w[:, :, 1].reshape(256, 1024)
    ups = [k[:, :512], k[:, 512:], q_r, q_n[:, :512], q_n[:, 512:], v[:, :512], v[:, 512:]]
    out["b_up"] = np.concatenate([by_cols(w, 2) for w in ups])[None]
    out["b_out"] = by_out(mem_first(x["b_w_out_2"][0]))[None]

    g, u = (x[n].reshape(2, 8, 4, 8, 128, 256) for n in ("moe_w_gate_2", "moe_w_up_2"))
    gu = np.empty((2, 8, 8, 128, 4, 512), np.float32)
    gu[..., :256], gu[..., 256:] = g.transpose(0, 1, 3, 4, 2, 5), u.transpose(0, 1, 3, 4, 2, 5)
    gu = gu.reshape(2, 8, 8, 128, 2, 1024).transpose(0, 1, 2, 4, 3, 5).reshape(2, 8, 16, 128, 1024)
    d = x["moe_w_down_2"].reshape(2, 8, 4, 2, 128, 4, 256).transpose(0, 1, 5, 3, 4, 2, 6).reshape(2, 8, 8, 128, 1024)
    out["moe"] = np.concatenate([gu, d], 2).reshape(2, 192, 128, 1024)
    return {k: np.ascontiguousarray(v) for k, v in out.items()}


def kernel(**inputs):
    import concourse.bacc as _bacc
    from concourse import mybir as _mybir
    from concourse.bass_utils import run_bass_kernel_spmd as _run

    nc = _bacc.Bacc("TRN2", target_bir_lowering=False, num_devices=1)
    arrays = layout(inputs)
    args = {n: nc.dram_tensor(n, v.shape, _mybir.dt.from_np(v.dtype), kind="ExternalInput").ap()
            for n, v in arrays.items()}
    y = nc.dram_tensor("out_0_dram", (128, 2048), _mybir.dt.float32, kind="ExternalOutput").ap()
    blocks_kernel(nc, args, y)
    r = _run(nc, [arrays], core_ids=[0])
    got = np.asarray(r.results[0]["out_0_dram"])
    return got.reshape(128, 8, 256).transpose(2, 1, 0).reshape(1, 256, 1024)
```
